# Optimizing a Trainium2 kernel written in Bass

```python
import math
import jax, jax.numpy as jnp
from jax import lax
import numpy as np

D_MODEL = 2048
BATCH = 1
SEQ = 256
DEPTH = 1

CHUNK = 64
LEFT_CHUNKS = 8
BAND = LEFT_CHUNKS + 1

MIX_WIDTH = D_MODEL
ATTN_WIDTH = MIX_WIDTH // 2
POOL_WIDTH = MIX_WIDTH - ATTN_WIDTH
HEAD_DIM = 128
N_HEADS = ATTN_WIDTH // HEAD_DIM
REL_CLIP = 128
POOL_WINDOWS = (2, 4, 8, 16)
N_POOL_GROUPS = len(POOL_WINDOWS)
POOL_GROUP = POOL_WIDTH // N_POOL_GROUPS
IN_WIDTH = 3 * ATTN_WIDTH + POOL_WIDTH

D_FF = 5632
CONV_WIDTH = 3
NORM_EPS = 1e-6


def rms_norm(x, g):
    xf = x.astype(jnp.float32)
    y = xf * lax.rsqrt(jnp.mean(xf * xf, axis=-1, keepdims=True) + NORM_EPS)
    return (y * g.astype(jnp.float32)).astype(x.dtype)

def _band_bias_index():
    q_pos = np.arange(CHUNK) + LEFT_CHUNKS * CHUNK
    k_pos = np.arange(BAND * CHUNK)
    rel = np.clip(q_pos[:, None] - k_pos[None, :], -REL_CLIP, REL_CLIP)
    return (rel + REL_CLIP).astype(np.int32)

def chunked_attention(q, k, v, rel_bias):
    B, S, H, Dh = q.shape
    N = S // CHUNK
    qc = q.reshape(B, N, CHUNK, H, Dh)
    pad = ((0, 0), (LEFT_CHUNKS * CHUNK, 0), (0, 0), (0, 0))
    kc = jnp.pad(k, pad).reshape(B, N + LEFT_CHUNKS, CHUNK, H, Dh)
    vc = jnp.pad(v, pad).reshape(B, N + LEFT_CHUNKS, CHUNK, H, Dh)
    scale = 1.0 / math.sqrt(Dh)
    scores = jnp.concatenate(
        [jnp.einsum('bnqhd,bnkhd->bnhqk', qc, kc[:, j:j + N],
                    preferred_element_type=jnp.float32) for j in range(BAND)],
        axis=-1) * scale
    bias = rel_bias.astype(jnp.float32)[:, _band_bias_index()]
    scores = scores + bias[None, None]
    key_chunk = np.repeat(np.arange(BAND), CHUNK)
    valid = (jnp.arange(N)[:, None] + key_chunk[None, :]) >= LEFT_CHUNKS
    scores = jnp.where(valid[None, :, None, None, :], scores, jnp.float32(-1e30))
    probs = jax.nn.softmax(scores, axis=-1).astype(v.dtype)
    out = 0.0
    for j in range(BAND):
        out = out + jnp.einsum('bnhqk,bnkhd->bnqhd',
                               probs[..., j * CHUNK:(j + 1) * CHUNK], vc[:, j:j + N])
    return out.reshape(B, S, H, Dh)

def multiscale_pool(u, pool_w, pool_scale):
    B, S, _ = u.shape
    uf = u.astype(jnp.float32)
    cs = jnp.cumsum(uf, axis=1)
    pos_count = jnp.arange(1, S + 1, dtype=jnp.float32)
    groups = []
    for g, w in enumerate(POOL_WINDOWS):
        sl = slice(g * POOL_GROUP, (g + 1) * POOL_GROUP)
        csg = cs[..., sl]
        shifted = jnp.pad(csg, ((0, 0), (w, 0), (0, 0)))[:, :S]
        count = jnp.minimum(pos_count, jnp.float32(w))[None, :, None]
        groups.append((csg - shifted) / count - uf[..., sl])
    pooled = jnp.stack(groups, axis=2).astype(u.dtype)
    mixed = jnp.einsum('bsgc,gcd->bsgd', pooled, pool_w).reshape(B, S, POOL_WIDTH)
    return mixed * pool_scale

def causal_dwconv(u, conv_w, conv_b):
    S = u.shape[1]
    up = jnp.pad(u, ((0, 0), (CONV_WIDTH - 1, 0), (0, 0)))
    out = conv_b
    for t in range(CONV_WIDTH):
        out = out + up[:, t:t + S] * conv_w[t]
    return out

def first_inputs(seed: int = 0) -> dict:
    key = jax.random.key(seed)
    ks = jax.random.split(key, 16)
    f32 = jnp.float32
    nrm = lambda k, shape, s: jax.random.normal(k, shape, f32) * s
    gain = lambda k, n: 1.0 + 0.02 * jax.random.normal(k, (DEPTH, n), f32)
    return {
        "x": nrm(ks[0], (BATCH, SEQ, D_MODEL), 1.0),
        "pre_mix_g": gain(ks[1], D_MODEL),
        "w_in": nrm(ks[2], (DEPTH, D_MODEL, IN_WIDTH), D_MODEL ** -0.5),
        "rel_bias": nrm(ks[3], (DEPTH, N_HEADS, 2 * REL_CLIP + 1), 0.1),
        "pool_w": nrm(ks[4], (DEPTH, N_POOL_GROUPS, POOL_GROUP, POOL_GROUP), POOL_GROUP ** -0.5),
        "pool_scale": gain(ks[5], POOL_WIDTH),
        "w_o": nrm(ks[6], (DEPTH, MIX_WIDTH, D_MODEL), MIX_WIDTH ** -0.5),
        "post_mix_g": gain(ks[7], D_MODEL),
        "pre_ffn_g": gain(ks[8], D_MODEL),
        "w_up": nrm(ks[9], (DEPTH, D_MODEL, 2 * D_FF), D_MODEL ** -0.5),
        "conv_w": nrm(ks[10], (DEPTH, CONV_WIDTH, 2 * D_FF), CONV_WIDTH ** -0.5),
        "conv_b": nrm(ks[11], (DEPTH, 2 * D_FF), 0.01),
        "w_down": nrm(ks[12], (DEPTH, D_FF, D_MODEL), D_FF ** -0.5),
        "post_ffn_g": gain(ks[13], D_MODEL),
    }

def first_block(x, pre_mix_g, w_in, rel_bias, pool_w, pool_scale, w_o, post_mix_g,
              pre_ffn_g, w_up, conv_w, conv_b, w_down, post_ffn_g):
    B, S, _ = x.shape
    for l in range(DEPTH):
        h = rms_norm(x, pre_mix_g[l])
        z = h @ w_in[l]
        q = z[..., :ATTN_WIDTH].reshape(B, S, N_HEADS, HEAD_DIM)
        k = z[..., ATTN_WIDTH:2 * ATTN_WIDTH].reshape(B, S, N_HEADS, HEAD_DIM)
        v = z[..., 2 * ATTN_WIDTH:3 * ATTN_WIDTH].reshape(B, S, N_HEADS, HEAD_DIM)
        u = z[..., 3 * ATTN_WIDTH:]
        a = chunked_attention(q, k, v, rel_bias[l]).reshape(B, S, ATTN_WIDTH)
        p = multiscale_pool(u, pool_w[l], pool_scale[l])
        m = jnp.concatenate([a, p], axis=-1) @ w_o[l]
        x = x + rms_norm(m, post_mix_g[l])
        h = rms_norm(x, pre_ffn_g[l])
        up = causal_dwconv(h @ w_up[l], conv_w[l], conv_b[l])
        y = (jax.nn.gelu(up[..., :D_FF], approximate=True) * up[..., D_FF:]) @ w_down[l]
        x = x + rms_norm(y, post_ffn_g[l])
    return x


DEPTH_2 = 2

Q_BLOCK = 128
N_A = DEPTH_2 // 2
N_B = DEPTH_2 - N_A
RWKV_HEAD = 64
RWKV_HEADS = D_MODEL // RWKV_HEAD
DECAY_LORA = max(32, int(round(1.8 * D_MODEL ** 0.5 / 32)) * 32)
AAA_LORA = max(32, int(round(1.8 * D_MODEL ** 0.5 / 32)) * 32)
GN_EPS = 64e-5
DIFF_HEADS = D_MODEL // 256
DIFF_HEAD_DIM = D_MODEL // DIFF_HEADS // 2
SUBLN_EPS = 1e-5
DEEPNORM_ALPHA = (2.0 * DEPTH_2) ** 0.25
DEEPNORM_BETA = (8.0 * DEPTH_2) ** -0.25
LN_EPS = 1e-5


def _layernorm(x, g, b):
    xf = x.astype(jnp.float32)
    mu = jnp.mean(xf, -1, keepdims=True)
    xc = xf - mu
    var = jnp.mean(xc * xc, -1, keepdims=True)
    return (xc * lax.rsqrt(var + LN_EPS) * g + b).astype(x.dtype)

def _wkv7_scan(r, w, k, v, kk, a):
    B, T, H, N = r.shape

    def step(S, inp):
        r_t, w_t, k_t, v_t, kk_t, a_t = inp
        sa = jnp.einsum('bhvk,bhk->bhv', S, kk_t)
        S = (S * w_t[:, :, None, :]
             - sa[..., None] * (kk_t * a_t)[:, :, None, :]
             + v_t[..., None] * k_t[:, :, None, :])
        y = jnp.einsum('bhvk,bhk->bhv', S, r_t)
        return S, y

    xs = tuple(jnp.moveaxis(t.astype(jnp.float32), 1, 0) for t in (r, w, k, v, kk, a))
    S0 = jnp.zeros((B, H, N, N), jnp.float32)
    _, ys = lax.scan(step, S0, xs)
    return jnp.moveaxis(ys, 0, 1)

def _rwkv7_mixer(x, mu_proj, mu_lora, w_in, w0, w1, w2, a0, a1, a2,
                 k_k, k_a, r_k, gn_g, gn_b, w_out):
    B, T, C = x.shape
    H, N = RWKV_HEADS, RWKV_HEAD
    xx = jnp.pad(x, ((0, 0), (1, 0), (0, 0)))[:, :-1] - x
    xs = x[None] + xx[None] * mu_proj[:, None, None, :]
    proj = jnp.einsum('sbtd,sde->sbte', xs, w_in)
    r, k, v, g = proj[0], proj[1], proj[2], proj[3]
    xw = x + xx * mu_lora[0]
    xa = x + xx * mu_lora[1]
    w_log = -jax.nn.softplus(-(w0 + jnp.tanh(xw @ w1) @ w2)) - 0.5
    decay = jnp.exp(-jnp.exp(w_log.astype(jnp.float32)))
    a = jax.nn.sigmoid(a0 + (xa @ a1) @ a2)
    kk = (k * k_k).reshape(B, T, H, N).astype(jnp.float32)
    kk = kk / jnp.maximum(jnp.sqrt(jnp.sum(kk * kk, -1, keepdims=True)), 1e-12)
    k = k * (1.0 + (a - 1.0) * k_a)
    rh = r.reshape(B, T, H, N)
    kh = k.reshape(B, T, H, N)
    vh = v.reshape(B, T, H, N)
    y = _wkv7_scan(rh, decay.reshape(B, T, H, N), kh, vh, kk, a.reshape(B, T, H, N))
    mu = jnp.mean(y, -1, keepdims=True)
    yc = y - mu
    var = jnp.mean(yc * yc, -1, keepdims=True)
    y = (yc * lax.rsqrt(var + GN_EPS)).reshape(B, T, C) * gn_g + gn_b
    bonus = jnp.sum(rh.astype(jnp.float32) * kh.astype(jnp.float32) * r_k, -1, keepdims=True) * vh.astype(jnp.float32)
    y = (y + bonus.reshape(B, T, C)).astype(x.dtype)
    return (y * jax.nn.silu(g)) @ w_out

def _diff_attention(q, k, v, lam):
    B, H2, T, dh = q.shape
    H = H2 // 2
    slopes = jnp.repeat(2.0 ** (-(8.0 / H) * jnp.arange(1, H + 1, dtype=jnp.float32)), 2)
    scale = dh ** -0.5
    outs = []
    for i in range(T // Q_BLOCK):
        q0, q1 = i * Q_BLOCK, (i + 1) * Q_BLOCK
        qb = q[:, :, q0:q1]
        kb = k[:, :, :q1]
        vb = v[:, :, :q1]
        s = jnp.einsum('bmqd,bmkd->bmqk', qb, kb).astype(jnp.float32) * scale
        tq = jnp.arange(q0, q1)
        tk = jnp.arange(q1)
        dist = jnp.abs(tq[:, None] - tk[None, :]).astype(jnp.float32)
        allowed = (tk[None, :] // CHUNK) <= (tq[:, None] // CHUNK)
        s = jnp.where(allowed, s - slopes[:, None, None] * dist, -jnp.inf)
        p = jax.nn.softmax(s, axis=-1).reshape(B, H, 2, Q_BLOCK, q1)
        attn = p[:, :, 0] - lam * p[:, :, 1]
        outs.append(jnp.einsum('bhqk,bhkd->bhqd', attn.astype(vb.dtype), vb))
    return jnp.concatenate(outs, axis=2)

def _diff_mixer(x, k_sh, v_sh, w_qg, lam_p, subln_g, w_out, layer):
    B, T, C = x.shape
    H, dh = DIFF_HEADS, DIFF_HEAD_DIM
    qg = x @ w_qg
    q = qg[..., :C].reshape(B, T, 2 * H, dh).transpose(0, 2, 1, 3)
    g = qg[..., C:]
    lam_init = 0.8 - 0.6 * math.exp(-0.3 * layer)
    lam_f = lam_p.astype(jnp.float32)
    lam = (jnp.exp(jnp.sum(lam_f[0] * lam_f[1])) - jnp.exp(jnp.sum(lam_f[2] * lam_f[3])) + lam_init)
    o = _diff_attention(q, k_sh, v_sh, lam).astype(jnp.float32)
    o = o * lax.rsqrt(jnp.mean(o * o, -1, keepdims=True) + SUBLN_EPS) * subln_g * (1.0 - lam_init)
    o = o.transpose(0, 2, 1, 3).reshape(B, T, C).astype(x.dtype)
    return (o * jax.nn.silu(g)) @ w_out

def second_inputs(seed: int = 0) -> dict:
    key = jax.random.key(seed)
    ks = jax.random.split(key, 32)
    C, H, N, dh = D_MODEL, RWKV_HEADS, RWKV_HEAD, DIFF_HEAD_DIM
    f32 = jnp.float32
    nrm = lambda k, shape, s: jax.random.normal(k, shape, f32) * s
    return {
        "x": jax.random.normal(ks[0], (BATCH, SEQ, C), f32),
        "a_mu_proj": jax.random.uniform(ks[1], (N_A, 4, C), f32),
        "a_mu_lora": jax.random.uniform(ks[2], (N_A, 2, C), f32),
        "a_w_in": nrm(ks[3], (N_A, 4, C, C), C ** -0.5),
        "a_w0": jax.random.uniform(ks[4], (N_A, C), f32, -6.0, 0.0),
        "a_w1": nrm(ks[5], (N_A, C, DECAY_LORA), C ** -0.5),
        "a_w2": nrm(ks[6], (N_A, DECAY_LORA, C), 0.1 * DECAY_LORA ** -0.5),
        "a_a0": nrm(ks[7], (N_A, C), 0.5),
        "a_a1": nrm(ks[8], (N_A, C, AAA_LORA), C ** -0.5),
        "a_a2": nrm(ks[9], (N_A, AAA_LORA, C), 0.3 * AAA_LORA ** -0.5),
        "a_k_k": 0.85 + nrm(ks[10], (N_A, C), 0.05),
        "a_k_a": 1.0 + nrm(ks[11], (N_A, C), 0.05),
        "a_r_k": -0.04 + nrm(ks[12], (N_A, H, N), 0.1),
        "a_gn_g": 1.0 + nrm(ks[13], (N_A, C), 0.05),
        "a_gn_b": nrm(ks[14], (N_A, C), 0.01),
        "a_w_out": nrm(ks[15], (N_A, C, C), C ** -0.5 * DEEPNORM_BETA),
        "w_k_shared": nrm(ks[16], (C, C), C ** -0.5),
        "w_v_shared": nrm(ks[17], (C, C), C ** -0.5),
        "b_w_qg": nrm(ks[18], (N_B, C, 2 * C), C ** -0.5),
        "b_lambda": nrm(ks[19], (N_B, 4, dh), 0.1),
        "b_subln_g": 1.0 + nrm(ks[20], (N_B, 2 * dh), 0.05),
        "b_w_out": nrm(ks[21], (N_B, C, C), C ** -0.5 * DEEPNORM_BETA),
        "ln_g": 1.0 + nrm(ks[22], (DEPTH_2, C), 0.05),
        "ln_b": nrm(ks[23], (DEPTH_2, C), 0.01),
    }

def second_block(x, a_mu_proj, a_mu_lora, a_w_in, a_w0, a_w1, a_w2, a_a0, a_a1, a_a2,
              a_k_k, a_k_a, a_r_k, a_gn_g, a_gn_b, a_w_out, w_k_shared, w_v_shared,
              b_w_qg, b_lambda, b_subln_g, b_w_out, ln_g, ln_b):
    B, T, C = x.shape
    k_sh = None
    v_sh = None
    for layer in range(DEPTH_2):
        if layer < N_A:
            i = layer
            y = _rwkv7_mixer(x, a_mu_proj[i], a_mu_lora[i], a_w_in[i], a_w0[i], a_w1[i], a_w2[i],
                             a_a0[i], a_a1[i], a_a2[i], a_k_k[i], a_k_a[i], a_r_k[i],
                             a_gn_g[i], a_gn_b[i], a_w_out[i])
        else:
            j = layer - N_A
            y = _diff_mixer(x, k_sh, v_sh, b_w_qg[j], b_lambda[j], b_subln_g[j], b_w_out[j], layer)
        x = _layernorm(DEEPNORM_ALPHA * x + y, ln_g[layer], ln_b[layer])
        if layer == N_A - 1:
            k_sh = (x @ w_k_shared).reshape(B, T, 2 * DIFF_HEADS, DIFF_HEAD_DIM).transpose(0, 2, 1, 3)
            v_sh = (x @ w_v_shared).reshape(B, T, DIFF_HEADS, 2 * DIFF_HEAD_DIM).transpose(0, 2, 1, 3)
    return x


def setup_inputs(seed=0):
    out = dict(first_inputs(seed))
    for name, value in second_inputs(seed + 1).items():
        if name != "x":
            out[name + "_2"] = value
    return out


def reference(
    x, pre_mix_g, w_in, rel_bias, pool_w, pool_scale, w_o, post_mix_g, pre_ffn_g, w_up, conv_w,
    conv_b, w_down, post_ffn_g, a_mu_proj_2, a_mu_lora_2, a_w_in_2, a_w0_2, a_w1_2, a_w2_2,
    a_a0_2, a_a1_2, a_a2_2, a_k_k_2, a_k_a_2, a_r_k_2, a_gn_g_2, a_gn_b_2, a_w_out_2,
    w_k_shared_2, w_v_shared_2, b_w_qg_2, b_lambda_2, b_subln_g_2, b_w_out_2, ln_g_2, ln_b_2,
):
    x = first_block(
        x, pre_mix_g, w_in, rel_bias, pool_w, pool_scale, w_o, post_mix_g, pre_ffn_g, w_up,
        conv_w, conv_b, w_down, post_ffn_g,
    )
    return second_block(
        x, a_mu_proj_2, a_mu_lora_2, a_w_in_2, a_w0_2, a_w1_2, a_w2_2, a_a0_2, a_a1_2, a_a2_2,
        a_k_k_2, a_k_a_2, a_r_k_2, a_gn_g_2, a_gn_b_2, a_w_out_2, w_k_shared_2, w_v_shared_2,
        b_w_qg_2, b_lambda_2, b_subln_g_2, b_w_out_2, ln_g_2, ln_b_2,
    )


_drawn_inputs = setup_inputs


def setup_inputs(seed=0):
    import zlib

    import numpy as np

    out = dict(_drawn_inputs(seed))
    spreads = {}
    factors = {'pre_mix_g': 2.82,
     'rel_bias': 3.571,
     'pool_scale': 2.963,
     'post_mix_g': 2.988,
     'pre_ffn_g': 3.003,
     'conv_b': 5.853,
     'post_ffn_g': 4.209,
     'a_w1_2': 60.31,
     'a_w2_2': 58.872,
     'a_k_k_2': 200.0,
     'a_k_a_2': 4.022,
     'a_gn_g_2': 50.032,
     'a_gn_b_2': 200.0,
     'b_subln_g_2': 8.0,
     'ln_b_2': 3.824}
    for name, (base, spread) in spreads.items():
        noise = np.random.default_rng([zlib.crc32(name.encode()), seed]).standard_normal(out[name].shape)
        drawn = base * np.exp(spread * noise) if base else spread * noise
        out[name] = __import__('jax').numpy.asarray(drawn.astype(out[name].dtype))
    for name, factor in factors.items():
        out[name] = (out[name] * factor).astype(out[name].dtype)
    return out
```

```python
import math
from contextlib import ExitStack

import numpy as np
import concourse.bass as bass
from concourse import mybir

F32 = mybir.dt.float32
F32R = mybir.dt.float32r
ALU = mybir.AluOpType
ACT = mybir.ActivationFunctionType
AX = mybir.AxisListType
ds = bass.ds

P = 128
T = 256
D = 2048
KD = D // P
FF = 5632
KF = FF // P
HALF = D // 2
HT = HALF // P
CHUNK = 64
NCH = T // CHUNK
POOL_WINDOWS = (2, 4, 8, 16)
NEG = -1e30
NORM_EPS = 1e-6
LN_EPS = 1e-5
GN_EPS = 64e-5
SUBLN_EPS = 1e-5
ALPHA = 4.0 ** 0.25
DECAY = -math.exp(-0.5)
LAM_INIT = 0.8 - 0.6 * math.exp(-0.3)
LORA = 96
HEAD_SCALE = 128.0 ** -0.5

PARAMS = [("pre_mix_g", KD), ("post_mix_g", KD), ("pre_ffn_g", KD), ("post_ffn_g", KD),
          ("pool_scale", HT), ("conv_w", 3 * 2 * KF), ("conv_b", 2 * KF),
          ("a_mu_proj_2", 4 * KD), ("a_mu_lora_2", 2 * KD), ("a_w0_2", KD), ("a_a0_2", KD),
          ("a_k_k_2", KD), ("a_k_a_2", KD), ("a_r_k_2", KD), ("a_gn_g_2", KD), ("a_gn_b_2", KD),
          ("ln_g_2", 2 * KD), ("ln_b_2", 2 * KD), ("b_subln_g_2", 2), ("b_lambda_2", 4)]
COL = {}
_n = 0
for _name, _cols in PARAMS:
    COL[_name] = _n
    _n += _cols
N_PARAM = _n

CONSTS = [("ident", P), ("ones", P), ("headones", P), ("stack", CHUNK), ("quarter", CHUNK), ("headsel", CHUNK), ("flip", P),
          ("band", 2 * T), ("dist", 2 * T), ("invcount", 4 * T), ("scan", T), ("tri", 2 * 2 * CHUNK), ("expand", D)]
CCOL = {}
_n = 0
for _name, _cols in CONSTS:
    CCOL[_name] = _n
    _n += _cols
N_CONST = _n


def constants():
    c = np.zeros((P, N_CONST), np.float32)

    def put(name, a):
        c[:, CCOL[name]:CCOL[name] + a.shape[1]] = a

    p = np.arange(P)[:, None]
    t = np.arange(T)[None]
    put("ident", np.eye(P))
    put("ones", np.ones((P, P)))
    put("headones", (p // 64 == np.arange(P)[None] // 64))
    put("stack", (p % 64 == np.arange(64)[None]))
    put("quarter", (p // 64 == np.arange(64)[None] // 32) & (p % 64 < 32))
    put("headsel", (np.arange(64)[None] == 30 + p // 64))
    put("expand", (np.arange(D)[None] // 64 == p))
    put("flip", np.eye(P)[::-1])
    q = [p, p + P]
    seen = [(t // CHUNK) <= (x // CHUNK) for x in q]
    put("band", np.concatenate([np.where(s, 0.0, NEG) for s in seen], 1))
    put("dist", np.concatenate([np.where(s, np.abs(x - t), -100 * NEG) for s, x in zip(seen, q)], 1))
    put("invcount", np.concatenate([np.repeat(1.0 / np.minimum(t + 1, w), P, 0) for w in POOL_WINDOWS], 1))
    put("scan", np.repeat((t % CHUNK != 0), P, 0))
    h, s = p // 64, p % 64
    col = np.arange(2 * CHUNK)[None]
    same = (col // 64) == h
    tc = col[:, :64]
    put("tri", np.concatenate([same & (col % 64 > s), tc > s, tc >= s], 1))
    return c


KU = 4
UNIT_COLS = 256
RAW = 8
SPL = 4


class Counts:

    def __init__(self, eng):
        self.eng, self.n, self.reg = eng, {}, None

    def __call__(self, sem, k=1, what=""):
        key = (sem.name, what)
        self.n[key] = self.n.get(key, 0) + k
        if self.reg is None:
            return self.n[key]
        self.used.add(key)
        return self.n[key] + self.reg * self.per[key]

    def total(self, sem, what=""):
        return self.n[(sem.name, what)]

    def loop(self, iters, per):
        return _Loop(self, iters, {(s.name, "") if not isinstance(s, tuple) else (s[0].name, s[1]): k for s, k in per.items()})


class _Loop:
    def __init__(self, counts, iters, per):
        self.c, self.iters, self.per = counts, iters, per

    def __enter__(self):
        self.cm = self.c.eng.Fori(0, self.iters)
        i = self.cm.__enter__()
        self.c.reg, self.c.per, self.c.used = i, self.per, set()
        self.start = dict(self.c.n)
        return i

    def __exit__(self, *exc):
        if exc[0] is not None:
            return False
        c = self.c
        for key in c.used:
            did = c.n[key] - self.start.get(key, 0)
            assert did == self.per[key], (key, did, self.per[key])
            c.n[key] = self.start.get(key, 0) + self.per[key] * self.iters
        c.reg = None
        return self.cm.__exit__(*exc)


def program(nc, h):
    root = ExitStack()
    sems = {}

    def sem(name):
        sems[name] = root.enter_context(nc.semaphore(name))
        return sems[name]

    def sb(scope, name, shape, dt=F32):
        return scope.enter_context(nc.sbuf_tensor(name, shape, dt))

    def dram(name, shape):
        return nc.dram_tensor(name, shape, F32, kind="Internal").ap()

    with root:
        PV = sb(root, "params", [P, N_PARAM])
        NFIX = CCOL["flip"]
        CF = sb(root, "consts", [P, NFIX + 4 * CHUNK])
        IDENT, ONES, HEADONES = (CF[:, CCOL[n]:CCOL[n] + P] for n in ("ident", "ones", "headones"))
        TRI2 = CF[:, NFIX:NFIX + P]
        TRI_S = CF[:, NFIX + P:NFIX + P + CHUNK]
        TRI_I = CF[:, NFIX + P + CHUNK:]
        QUARTER = CF[:, CCOL["quarter"]:CCOL["quarter"] + CHUNK]
        HEADSEL = CF[:, CCOL["headsel"]:CCOL["headsel"] + CHUNK]
        STACK = CF[:, CCOL["stack"]:CCOL["stack"] + CHUNK]
        RAWW = sb(root, "raw_w", [P, RAW, KU, UNIT_COLS])
        WHI = sb(root, "w_hi", [P, SPL, KU, UNIT_COLS], F32R)
        WLO = sb(root, "w_lo", [P, SPL, KU, UNIT_COLS], F32R)
        X = sb(root, "x", [P, KD, T])

        def norm_buffers(scope, tag, deep=2):
            return (sb(scope, "sq" + tag, [P, deep, 4, T]), sb(scope, "ht" + tag, [P, deep, 4, T]),
                    sb(scope, "ms" + tag, [P, T]), sb(scope, "rstd" + tag, [P, T]))

        with ExitStack() as s1:
            B1H, B1L = (sb(s1, n, [P, KD, T], F32R) for n in ("mix_hi", "mix_lo"))
            Z = sb(s1, "z", [P, 2 * KD, T])
            with ExitStack() as s2:
                A1H, A1L = (sb(s2, n, [P, KD, T], F32R) for n in ("h1_hi", "h1_lo"))
                N1 = norm_buffers(s2, "_1")
            with ExitStack() as s2:
                VTOK = sb(s2, "v_tok", [P, 8, 2, P])
                HANK = sb(s2, "bias_hankel", [P, 8, 384])
                FLIP = sb(s2, "flip", [P, P])
                BAND = sb(s2, "band", [P, 2, T])
                SS = sb(s2, "scores", [P, 2, 2, T])
                PT = sb(s2, "probs_t", [P, 2, 384])
                ST = sb(s2, "softmax_stats", [P, 2, 4])
                INVC = sb(s2, "invcount", [P, 4, T])
                PA = sb(s2, "pool_a", [P, HT, T])
                PB = sb(s2, "pool_b", [P, HT, T])
                POOLW = sb(s2, "pool_w", [P, 4, 2, 2 * P])
        with ExitStack() as s1:
            B2H, B2L = (sb(s1, n, [P, KD, T], F32R) for n in ("ff_hi", "ff_lo"))
            Y = sb(s1, "y", [P, KD, T])
            A2H, A2L = (sb(s1, n, [P, KD, T], F32R) for n in ("h2_hi", "h2_lo"))
            N2 = norm_buffers(s1, "_2")
            CV = sb(s1, "conv", [P, 4, T])
            GE = sb(s1, "gate", [P, 2, T])
            HG = sb(s1, "gated", [P, 2, T])

        with ExitStack() as s1:
            K, V = (sb(s1, n, [P, KD, T]) for n in ("k", "v"))
            with ExitStack() as s2:
                RK = sb(s2, "r_kappa", [P, 2, KD, T])
                R, KAP = RK[:, 0, :, :], RK[:, 1, :, :]
            with ExitStack() as s2:
                sb(s2, "place_of_r", [P, KD, T])
                A3H, A3L, B3H, B3L = (sb(s2, n, [P, KD, T], F32R) for n in ("xs_a_hi", "xs_a_lo", "xs_b_hi", "xs_b_lo"))
                XX3 = sb(s2, "shift_diff", [P, 4, T])
                HT3 = sb(s2, "xs_quarter", [P, 4, T])
            with ExitStack() as s2:
                sb(s2, "place_of_r_kappa", [P, 2, KD, T])
                BET, BON = (sb(s2, n, [P, KD, T]) for n in ("beta", "bonus"))
                with ExitStack() as s3:
                    W2S = sb(s3, "lora_2", [LORA, 2, D])
                    LOW = sb(s3, "lora_low", [LORA, 2, T])
                with ExitStack() as s3:
                    FMB = sb(s3, "beta_k_v_blocks", [P, 2, 3, 4, P])
                    XS, US, S = (sb(s3, n, [P, 4, CHUNK]) for n in ("wkv_x", "wkv_u", "wkv_s"))
                    SBD, UBD = (sb(s3, n, [P, 4, P]) for n in ("wkv_s_blocks", "wkv_u_blocks"))
                    OUTER = sb(s3, "outer", [P, 1024])
                    GCE = sb(s3, "chunk_decay", [P, KD, NCH])
                with ExitStack() as s3:
                    GNT = sb(s3, "group_norm_temps", [P, 2, 4, T])
                    EXP4 = sb(s3, "head_expand", [32, D])
                    RS4 = sb(s3, "head_rstd", [32, 2, T])
        with ExitStack() as s1:
            C4H, C4L = (sb(s1, n, [P, KD, T], F32R) for n in ("wkv_hi", "wkv_lo"))
            G4 = sb(s1, "silu_g", [P, KD, T])
            Y4 = sb(s1, "y_rwkv", [P, KD, T])
            L4 = (sb(s1, "ln_sq_4", [P, 2, 4, T]), sb(s1, "ln_mean_4", [P, T]), sb(s1, "ln_var_4", [P, T]), sb(s1, "ln_rstd_4", [P, T]))
        with ExitStack() as s1:
            A5H, A5L = (sb(s1, n, [P, KD, T], F32R) for n in ("x_hi", "x_lo"))
            KS5, VS5, Q5, G5 = (sb(s1, n, [P, KD, T]) for n in ("k_shared", "v_shared", "q_diff", "silu_g_diff"))
            DIST = sb(s1, "distance", [P, 2, T])
            SS5 = sb(s1, "diff_scores", [P, 2, 4, T])
            PT5 = sb(s1, "diff_probs_t", [P, 2, 384])
            ST5 = sb(s1, "diff_stats", [P, 2, 8])
            LAM = sb(s1, "lambda", [P, 4])
        with ExitStack() as s1:
            VT5 = sb(s1, "v_shared_tok", [P, 2, KD, P])
            sb(s1, "unused_5", [P, KD, T])
            C5H, C5L = (sb(s1, n, [P, KD, T], F32R) for n in ("o_hi", "o_lo"))
            Y5 = sb(s1, "y_diff", [P, KD, T])
            L5 = (sb(s1, "ln_sq_5", [P, 2, 4, T]), sb(s1, "ln_mean_5", [P, T]), sb(s1, "ln_var_5", [P, T]), sb(s1, "ln_rstd_5", [P, T]))

        def tmp(n, sz=1):
            return RAWW[:, n // 4, n % 4, :]

        ACC = [root.enter_context(nc.psum_tensor(f"acc{i}", [P, 512], F32)) for i in range(4)]
        AUX = [root.enter_context(nc.psum_tensor(f"aux{i}", [P, 512], F32)) for i in range(4)]

        loaded = sem("loaded")
        side = sem("side_loaded")
        landed = [sem(f"raw_landed{i}") for i in range(RAW)]
        hi_made = sem("hi_made")
        lo_made = sem("lo_made")
        unit_done = sem("unit_done")
        acc_free = sem("acc_free")
        sq_ready, sq_free = sem("sq_ready"), sem("sq_free")
        var_ready, rstd_ready = sem("var_ready"), sem("rstd_ready")
        normed = sem("normed")
        nh_made = sem("operand_hi_made")
        operand = sem("operand_ready")
        dstep, astep, gstep = sem("dve_step"), sem("act_step"), sem("pool_step")
        v_turned, v_tok = sem("v_turned"), sem("v_tok")
        scored, sc_free = sem("scored"), sem("score_bank_free")
        maxed, expd, probs = sem("maxed"), sem("exp_done"), sem("probs_ready")
        turned, pt_ready = sem("probs_turned"), sem("probs_t_ready")
        pv_done, pv_hi = sem("pv_done"), sem("pv_hi")
        mixed, mixed_hi = sem("pool_mixed"), sem("pool_mixed_hi")
        mix_ready = sem("mix_ready")
        pooled = sem("pooled")
        conv_base, gelu_done = sem("conv_base"), sem("gelu_done")
        gated, gated_hi, gated_ready = sem("gated"), sem("gated_hi"), sem("gated_ready")
        x_ready = sem("x_ready")
        stored = sem("stored")
        g_stored, lora_in, xw_ready = sem("silu_g_stored"), sem("lora_loaded"), sem("xw_quarters")
        low_done, low_ready = sem("lora_low_done"), sem("lora_low_ready")
        lora_done, sig_ready = sem("lora_done"), sem("sigmoids_ready")
        kk_summed, kk_sq, kk_inverse = sem("kk_summed"), sem("kk_squares"), sem("kk_inverse")
        kk_norm, kk_ready, kk_wide = sem("kk_norm"), sem("kk_ready"), sem("kk_wide")
        exp_in, exp4_in = sem("expand_loaded"), sem("expand_loaded_again")
        l_ready, lp_ready, decays = sem("log_decay"), sem("log_decay_prev"), sem("decays_ready")
        rk_ready, bonus_sum, b1_ready = sem("rk_product"), sem("bonus_sum"), sem("kk_a_ready")
        tile_done, pool_done = sem("tile_prepared"), sem("rho_ready")
        blk_ready, lt_done, lt_ready = sem("beta_blocks"), sem("lt_done"), sem("lt_ready")
        lt_stored = [sem("lt_stored_even"), sem("lt_stored_odd")]
        inv_in, inv_init = sem("lt_loaded"), sem("inverse_started")
        inverted, t_stored = sem("inverted"), sem("inverse_stored")
        fm_ready, kap_ready, prep_done, tok_done = sem("blocks_ready"), sem("kappa_blocks"), sem("pairs_done"), sem("tok_turned")
        pairs_read, rest_out, tok_out = sem("pairs_read"), sem("output_pairs_read"), sem("tok_ready")
        t_loaded = [sem("t_loaded_even"), sem("t_loaded_odd")]
        t_zero = sem("t_zeroed")
        vb_ready = sem("v_tok_blocks")
        v_done, vc_ready, w_done, ws_ready = sem("v_tok_turned"), sem("v_tok_ready"), sem("wkv_w_done"), sem("wkv_xw_ready")
        x_done, xs_ready, u_done, us_ready = sem("wkv_x_done"), sem("wkv_x_ready"), sem("wkv_u_done"), sem("wkv_u_ready")
        s_done, s_ready, sbd_ready, ubd_ready = sem("wkv_s_done"), sem("wkv_s_ready"), sem("s_blocks"), sem("u_blocks")
        y_done, y_out = sem("wkv_y_done"), sem("wkv_y_out")
        g_loaded = sem("silu_g_loaded")
        gn_sum, gn_centred, gn_sq = sem("gn_sum"), sem("gn_centred"), sem("gn_squares")
        gn_sq_sum, gn_var, gn_rstd = sem("gn_sq_sum"), sem("gn_var"), sem("gn_rstd")
        gn_wide = sem("gn_rstd_wide")
        gn_out, gn_gated, gn_hi, gn_ready = sem("gn_out"), sem("gn_gated"), sem("gn_hi"), sem("gn_ready")
        xr_ready, ln_sum, xc_ready, xn_ready = sem("ln_input"), sem("ln_sum"), sem("ln_centred"), sem("ln_scaled")
        dist_in, lam_prod, lam_sum, lam_exp = sem("dist_loaded"), sem("lam_products"), sem("lam_sum"), sem("lam_exp")
        v5_turned, v5_tok = sem("v_shared_turned"), sem("v_shared_tok")
        d_scored, d_max, d_exp, d_probs = sem("diff_scored"), sem("diff_maxed"), sem("diff_exp"), sem("diff_probs")
        d_turned, d_pt, d_pv, o_out = sem("diff_turned"), sem("diff_probs_t"), sem("diff_pv"), sem("diff_o")
        o_sq, o_sum, o_var, o_rstd = sem("o_squares"), sem("o_sum"), sem("o_var"), sem("o_rstd")
        o_scaled, o_gated, o_hi, o_ready = sem("o_scaled"), sem("o_gated"), sem("o_hi"), sem("o_ready")

        FIRST_TILES = 2 * KD + KD + 2 * KF + 3 * KD
        ALL_TILES = FIRST_TILES + 4 * KD

        def gnt(kind, f):
            return GNT[:, kind, f % 4, :]

        block = root.enter_context(nc.Block())
        w_in = h["w_in"][0]
        w_up, w_down = h["w_up"][0], h["w_down"][0]
        GROUPS = [(0, 16), (16, 16), (32, 12)]

        STREAMS = [(3, A3H, A3L, V), (0, B3H, B3L, R), (1, A3H, A3L, K), (2, B3H, B3L, V)]
        W1S = RAWW[:, 0:3, :, :].rearrange("p a b c -> p (a b c)").rearrange("p (w k n) -> p w k n", w=2, k=KD)
        SCAN = tmp(30)
        FLAT = RAWW[:, :, :, :].rearrange("p a b c -> p (a b c)")
        EXP3 = FLAT[0:32, 22 * T:30 * T]
        lt_dram, t_dram, g_dram = dram("lt_scratch", (P, CHUNK, CHUNK)), dram("t_scratch", (P, CHUNK, CHUNK)), dram("g_scratch", (P, KD, T))
        H = CHUNK // 2
        LT = RAWW[:, 0:2, :, :].rearrange("p a b c -> p (a b c)").rearrange("p (b s t) -> p b s t", b=2, t=H)
        TFLAT = RAWW[:, 3:8, :, :].rearrange("p a b c -> p (a b c)")
        TT = TFLAT[:, 0:CHUNK * CHUNK].rearrange("p (s t) -> p s t", t=CHUNK)
        TDIAG = TFLAT[:, 0:2 * H * (CHUNK + 1)].rearrange("p (b x) -> p b x", b=2)[:, :, 0:H * CHUNK]\
            .rearrange("p b (s t) -> p b s t", t=CHUNK)

        def blocks(m, kind):
            return RAWW[:, 4 * m + kind // 2, 2 * (kind % 2):2 * (kind % 2) + 2, :].rearrange("p a c -> p (a c)")\
                .rearrange("p (i c) -> p i c", i=4)
        KBD, TBD, AKK, BT, KT, VBD = 0, 1, 2, 3, 4, 5

        def small(m, n):
            return RAWW[:, 4 * m + 3, n, :].rearrange("p (i c) -> p i c", i=4)
        ARK, ARB, VC = 0, 1, 2

        def cross(m):
            return OUTER[:, m * 512:(m + 1) * 512].rearrange("p (i c) -> p i c", i=4)

        def diag(x):
            return x.unsqueeze(2).broadcast_to([P, 4, 2, CHUNK])
        MASK4 = HEADONES.rearrange("p (o h t) -> p o h t", o=1, h=2).broadcast_to([P, 4, 2, CHUNK])

        @block.sync
        def _(sp):
            seen = Counts(sp)

            def weights(iters, at, ku=KU, kt0=0, k0=0):
                with seen.loop(iters, {lo_made: RAW}) as i:
                    for b in range(2):
                        w, col = at(i, b)
                        wk = w.rearrange("(k p) n -> p k n", p=P)
                        for q in range(4):
                            u = 4 * b + q
                            sp.wait_ge(lo_made, seen(lo_made))
                            sp.dma_start(RAWW[:, u, 0:ku, :],
                                         wk[:, kt0 + q * ku:kt0 + (q + 1) * ku, ds(col, UNIT_COLS)])\
                              .then_inc(landed[u], 16)

            for dst, src in ((PV[:, :], h["params"]), (CF[:, 0:NFIX], h["consts"][:, 0:NFIX]),
                             (CF[:, NFIX:], h["consts"][:, CCOL["tri"]:CCOL["expand"]]),
                             (X[:, :, :], h["x_t"].rearrange("(k p) t -> p k t", p=P))):
                sp.dma_start(dst, src).then_inc(loaded, 16)
            weights(8, lambda i, b: (w_in, i * 512 + b * 256))
            weights(4, lambda i, b: (h["w_o"][0], i * 512 + b * 256))
            for t0, tiles in GROUPS:
                weights(tiles // 2, lambda i, b: (w_up, i * 256 + (t0 * P + b * FF)))
                weights(4, lambda i, b: (w_down, i * 512 + b * 256), ku=tiles // 4, kt0=t0)
            for s_, *_ in STREAMS:
                weights(4, lambda i, b: (h["a_w_in_2"][0, s_], i * 512 + b * 256))
            sp.wait_ge(lo_made, seen.total(lo_made) + RAW)
            for w, n in enumerate(("a_w1_2", "a_a1_2")):
                sp.dma_start(W1S[:, w, :, :], h[n][0].rearrange("(k p) n -> p k n", p=P)).then_inc(lora_in, 16)
            sp.dma_start(EXP3, h["consts"][0:32, CCOL["expand"]:CCOL["expand"] + D]).then_inc(exp_in, 16)
            sp.dma_start(SCAN, h["consts"][:, CCOL["scan"]:CCOL["scan"] + T]).then_inc(lora_in, 16)
            sp.wait_ge(acc_free, 4 + ALL_TILES)
            for w, n in enumerate(("a_w2_2", "a_a2_2")):
                sp.dma_start(W2S[:, w, :], h[n][0]).then_inc(lora_in, 16)
            for f in range(KD):
                sp.wait_ge(lt_ready, f + 1)
                for hh in range(2):
                    dst = lt_dram[8 * f:8 * f + 8].rearrange("(c h) s t -> h s c t", h=2)[hh]
                    sp.dma_start(dst, (XS, US)[f % 2][64 * hh:64 * hh + 64, :, :]).then_inc(lt_stored[f % 2], 16)
            for m in range(2):
                sp.wait_ge(lt_stored[m], 16 * KD)
            sp.wait_ge(tile_done, KD)
            sp.wait_ge(pool_done, KD)
            for b in range(2):
                sp.dma_start(LT[:, b, :, :], lt_dram[:, b * H:(b + 1) * H, b * H:(b + 1) * H]).then_inc(inv_in, 16)
            sp.wait_ge(inverted, 1)
            sp.dma_start(t_dram, TT).then_inc(t_stored, 16)
            sp.wait_ge(t_stored, 16)

            def load_t(g, c):
                m = c % 2
                src = t_dram.rearrange("(f c h) s t -> c h s f t", c=NCH, h=2)
                for hh in range(2):
                    sp.dma_start(blocks(m, TBD)[64 * hh:64 * hh + 64, :, 64 * hh:64 * hh + 64], src[c, hh, :, ds(4 * g, 4), :])\
                      .then_inc(t_loaded[m], 16)
            sp.wait_ge(t_zero, 1)
            seen(y_done, 1)
            load_t(0, 0)
            load_t(0, 1)
            with seen.loop(3, {y_done: 4}) as g:
                for c in range(NCH):
                    sp.wait_ge(y_done, seen(y_done))
                    load_t(g + (c + 2) // NCH, (c + 2) % NCH)
            for c in range(2):
                sp.wait_ge(y_done, seen(y_done))
                load_t(3, c + 2)

            sp.wait_ge(y_done, 1 + 4 * NCH)
            sp.wait_ge(y_out, 1 + 4 * NCH)
            sp.dma_start(EXP4[:, :], h["consts"][0:32, CCOL["expand"]:CCOL["expand"] + D]).then_inc(exp4_in, 16)
            sp.dma_start(G4[:, :, :], g_dram).then_inc(g_loaded, 16)
            weights(4, lambda i, b: (h["a_w_out_2"][0], i * 512 + b * 256))
            for w in (h["w_k_shared_2"], h["w_v_shared_2"]):
                weights(4, lambda i, b: (w, i * 512 + b * 256))
            weights(8, lambda i, b: (h["b_w_qg_2"][0], i * 512 + b * 256))
            weights(4, lambda i, b: (h["b_w_out_2"][0], i * 512 + b * 256))
            out = h["out"].rearrange("(k p) t -> p k t", p=P)
            for q in range(4):
                sp.wait_ge(xn_ready, 4 + q + 1)
                sp.dma_start(out[:, 4 * q:4 * q + 4, :], X[:, 4 * q:4 * q + 4, :]).then_inc(stored, 16)
            sp.wait_ge(stored, 64)

        @block.gpsimd
        def _(pool):
            seen = Counts(pool)
            pool.sem_inc(lo_made, RAW)
            pool.sem_inc(unit_done, SPL)
            pool.sem_inc(acc_free, 4)
            pool.sem_inc(sq_free, 2)
            pool.sem_inc(sc_free, 2)
            pool.sem_inc(y_done, 1)
            pool.sem_inc(y_out, 1)

            pool.wait_ge(acc_free, 4 + 32)
            band0 = CCOL["band"]
            for dst, src in ((HANK[:, :, :], h["bias_rows"]),
                             (FLIP[:, :], h["consts"][:, CCOL["flip"]:CCOL["flip"] + P]),
                             (BAND[:, :, :], h["consts"][:, band0:band0 + 2 * T].rearrange("p (q t) -> p q t", q=2)),
                             (INVC[:, :, :], h["consts"][:, CCOL["invcount"]:CCOL["invcount"] + 4 * T].rearrange("p (g t) -> p g t", g=4)),
                             (POOLW[:, :, :, :], h["pool_w"][0].rearrange("g (c p) d -> p g c d", p=P))):
                pool.dma_start(dst, src).then_inc(side, 16)

            def link(ins):
                ins.then_inc(gstep, 1)
                pool.wait_ge(gstep, seen(gstep))

            U = Z[:, 3 * HT:4 * HT, :]
            src, dst, first = U, PA, 0
            for n, w in enumerate(POOL_WINDOWS):
                r = w // 2
                link(pool.tensor_tensor(dst[:, first:, r:], src[:, first:, r:], src[:, first:, 0:T - r], ALU.add))
                link(pool.tensor_copy(dst[:, first:, 0:r], src[:, first:, 0:r]))
                src, dst, first = dst, (PB if dst is PA else PA), first + 2
            pool.wait_ge(side, 5 * 16)
            for g in range(4):
                W = (PA, PB)[g % 2][:, 2 * g:2 * g + 2, :]
                link(pool.tensor_tensor(W, W, INVC[:, g:g + 1, :].broadcast_to([P, 2, T]), ALU.mult))
                pool.tensor_tensor(W, W, U[:, 2 * g:2 * g + 2, :], ALU.subtract).then_inc(pooled, 1)

            pool.wait_ge(acc_free, 4 + FIRST_TILES + 16)
            pool.dma_start(g_dram, V[:, :, :]).then_inc(g_stored, 16)

            def widen(dst, src):
                return pool.tensor_tensor(dst.rearrange("p i (h t) -> p i h t", h=2), diag(src), MASK4, ALU.mult)

            for s_ in range(KD + 2):
                if s_ < KD:
                    f, p = s_, s_ % 2
                    pool.wait_ge(l_ready, f + 1)
                    if f >= 2:
                        pool.wait_ge(tile_done, f - 1)
                    pool.tensor_tensor(tmp(14 + p), tmp(12 + p), KAP[:, f, :], ALU.subtract).then_inc(lp_ready, 1)
                    pool.tensor_tensor(tmp(24 + p), BON[:, f, :], BET[:, f, :], ALU.mult).then_inc(b1_ready, 1)
                if 1 <= s_ < KD + 1:
                    f, p = s_ - 1, (s_ - 1) % 2
                    pool.wait_ge(decays, f + 1)
                    pool.wait_ge(rk_ready, f + 1)
                    pool.tensor_copy(GCE[:, f, :], tmp(16 + p).rearrange("p (c t) -> p c t", c=NCH)[:, :, CHUNK - 1])
                    pool.tensor_tensor(R[:, f, :], R[:, f, :], tmp(16 + p), ALU.mult).then_inc(pool_done, 1)
                if s_ >= 2:
                    f, p = s_ - 2, s_ % 2
                    pool.wait_ge(tile_done, f + 1)
                    if f >= 2:
                        pool.wait_ge(lt_done, f - 1)
                    widen(FMB[:, p, 0, :, :], BET[:, f, :].rearrange("p (c t) -> p c t", c=NCH)).then_inc(blk_ready, 1)
            pool.wait_ge(tile_done, KD)
            pool.wait_ge(lt_done, KD)
            pool.wait_ge(pool_done, KD)
            link(pool.memset(TT[:, :, :], 0.0))
            pool.memset(TFLAT[:, 0:CHUNK * CHUNK:CHUNK + 1], 1.0).then_inc(inv_init, 1)

            pool.wait_ge(t_stored, 16)
            for m in range(2):
                pool.memset(blocks(m, TBD), 0.0)
                z = pool.memset(cross(m), 0.0)
            z.then_inc(t_zero, 1)

            def widen_step(g, c, first=False):
                m = c % 2
                sl = lambda x: x[:, ds(4 * g, 4), c * CHUNK:(c + 1) * CHUNK]
                if not first:
                    pool.wait_ge(tok_done, seen(tok_done))
                for n, x in enumerate((BET, K, V)):
                    w = widen(FMB[:, m, n, :, :], sl(x))
                w.then_inc(fm_ready, 1)
                if not first:
                    pool.wait_ge(x_done, seen(x_done))
                widen(blocks(m, KBD), sl(KAP)).then_inc(kap_ready, 1)
            widen_step(0, 0, True)
            widen_step(0, 1, True)
            with seen.loop(3, {tok_done: 4, x_done: 4}) as g:
                for c in range(NCH):
                    widen_step(g + (c + 2) // NCH, (c + 2) % NCH)
            for c in range(2):
                widen_step(3, c + 2)

            pool.wait_ge(g_loaded, 16)
            for f in range(KD):
                pool.wait_ge(gn_out, f + 1)
                pool.tensor_tensor(gnt(1, f), gnt(1, f), G4[:, f, :], ALU.mult).then_inc(gn_gated, 1)

            pool.wait_ge(gn_ready, KD)
            pool.dma_start(DIST[:, :, :], h["consts"][:, CCOL["dist"]:CCOL["dist"] + 2 * T].rearrange("p (q t) -> p q t", q=2))\
                .then_inc(dist_in, 16)
            for n in range(KD):
                pool.wait_ge(o_scaled, n + 1)
                pool.tensor_tensor(Q5[:, n, :], Q5[:, n, :], G5[:, n, :], ALU.mult).then_inc(o_gated, 1)

        @block.tensor
        def _(pe):
            seen = Counts(pe)
            seen(lo_made, RAW)

            def gemm(iters, hi, lo, gates, ku=KU):
                with seen.loop(iters, {lo_made: 8, acc_free: 4}):
                    for b in range(2):
                        for q in range(4):
                            slot = q
                            if b == 0 and q < len(gates):
                                pe.wait_ge(*gates[q])
                            pe.wait_ge(lo_made, seen(lo_made))
                            for f in range(2):
                                if q == 0:
                                    pe.wait_ge(acc_free, seen(acc_free))
                                out = ACC[2 * b + f][:, 0:T]
                                for k in range(ku):
                                    kt = q * ku + k
                                    wh = WHI[:, slot, k, f * P:(f + 1) * P]
                                    wl = WLO[:, slot, k, f * P:(f + 1) * P]
                                    first, last = kt == 0, kt == 4 * ku - 1
                                    pe.matmul(out, wh, hi[:, kt, :], start=first, stop=False)
                                    pe.matmul(out, wh, lo[:, kt, :], start=False, stop=False)
                                    mm = pe.matmul(out, wl, hi[:, kt, :], start=False, stop=last)
                            mm.then_inc(unit_done, 1)

            def square_sum():
                for j in range(4):
                    pe.wait_ge(sq_ready, seen(sq_ready))
                    for k in range(4):
                        mm = pe.matmul(AUX[0][:, 0:T], ONES, SQB[0][:, j % 2, k, :],
                                       start=(j + k == 0), stop=(j + k == 6))
                    mm.then_inc(sq_free, 1)

            def quarters(sem_, per):
                base = seen(sem_, 4 * per) - 4 * per
                return [(sem_, base + per * (q + 1)) for q in range(4)]

            pe.wait_ge(loaded, 64)
            SQB = [N1[0]]
            square_sum()
            gemm(8, A1H, A1L, quarters(operand, 1))

            pe.wait_ge(acc_free, 4 + 32)
            for b in range(4):
                for j in range(4):
                    hd, kt = 2 * b + j // 2, j % 2
                    mm = pe.transpose(AUX[b][:, j * P:(j + 1) * P], Z[:, 2 * HT + hd, kt * P:(kt + 1) * P], IDENT)
                mm.then_inc(v_turned, 1)

            def scores(n):
                pe.wait_ge(sc_free, seen(sc_free))
                for q in range(2):
                    out = AUX[n % 2][:, q * T:(q + 1) * T]
                    pe.matmul(out, Z[:, n, q * P:(q + 1) * P], Z[:, HT + n, :], start=True, stop=False)
                    mm = pe.matmul(out, FLIP[:, :], HANK[:, n, (1 - q) * P:(1 - q) * P + T], start=False, stop=True)
                mm.then_inc(scored, 1)

            def turn(n):
                pe.wait_ge(probs, seen(probs))
                if n >= 1:
                    pe.wait_ge(pt_ready, seen(pt_ready))
                for j, (q, kt) in enumerate(((0, 0), (1, 0), (1, 1))):
                    mm = pe.transpose(AUX[2 + n % 2][:, j * P:(j + 1) * P], SS[:, n % 2, q, kt * P:(kt + 1) * P], IDENT)
                mm.then_inc(turned, 1)

            def pv(n):
                if n == 7:
                    pe.wait_ge(pt_ready, seen(pt_ready))
                if n >= 2:
                    pe.wait_ge(mix_ready, seen(mix_ready))
                out = ACC[n % 2]
                pe.matmul(out[:, 0:T], VTOK[:, n, 0, :], PT[:, n % 2, 0:T], start=True, stop=False)
                pe.matmul(out[:, P:T], VTOK[:, n, 1, :], PT[:, n % 2, T:384], start=False, stop=True).then_inc(pv_done, 1)

            pe.wait_ge(side, 5 * 16)
            pe.wait_ge(v_tok, 4)
            scores(0)
            for s in range(8 + 2):
                if s < 7:
                    scores(s + 1)
                if 1 <= s < 9:
                    turn(s - 1)
                if s >= 2:
                    pv(s - 2)
            pe.wait_ge(pooled, 4)
            for n in range(8):
                g, d = n // 2, n % 2
                if n >= 2:
                    pe.wait_ge(mix_ready, 8 + n - 1)
                for c in range(2):
                    mm = pe.matmul(ACC[2 + n % 2][:, 0:T], POOLW[:, g, c, d * P:(d + 1) * P],
                                   (PA, PB)[g % 2][:, 2 * g + c, :], start=(c == 0), stop=(c == 1))
                mm.then_inc(mixed, 1)
            gemm(4, B1H, B1L, [(mix_ready, 16)])
            seen(mix_ready, 10)

            SQB[0] = N2[0]
            square_sum()
            square_sum()
            gates = quarters(operand, 1)
            for t0, tiles in GROUPS:
                gemm(tiles // 2, A2H, A2L, gates)
                gemm(4, B2H, B2L, quarters(gated_ready, tiles // 4), ku=tiles // 4)

            SQB[0] = N2[0]
            square_sum()
            for s_, ah, al, _ in STREAMS:
                gemm(4, ah, al, quarters(operand, 1))
            pe.wait_ge(acc_free, seen.total(acc_free) + 4)

            for f in range(KD):
                pe.wait_ge(kk_sq, f + 1)
                pe.matmul(AUX[2][0:32, 0:T], HEADSEL[:, 30 - 2 * f:62 - 2 * f], tmp(16 + f % 4), start=(f == 0), stop=(f == KD - 1))\
                    .then_inc(kk_summed, 1)

            pe.wait_ge(lora_in, 80)
            pe.wait_ge(xw_ready, 4)
            for w, x in enumerate((KAP, BET)):
                for k in range(KD):
                    mm = pe.matmul(AUX[w][0:LORA, 0:T], W1S[:, w, k, :], x[:, k, :], start=(k == 0), stop=(k == KD - 1))
                mm.then_inc(low_done, 1)
            pe.wait_ge(exp_in, 16)
            pe.wait_ge(kk_inverse, 1)
            pe.wait_ge(low_ready, 2)
            for f in range(KD):
                if f >= 2:
                    pe.wait_ge(kk_ready, f - 1)
                pe.matmul(AUX[f % 2][:, 0:T], EXP3[:, f * P:(f + 1) * P], tmp(20)[0:32, :], start=True, stop=True).then_inc(kk_wide, 1)
            for n in range(2 * KD):
                f, w = n // 2, n % 2
                if n < 2:
                    pe.wait_ge(low_ready, n + 1)
                if n >= 4:
                    pe.wait_ge(sig_ready, n - 3)
                pe.matmul(ACC[n % 4][:, 0:T], W2S[:, w, f * P:(f + 1) * P], LOW[:, w, :], start=True, stop=True).then_inc(lora_done, 1)
            for s_ in range(KD + 3):
                if s_ < KD:
                    f = s_
                    pe.wait_ge(rk_ready, f + 1)
                    if f >= 2:
                        pe.wait_ge(tile_done, f - 1)
                    pe.matmul(AUX[2 + f % 2][:, 0:T], HEADONES, tmp(26 + f % 2), start=True, stop=True).then_inc(bonus_sum, 1)
                if s_ >= 3:
                    f = s_ - 3
                    pe.wait_ge(blk_ready, f + 1)
                    if f >= 2:
                        pe.wait_ge(lt_ready, f - 1)
                    for c in range(NCH):
                        mm = pe.matmul(ACC[f % 2][:, c * CHUNK:(c + 1) * CHUNK], FMB[:, f % 2, 0, c, :],
                                       KAP[:, f, c * CHUNK:(c + 1) * CHUNK], start=(c == 0), stop=(c == NCH - 1))
                    mm.then_inc(lt_done, 1)

            def pairs(g, c, first=False):
                m = c % 2
                fm = FMB[:, m, :, :, :]
                pe.wait_ge(fm_ready, seen(fm_ready))
                if not first:
                    pe.wait_ge(rest_out, seen(rest_out))
                for i in range(4):
                    rho_kappa = RK[:, :, ds(4 * g + i, 1), c * CHUNK:(c + 1) * CHUNK]
                    pe.matmul(ACC[0][:, i * P:(i + 1) * P], fm[:, 1, i, :], rho_kappa, start=(i == 0), stop=(i == 3))
                    mm = pe.matmul(ACC[1][:, i * P:(i + 1) * P], fm[:, 0, i, :], rho_kappa, start=(i == 0), stop=(i == 3))
                mm.then_inc(prep_done, 1)

            def turns(g, c, first=False):
                m = c % 2
                if not first:
                    pe.wait_ge(tok_out, seen(tok_out))
                for n, bank in ((2, AUX[2]), (0, ACC[2]), (1, ACC[3])):
                    for i in range(4):
                        mm = pe.transpose(bank[:, i * P:(i + 1) * P], FMB[:, m, n, i, :], IDENT)
                    if n == 2:
                        mm.then_inc(v_done, 1)
                mm.then_inc(tok_done, 1)

            def four(bank, lhs, rhs, start, stop):
                for i in range(4):
                    mm = pe.matmul(bank[:, i * CHUNK:(i + 1) * CHUNK], lhs[:, i, :], rhs(i), start=(start and i == 0),
                                   stop=(stop and i == 3))
                return mm

            def step(g, c, nxt):
                m = c % 2
                of = lambda x: (lambda i: x[:, i, :])
                pe.wait_ge(pairs_read, seen(pairs_read))
                pe.wait_ge(vc_ready, seen(vc_ready))
                pe.wait_ge(kap_ready, seen(kap_ready))
                mm = four(AUX[0], blocks(m, AKK), of(small(m, VC)), True, c == 0)
                if c > 0:
                    pe.wait_ge(s_ready, seen(s_ready))
                    mm = four(AUX[0], blocks(m, KBD), of(S), False, True)
                mm.then_inc(x_done, 1)
                pe.wait_ge(t_loaded[m], seen(t_loaded[m], 32))
                pe.wait_ge(xs_ready, seen(xs_ready))
                four(AUX[1], blocks(m, TBD), of(XS), True, True).then_inc(u_done, 1)
                if nxt:
                    pairs(*nxt)
                pe.wait_ge(us_ready, seen(us_ready))
                four(AUX[0], cross(m), of(US), True, True).then_inc(w_done, 1)
                pe.wait_ge(tok_out, seen(tok_out, 1, "step"))
                if c < 3:
                    four(AUX[3], blocks(m, KT), of(small(m, VC)), True, False)
                pe.wait_ge(ws_ready, seen(ws_ready))
                four(AUX[1], blocks(m, TBD), of(XS), True, True).then_inc(u_done, 1)
                if nxt:
                    turns(*nxt)
                pe.wait_ge(us_ready, seen(us_ready))
                if c < 3:
                    four(AUX[3], blocks(m, BT), of(US), False, True).then_inc(s_done, 1)
                pe.wait_ge(rest_out, seen(rest_out, 1, "step"))
                y = AUX[1][:, T:]
                four(y, blocks(m, VBD), of(small(m, ARK)), True, False)
                if c > 0:
                    pe.wait_ge(sbd_ready, seen(sbd_ready))
                    four(y, SBD, lambda i: R[:, ds(4 * g + i, 1), c * CHUNK:(c + 1) * CHUNK], False, False)
                pe.wait_ge(ubd_ready, seen(ubd_ready))
                four(y, UBD, of(small(m, ARB)), False, True).then_inc(y_done, 1)

            pairs(0, 0, True)
            turns(0, 0, True)
            with seen.loop(3, {fm_ready: 4, rest_out: 4, (rest_out, "step"): 4, pairs_read: 4, tok_out: 4, (tok_out, "step"): 4,
                               kap_ready: 4, vc_ready: 4, s_ready: 3, xs_ready: 4, ws_ready: 4, t_loaded[0]: 64, t_loaded[1]: 64,
                               sbd_ready: 3, us_ready: 8, ubd_ready: 4}) as g:
                for c in range(NCH):
                    step(g, c, (g + (c + 1) // NCH, (c + 1) % NCH))
            for c in range(NCH):
                step(3, c, (3, c + 1) if c < 3 else None)

            pe.wait_ge(y_out, 1 + 4 * NCH)
            for s_ in range(KD + 2):
                if s_ < KD:
                    if s_ >= 2:
                        pe.wait_ge(gn_centred, s_ - 1)
                    pe.matmul(AUX[s_ % 2][:, 0:T], HEADONES, BET[:, s_, :], start=True, stop=True).then_inc(gn_sum, 1)
                if s_ >= 2:
                    f = s_ - 2
                    pe.wait_ge(gn_sq, f + 1)
                    pe.matmul(AUX[2][0:32, 0:T], HEADSEL[:, 30 - 2 * f:62 - 2 * f], gnt(0, f), start=(f == 0), stop=(f == KD - 1))\
                        .then_inc(gn_sq_sum, 1)
            pe.wait_ge(exp4_in, 16)
            pe.wait_ge(gn_rstd, 1)
            for f in range(KD):
                if f >= 2:
                    pe.wait_ge(gn_out, f - 1)
                pe.matmul(AUX[f % 2][:, 0:T], EXP4[:, f * P:(f + 1) * P], RS4[:, 1, :], start=True, stop=True).then_inc(gn_wide, 1)
            gemm(4, C4H, C4L, quarters(gn_ready, 4))

            def layer_sums(bufs):
                for q in range(4):
                    pe.wait_ge(xr_ready, seen(xr_ready))
                    for k in range(4):
                        mm = pe.matmul(AUX[1][:, 0:T], ONES, X[:, 4 * q + k, :], start=(q + k == 0), stop=(q + k == 6))
                mm.then_inc(ln_sum, 1)
                SQB[0] = bufs[0]
                square_sum()
            layer_sums(L4)

            gates = quarters(operand, 1)
            for n in range(4):
                gemm(4, A5H, A5L, gates)
            pe.wait_ge(acc_free, seen.total(acc_free) + 4)
            pe.wait_ge(lam_prod, 1)
            pe.matmul(AUX[0][:, 0:2], ONES, LAM[:, 0:2], start=True, stop=True).then_inc(lam_sum, 1)
            for n in range(8):
                if n >= 4:
                    pe.wait_ge(v5_tok, n - 3)
                for j in range(4):
                    mm = pe.transpose(ACC[n % 4][:, j * P:(j + 1) * P], VS5[:, 4 * (n % 4) + j, (n // 4) * P:(n // 4 + 1) * P], IDENT)
                mm.then_inc(v5_turned, 1)

            def scores(n):
                if n >= 2:
                    pe.wait_ge(d_max, n - 1)
                for m in range(2):
                    for q in range(2):
                        mm = pe.matmul(AUX[2 * (n % 2) + m][:, q * T:(q + 1) * T], Q5[:, 2 * n + m, q * P:(q + 1) * P],
                                       KS5[:, 2 * n + m, :], start=(q == 0), stop=(q == 1))
                mm.then_inc(d_scored, 1)

            def turn(n):
                pe.wait_ge(d_probs, n + 1)
                if n >= 2:
                    pe.wait_ge(d_pt, n - 1)
                for j, (q, kt) in enumerate(((0, 0), (1, 0), (1, 1))):
                    mm = pe.transpose(ACC[2 + n % 2][:, j * P:(j + 1) * P], SS5[:, n % 2, q, kt * P:(kt + 1) * P], IDENT)
                mm.then_inc(d_turned, 1)

            def pv(n):
                pe.wait_ge(d_pt, n + 1)
                if n >= 2:
                    pe.wait_ge(o_out, n - 1)
                out = ACC[n % 2]
                for d in range(2):
                    pe.matmul(out[:, d * T:(d + 1) * T], VT5[:, 0, 2 * n + d, :], PT5[:, n % 2, 0:T], start=(d == 0), stop=False)
                    mm = pe.matmul(out[:, d * T + P:(d + 1) * T], VT5[:, 1, 2 * n + d, :], PT5[:, n % 2, T:384], start=False, stop=(d == 1))
                mm.then_inc(d_pv, 1)

            pe.wait_ge(v5_tok, 8)
            pe.wait_ge(lam_exp, 1)
            scores(0)
            for s_ in range(8 + 2):
                if s_ < 7:
                    scores(s_ + 1)
                if 1 <= s_ < 9:
                    turn(s_ - 1)
                if s_ >= 2:
                    pv(s_ - 2)
            for n in range(8):
                pe.wait_ge(o_sq, n + 1)
                if n >= 2:
                    pe.wait_ge(o_var, n - 1)
                for d in range(2):
                    mm = pe.matmul(AUX[n % 2][:, 0:T], ONES, SS5[:, n % 2, d, :], start=(d == 0), stop=(d == 1))
                mm.then_inc(o_sum, 1)
            gemm(4, C5H, C5L, quarters(o_ready, 4))
            layer_sums(L5)

        @block.scalar
        def _(act):
            seen = Counts(act)
            seen(unit_done, SPL, "tile")
            seen(acc_free, 4, "tile")

            def gemm(iters, evac, pending=None, ku=KU, keep=False):
                def split(b):
                    for q in range(4):
                        u = 4 * b + q
                        act.wait_ge(landed[u], seen(landed[u], 16))
                        act.wait_ge(unit_done, seen(unit_done))
                        act.activation(WHI[:, q, 0:ku, :], RAWW[:, u, 0:ku, :], ACT.Copy).then_inc(hi_made, 1)

                def out(i, j0):
                    act.wait_ge(unit_done, seen(unit_done, 4, "tile"))
                    seen(acc_free, 2, "tile")
                    evac(i, j0)

                split(0)
                if pending is not None:
                    pending()
                split(1)
                out(0, 0)
                with seen.loop(iters - 1, {**{s: 16 for s in landed}, unit_done: 8, (unit_done, "tile"): 8,
                                           (acc_free, "tile"): 4, **evac.per}) as j:
                    split(0)
                    out(j, 2)
                    split(1)
                    out(j + 1, 0)

                def rest():
                    out(iters - 1, 2)
                    if evac.last:
                        evac.last(iters)
                if keep:
                    return rest
                rest()

            def copier(dst, scale=1.0, tile0=0):
                def evac(i, j0):
                    for j in (j0, j0 + 1):
                        act.activation(dst[:, ds(4 * i + (tile0 + j), 1), :], ACC[j][:, 0:T].rearrange("p (o t) -> p o t", o=1), ACT.Copy, scale=scale)\
                           .then_inc(acc_free, 1)
                evac.per, evac.last = {}, None
                return evac

            def squares(src, sq, ready=None):
                for j in range(4):
                    if ready is not None:
                        act.wait_ge(ready, seen(ready))
                    act.wait_ge(sq_free, seen(sq_free))
                    act.activation(sq[:, j % 2, :, :], src[:, 4 * j:4 * j + 4, :], ACT.Square).then_inc(sq_ready, 1)

            def rsqrt(ms, rstd):
                act.wait_ge(var_ready, seen(var_ready))
                act.activation(rstd[:, :], ms[:, :], ACT.Sqrt).then_inc(rstd_ready, 1)

            def operand_hi(ht, hi):
                for j in range(4):
                    act.wait_ge(normed, seen(normed))
                    act.activation(hi[:, 4 * j:4 * j + 4, :], ht[:, j % 2, :, :], ACT.Copy).then_inc(nh_made, 1)

            act.wait_ge(loaded, 64)
            squares(X, N1[0])
            rsqrt(N1[2], N1[3])
            operand_hi(N1[1], A1H)
            rest = None
            pend = gemm(2, copier(Z, HEAD_SCALE), keep=True)
            gemm(6, copier(Z, tile0=8), pending=pend)

            for b in range(4):
                act.wait_ge(v_turned, seen(v_turned))
                act.activation(VTOK[:, 2 * b:2 * b + 2, :, :], AUX[b][:, :].rearrange("p (a b c) -> p a b c", a=2, b=2), ACT.Copy).then_inc(v_tok, 1)

            def exps(n):
                act.wait_ge(maxed, seen(maxed))
                for q in range(2):
                    e = act.activation(SS[:, n % 2, q, :], SS[:, n % 2, q, :], ACT.Exp, bias=ST[:, n % 2, q:q + 1],
                                       accum_out=ST[:, n % 2, 2 + q:3 + q])
                e.then_inc(expd, 1)

            def turned_out(n):
                act.wait_ge(turned, seen(turned))
                if n >= 2:
                    act.wait_ge(pv_done, n - 1)
                act.activation(PT[:, n % 2, :], AUX[2 + n % 2][:, 0:384], ACT.Copy).then_inc(pt_ready, 1)

            def head_hi(n):
                act.wait_ge(pv_done, n + 1)
                act.activation(B1H[:, n, :], ACC[n % 2][:, 0:T], ACT.Copy).then_inc(pv_hi, 1)

            for s in range(8 + 2):
                if s < 8:
                    exps(s)
                if 1 <= s < 9:
                    turned_out(s - 1)
                if s >= 2:
                    head_hi(s - 2)
            ps = COL["pool_scale"]
            for n in range(8):
                act.wait_ge(mixed, seen(mixed))
                act.activation(B1H[:, HT + n, :], ACC[2 + n % 2][:, 0:T], ACT.Copy, scale=PV[:, ps + n:ps + n + 1])\
                   .then_inc(mixed_hi, 1)
            gemm(4, copier(Y))

            squares(Y, N2[0])
            rsqrt(N2[2], N2[3])
            squares(X, N2[0], x_ready)
            rsqrt(N2[2], N2[3])
            operand_hi(N2[1], A2H)

            def up_evac(t0):
                cw, cb = COL["conv_w"], COL["conv_b"]

                def base(i, j):
                    col = 2 * i + (t0 + (j % 2) + KF * (j // 2))
                    act.activation(CV[:, j, :], ACC[j][:, 0:T], ACT.Identity,
                                   bias=PV[:, ds(col + cb, 1)], scale=PV[:, ds(col + (cw + 4 * KF), 1)]).then_inc(conv_base, 1)

                def split(i):
                    act.wait_ge(gated, seen(gated, 2))
                    act.activation(B2H[:, ds(2 * i, 2), :], HG[:, :, :], ACT.Copy).then_inc(gated_hi, 1)

                def evac(i, j0):
                    if j0 == 0:
                        if not isinstance(i, int):
                            split(i - 1)
                        base(i, 0)
                        base(i, 1)
                    else:
                        base(i, 2)
                        base(i, 3)
                        act.wait_ge(acc_free, seen(acc_free, 0, "tile") - 2)
                        for j in range(2):
                            act.activation(GE[:, j, :], CV[:, j, :], ACT.Gelu_apprx_tanh).then_inc(gelu_done, 1)
                evac.per = {gated: 2}
                evac.last = lambda iters: split(iters - 1)
                return evac

            def adder():
                def evac(i, j0):
                    pass
                evac.per, evac.last = {}, None
                return evac

            pend = None
            for n, (t0, tiles) in enumerate(GROUPS):
                pend = gemm(tiles // 2, up_evac(t0), pending=pend, keep=True)
                pend = gemm(4, copier(Y) if n == 0 else adder(), pending=pend, ku=tiles // 4, keep=True)
            pend()

            act.wait_ge(acc_free, 4 + FIRST_TILES)
            squares(Y, N2[0])
            rsqrt(N2[2], N2[3])

            def with_side(evac, side, per):
                def both(i, j0):
                    evac(i, j0)
                    if j0 == 0:
                        side(i)
                both.per, both.last = {**evac.per, **per}, evac.last
                return both

            def mixed_hi_part(hi):
                def side(i):
                    act.wait_ge(normed, seen(normed))
                    act.activation(hi[:, ds(4 * i, 4), :], HT3[:, :, :], ACT.Copy).then_inc(nh_made, 1)
                return side

            def silu_out(dst):
                def evac(i, j0):
                    for j in (j0, j0 + 1):
                        act.activation(dst[:, ds(4 * i + j, 1), :], ACC[j][:, 0:T].rearrange("p (o t) -> p o t", o=1), ACT.Silu)\
                           .then_inc(acc_free, 1)
                evac.per, evac.last = {}, None
                return evac

            first_part = mixed_hi_part(A3H)
            for i in range(4):
                first_part(i)
            pend = None
            for n, (s_, _, _, dst) in enumerate(STREAMS):
                ev = silu_out(dst) if n == 0 else copier(dst)
                if n < 3:
                    ev = with_side(ev, mixed_hi_part(STREAMS[n + 1][1]), {normed: 1})
                if n == 3:
                    pend()
                    pend = None
                    act.wait_ge(g_stored, 16)
                pend = gemm(4, ev, pending=pend, keep=True)
            pend()

            act.wait_ge(acc_free, 4 + ALL_TILES)
            for f in range(KD):
                if f >= 4:
                    act.wait_ge(kk_summed, f - 3)
                c = COL["a_k_k_2"] + f
                act.activation(tmp(16 + f % 4), K[:, f, :], ACT.Square, scale=PV[:, c:c + 1]).then_inc(kk_sq, 1)

            act.wait_ge(kk_summed, KD)
            act.activation(tmp(20)[0:32, :], AUX[2][0:32, 0:T], ACT.Sqrt).then_inc(kk_norm, 1)
            act.wait_ge(low_done, 1)
            act.activation(LOW[:, 0, :], AUX[0][0:LORA, 0:T], ACT.Tanh).then_inc(low_ready, 1)
            act.wait_ge(low_done, 2)
            act.activation(LOW[:, 1, :], AUX[1][0:LORA, 0:T], ACT.Copy).then_inc(low_ready, 1)
            for n in range(2 * KD):
                f, w = n // 2, n % 2
                act.wait_ge(lora_done, n + 1)
                b = COL[("a_w0_2", "a_a0_2")[w]] + f
                act.activation((KAP, BET)[w][:, f, :], ACC[n % 4][:, 0:T], ACT.Sigmoid, bias=PV[:, b:b + 1]).then_inc(sig_ready, 1)
            for f in range(KD):
                p = f % 2
                act.wait_ge(l_ready, f + 1)
                if f >= 2:
                    act.wait_ge(tile_done, f - 1)
                    act.wait_ge(pool_done, f - 1)
                act.activation(tmp(16 + p), tmp(12 + p), ACT.Exp, scale=DECAY)
                act.activation(tmp(18 + p), tmp(12 + p), ACT.Exp, scale=-DECAY)
                act.wait_ge(lp_ready, f + 1)
                act.activation(tmp(20 + p), tmp(14 + p), ACT.Exp, scale=DECAY).then_inc(decays, 1)

            def step(g, c, nxt):
                m = c % 2
                w4 = lambda bank: bank[:, 0:T].rearrange("p (i c) -> p i c", i=4)

                act.wait_ge(x_done, seen(x_done))
                act.activation(XS[:, :, :], w4(AUX[0]), ACT.Copy).then_inc(xs_ready, 1)
                act.wait_ge(u_done, seen(u_done))
                act.activation(US[:, :, :], w4(AUX[1]), ACT.Copy).then_inc(us_ready, 1)
                act.wait_ge(tok_done, seen(tok_done))
                act.activation(blocks(m, BT), ACC[2][:, :].rearrange("p (i c) -> p i c", i=4), ACT.Copy)
                act.activation(blocks(m, KT), ACC[3][:, :].rearrange("p (i c) -> p i c", i=4), ACT.Copy).then_inc(tok_out, 1)
                act.wait_ge(u_done, seen(u_done))
                act.activation(US[:, :, :], w4(AUX[1]), ACT.Copy).then_inc(us_ready, 1)
                if nxt:
                    v_copy(*nxt)
                act.wait_ge(y_done, seen(y_done))
                act.activation(BET[:, ds(4 * g, 4), c * CHUNK:(c + 1) * CHUNK], w4(AUX[1][:, T:]), ACT.Copy).then_inc(y_out, 1)

            def v_copy(g, c):
                act.wait_ge(v_done, seen(v_done))
                act.activation(blocks(c % 2, VBD), AUX[2][:, :].rearrange("p (i c) -> p i c", i=4), ACT.Copy).then_inc(vb_ready, 1)

            act.wait_ge(t_stored, 16)
            seen(y_done, 1)
            v_copy(0, 0)
            with seen.loop(3, {tok_done: 4, x_done: 4, u_done: 8, y_done: 4, v_done: 4}) as g:
                for c in range(NCH):
                    step(g, c, (g + (c + 1) // NCH, (c + 1) % NCH))
            for c in range(NCH):
                step(3, c, (3, c + 1) if c < 3 else None)

            for f in range(KD):
                act.wait_ge(gn_centred, f + 1)
                if f >= 4:
                    act.wait_ge(gn_sq_sum, f - 3)
                act.activation(gnt(0, f), BET[:, f, :], ACT.Square).then_inc(gn_sq, 1)
            act.wait_ge(gn_var, 1)
            act.activation(RS4[:, 1, :], RS4[:, 0, :], ACT.Sqrt).then_inc(gn_rstd, 1)
            for f in range(KD):
                act.wait_ge(gn_gated, f + 1)
                act.activation(C4H[:, f, :], gnt(1, f), ACT.Copy).then_inc(gn_hi, 1)
            gemm(4, copier(Y4))

            def layer_norm_part(bufs):
                squares(X, bufs[0], xc_ready)
                rsqrt(bufs[2], bufs[3])

            def split_x(hi):
                for q in range(4):
                    act.wait_ge(xn_ready, q + 1)
                    act.activation(hi[:, 4 * q:4 * q + 4, :], X[:, 4 * q:4 * q + 4, :], ACT.Copy).then_inc(nh_made, 1)

            layer_norm_part(L4)

            split_x(A5H)
            pend = gemm(4, copier(KS5), keep=True)
            pend = gemm(4, copier(VS5), pending=pend, keep=True)
            pend = gemm(4, copier(Q5, HEAD_SCALE), pending=pend, keep=True)
            gemm(4, silu_out(G5), pending=pend)
            act.wait_ge(lam_sum, 1)
            act.activation(LAM[:, 2:4], AUX[0][:, 0:2], ACT.Exp).then_inc(lam_exp, 1)
            for n in range(8):
                act.wait_ge(v5_turned, n + 1)
                act.activation(VT5[:, n // 4, 4 * (n % 4):4 * (n % 4) + 4, :], ACC[n % 4][:, :].rearrange("p (a b) -> p a b", a=4), ACT.Copy)\
                   .then_inc(v5_tok, 1)

            for s_ in range(8 + 2):
                if s_ < 8:
                    act.wait_ge(d_max, s_ + 1)
                    for m in range(4):
                        e = act.activation(SS5[:, s_ % 2, m, :], SS5[:, s_ % 2, m, :], ACT.Exp, bias=ST5[:, s_ % 2, m:m + 1],
                                           accum_out=ST5[:, s_ % 2, 4 + m:5 + m])
                    e.then_inc(d_exp, 1)
                if 1 <= s_ < 9:
                    n = s_ - 1
                    act.wait_ge(d_turned, n + 1)
                    if n >= 2:
                        act.wait_ge(d_pv, n - 1)
                    act.activation(PT5[:, n % 2, :], ACC[2 + n % 2][:, 0:384], ACT.Copy).then_inc(d_pt, 1)
                if s_ >= 2:
                    n = s_ - 2
                    act.wait_ge(d_pv, n + 1)
                    act.activation(Q5[:, 2 * n:2 * n + 2, :], ACC[n % 2][:, :].rearrange("p (d t) -> p d t", d=2), ACT.Copy).then_inc(o_out, 1)
            act.wait_ge(o_out, 8)
            for s_ in range(8 + 2):
                if s_ < 8:
                    n = s_
                    if n >= 2:
                        act.wait_ge(o_sum, n - 1)
                    act.activation(SS5[:, n % 2, 0:2, :], Q5[:, 2 * n:2 * n + 2, :], ACT.Square).then_inc(o_sq, 1)
                if 1 <= s_ < 9:
                    n = s_ - 1
                    act.wait_ge(o_var, n + 1)
                    act.activation(SS5[:, n % 2, 3, :], SS5[:, n % 2, 2, :], ACT.Sqrt).then_inc(o_rstd, 1)
                if s_ >= 2:
                    n = s_ - 2
                    act.wait_ge(o_gated, 2 * n + 2)
                    act.activation(C5H[:, 2 * n:2 * n + 2, :], Q5[:, 2 * n:2 * n + 2, :], ACT.Copy).then_inc(o_hi, 1)
            gemm(4, copier(Y5))
            layer_norm_part(L5)

        @block.vector
        def _(dve):
            seen = Counts(dve)
            seen(unit_done, SPL, "tile")
            seen(acc_free, 4, "tile")
            seen(sq_free, 2)

            def link(ins):
                ins.then_inc(dstep, 1)
                dve.wait_ge(dstep, seen(dstep))

            def gemm(iters, evac, pending=None, ku=KU, keep=False):
                def split(b):
                    for q in range(4):
                        u = 4 * b + q
                        dve.wait_ge(hi_made, seen(hi_made))
                        dve.tensor_tensor(WLO[:, q, 0:ku, :], RAWW[:, u, 0:ku, :],
                                          WHI[:, q, 0:ku, :].bitcast(F32), ALU.subtract)\
                           .then_inc(lo_made, 1)

                def out(i, j0):
                    seen(unit_done, 4, "tile")
                    seen(acc_free, 2, "tile")
                    evac(i, j0)

                split(0)
                if pending is not None:
                    pending()
                split(1)
                out(0, 0)
                with seen.loop(iters - 1, {hi_made: 8, (unit_done, "tile"): 8, (acc_free, "tile"): 4,
                                           **evac.per}) as j:
                    split(0)
                    out(j, 2)
                    split(1)
                    out(j + 1, 0)

                def rest():
                    out(iters - 1, 2)
                    if evac.last:
                        evac.last(iters)
                if keep:
                    return rest
                rest()

            def idle():
                def evac(i, j0):
                    pass
                evac.per, evac.last = {}, None
                return evac

            def variance(ms, eps=NORM_EPS):
                dve.wait_ge(sq_free, seen(sq_free, 4))
                link(dve.tensor_scalar(ms[:, :], AUX[0][:, 0:T], 1.0 / D, eps, ALU.mult, ALU.add))
                dve.reciprocal(ms[:, :], ms[:, :]).then_inc(var_ready, 1)

            def apply_norm(src, gain, ht, rstd, hi, lo):
                def low(j):
                    dve.wait_ge(nh_made, seen(nh_made))
                    dve.tensor_tensor(lo[:, 4 * j:4 * j + 4, :], ht[:, j % 2, :, :],
                                      hi[:, 4 * j:4 * j + 4, :].bitcast(F32), ALU.subtract).then_inc(operand, 1)
                g = COL[gain]
                dve.wait_ge(rstd_ready, seen(rstd_ready))
                for j in range(4):
                    if j >= 2:
                        dve.wait_ge(operand, seen(operand))
                    for k in range(4):
                        kt = 4 * j + k
                        ins = dve.scalar_tensor_tensor(ht[:, j % 2, k, :], src[:, kt, :], PV[:, g + kt:g + kt + 1],
                                                       rstd[:, :], ALU.mult, ALU.mult)
                    ins.then_inc(normed, 1)
                    if j >= 1:
                        low(j - 1)
                low(3)
                seen(operand, 2)

            def add_norm(src, gain, rstd):
                g = COL[gain]
                dve.wait_ge(rstd_ready, seen(rstd_ready))
                for j in range(4):
                    for k in range(4):
                        kt = 4 * j + k
                        ins = dve.scalar_tensor_tensor(src[:, kt, :], src[:, kt, :], PV[:, g + kt:g + kt + 1],
                                                       rstd[:, :], ALU.mult, ALU.mult)
                    link(ins)
                    dve.tensor_tensor(X[:, 4 * j:4 * j + 4, :], X[:, 4 * j:4 * j + 4, :],
                                      src[:, 4 * j:4 * j + 4, :], ALU.add).then_inc(x_ready, 1)

            dve.wait_ge(loaded, 64)
            variance(N1[2])
            apply_norm(X, "pre_mix_g", N1[1], N1[3], A1H, A1L)
            p_ = gemm(2, idle(), keep=True)
            gemm(6, idle(), pending=p_)

            dve.wait_ge(side, 5 * 16)

            def softmax_max(n):
                dve.wait_ge(scored, seen(scored))
                if n >= 2:
                    dve.wait_ge(turned, n - 1)
                s = dve.tensor_tensor(SS[:, n % 2, :, :], AUX[n % 2][:, :].rearrange("p (q t) -> p q t", q=2), BAND[:, :, :], ALU.add)
                s.then_inc(sc_free, 1)
                dve.wait_ge(sc_free, 2 + n + 1)
                link(dve.tensor_reduce(ST[:, n % 2, 0:2], SS[:, n % 2, :, :], AX.X, ALU.max))
                dve.tensor_scalar(ST[:, n % 2, 0:2], ST[:, n % 2, 0:2], -1.0, None, ALU.mult).then_inc(maxed, 1)

            def softmax_norm(n):
                dve.wait_ge(expd, seen(expd))
                link(dve.reciprocal(ST[:, n % 2, 2:4], ST[:, n % 2, 2:4]))
                for q in range(2):
                    ins = dve.tensor_scalar(SS[:, n % 2, q, :], SS[:, n % 2, q, :], ST[:, n % 2, 2 + q:3 + q], None, ALU.mult)
                ins.then_inc(probs, 1)

            def head_lo(n):
                dve.wait_ge(pv_hi, seen(pv_hi))
                dve.tensor_tensor(B1L[:, n, :], ACC[n % 2][:, 0:T], B1H[:, n, :].bitcast(F32), ALU.subtract).then_inc(mix_ready, 1)

            for s in range(8 + 2):
                if s < 8:
                    softmax_max(s)
                if 1 <= s < 9:
                    softmax_norm(s - 1)
                if s >= 2:
                    head_lo(s - 2)
            ps = COL["pool_scale"]
            for n in range(8):
                dve.wait_ge(mixed_hi, seen(mixed_hi))
                dve.scalar_tensor_tensor(B1L[:, HT + n, :], ACC[2 + n % 2][:, 0:T], PV[:, ps + n:ps + n + 1],
                                         B1H[:, HT + n, :].bitcast(F32), ALU.mult, ALU.subtract).then_inc(mix_ready, 1)
            gemm(4, idle())

            variance(N2[2])
            add_norm(Y, "post_mix_g", N2[3])
            variance(N2[2])
            apply_norm(X, "pre_ffn_g", N2[1], N2[3], A2H, A2L)

            def up_evac(t0):
                cw = COL["conv_w"]

                def conv(i, j):
                    col = 2 * i + (t0 + (j % 2) + KF * (j // 2))
                    dve.wait_ge(conv_base, seen(conv_base))
                    link(dve.scalar_tensor_tensor(CV[:, j, 1:T], ACC[j][:, 0:T - 1], PV[:, ds(col + (cw + 2 * KF), 1)],
                                                  CV[:, j, 1:T], ALU.mult, ALU.add))
                    dve.scalar_tensor_tensor(CV[:, j, 2:T], ACC[j][:, 0:T - 2], PV[:, ds(col + cw, 1)],
                                             CV[:, j, 2:T], ALU.mult, ALU.add).then_inc(acc_free, 1)

                def low(i):
                    dve.wait_ge(gated_hi, seen(gated_hi))
                    dve.tensor_tensor(B2L[:, ds(2 * i, 2), :], HG[:, :, :], B2H[:, ds(2 * i, 2), :].bitcast(F32),
                                      ALU.subtract).then_inc(gated_ready, 2)

                def evac(i, j0):
                    if j0 == 0:
                        if not isinstance(i, int):
                            low(i - 1)
                        conv(i, 0)
                        conv(i, 1)
                    else:
                        conv(i, 2)
                        conv(i, 3)
                        dve.wait_ge(acc_free, seen(acc_free, 0, "tile"))
                        for j in range(2):
                            dve.wait_ge(gelu_done, seen(gelu_done))
                            dve.tensor_tensor(HG[:, j, :], GE[:, j, :], CV[:, 2 + j, :], ALU.mult).then_inc(gated, 1)
                evac.per = {conv_base: 4, dstep: 4, gelu_done: 2, gated_hi: 1}
                evac.last = lambda iters: low(iters - 1)
                return evac

            def adder():
                def evac(i, j0):
                    dve.wait_ge(unit_done, seen(unit_done, 0, "tile"))
                    for j in (j0, j0 + 1):
                        y = Y[:, ds(4 * i + j, 1), :]
                        dve.tensor_tensor(y, ACC[j][:, 0:T].rearrange("p (o t) -> p o t", o=1), y, ALU.add).then_inc(acc_free, 1)
                evac.per, evac.last = {}, None
                return evac

            pend = None
            for n, (t0, tiles) in enumerate(GROUPS):
                pend = gemm(tiles // 2, up_evac(t0), pending=pend, keep=True)
                pend = gemm(4, idle() if n == 0 else adder(), pending=pend, ku=tiles // 4, keep=True)
            pend()

            variance(N2[2])
            add_norm(Y, "post_ffn_g", N2[3])
            dve.wait_ge(x_ready, 8)

            def shift_diff(i):
                x4 = X[:, ds(4 * i, 4), :]
                dve.tensor_tensor(XX3[:, :, 1:T], x4[:, :, 0:T - 1], x4[:, :, 1:T], ALU.subtract)
                link(dve.tensor_scalar(XX3[:, :, 0:1], x4[:, :, 0:1], -1.0, None, ALU.mult))

            def mixed_part(s_, hi, lo):
                g = COL["a_mu_proj_2"] + s_ * KD

                def side(i):
                    shift_diff(i)
                    for k in range(4):
                        ins = dve.scalar_tensor_tensor(HT3[:, k:k + 1, :], XX3[:, k:k + 1, :], PV[:, ds(4 * i + (g + k), 1)],
                                                       X[:, ds(4 * i + k, 1), :], ALU.mult, ALU.add)
                    ins.then_inc(normed, 1)
                    dve.wait_ge(nh_made, seen(nh_made))
                    dve.tensor_tensor(lo[:, ds(4 * i, 4), :], HT3[:, :, :], hi[:, ds(4 * i, 4), :].bitcast(F32), ALU.subtract)\
                       .then_inc(operand, 1)
                    dve.wait_ge(operand, seen(operand))
                return side

            def lora_part():
                g = COL["a_mu_lora_2"]

                def side(i):
                    shift_diff(i)
                    for w, dst in enumerate((KAP, BET)):
                        for k in range(4):
                            ins = dve.scalar_tensor_tensor(dst[:, ds(4 * i + k, 1), :], XX3[:, k:k + 1, :],
                                                           PV[:, ds(4 * i + (g + w * KD + k), 1)],
                                                           X[:, ds(4 * i + k, 1), :], ALU.mult, ALU.add)
                    ins.then_inc(xw_ready, 1)
                    dve.wait_ge(xw_ready, seen(xw_ready))
                return side

            def beside(side, per):
                def evac(i, j0):
                    if j0 == 0:
                        if isinstance(i, int):
                            dve.wait_ge(unit_done, seen(unit_done, 0, "tile") - 4)
                        side(i)
                evac.per, evac.last = per, None
                return evac

            first_part = mixed_part(3, A3H, A3L)
            for i in range(4):
                first_part(i)
            pend = None
            for n in range(4):
                if n < 3:
                    ev = beside(mixed_part(STREAMS[n + 1][0], STREAMS[n + 1][1], STREAMS[n + 1][2]), {dstep: 1, nh_made: 1, operand: 1})
                else:
                    ev = beside(lora_part(), {dstep: 1, xw_ready: 1})
                pend = gemm(4, ev, pending=pend, keep=True)
            pend()

            dve.wait_ge(acc_free, 4 + ALL_TILES)
            dve.wait_ge(kk_norm, 1)
            link(dve.tensor_scalar(tmp(20)[0:32, :], tmp(20)[0:32, :], 1e-12, None, ALU.max))
            dve.reciprocal(tmp(20)[0:32, :], tmp(20)[0:32, :]).then_inc(kk_inverse, 1)
            for f in range(KD):
                c = COL["a_k_k_2"] + f
                dve.wait_ge(kk_wide, f + 1)
                dve.scalar_tensor_tensor(BON[:, f, :], K[:, f, :], PV[:, c:c + 1], AUX[f % 2][:, 0:T], ALU.mult, ALU.mult).then_inc(kk_ready, 1)

            dve.wait_ge(kk_ready, KD)
            for s_ in range(KD + 3):
                if s_ < KD:
                    f, p = s_, s_ % 2
                    ka, rk = COL["a_k_a_2"] + f, COL["a_r_k_2"] + f
                    if f >= 2:
                        dve.wait_ge(tile_done, f - 1)
                    dve.wait_ge(sig_ready, 2 * f + 2)
                    dve.wait_ge(lora_in, 80)
                    dve.tensor_tensor_scan(tmp(12 + p), SCAN, KAP[:, f, :], 0.0, ALU.mult, ALU.add).then_inc(l_ready, 1)
                    link(dve.tensor_scalar(tmp(22 + p), BET[:, f, :], -1.0, PV[:, ka:ka + 1], ALU.add, ALU.mult))
                    link(dve.scalar_tensor_tensor(tmp(22 + p), tmp(22 + p), 1.0, K[:, f, :], ALU.add, ALU.mult))
                    dve.scalar_tensor_tensor(tmp(26 + p), R[:, f, :], PV[:, rk:rk + 1], tmp(22 + p), ALU.mult, ALU.mult).then_inc(rk_ready, 1)
                if 1 <= s_ < KD + 1:
                    f, p = s_ - 1, (s_ - 1) % 2
                    dve.wait_ge(decays, f + 1)
                    dve.wait_ge(b1_ready, f + 1)
                    link(dve.scalar_tensor_tensor(KAP[:, f, :], BON[:, f, :], -1.0, tmp(20 + p), ALU.mult, ALU.mult))
                    dve.tensor_tensor(BET[:, f, :], tmp(24 + p), tmp(18 + p), ALU.mult)
                    dve.tensor_tensor(K[:, f, :], tmp(22 + p), tmp(18 + p), ALU.mult)
                    dve.wait_ge(bonus_sum, f + 1)
                    dve.tensor_tensor(BON[:, f, :], AUX[2 + p][:, 0:T], V[:, f, :], ALU.mult).then_inc(tile_done, 1)
                if s_ >= 3:
                    f, p = s_ - 3, (s_ - 3) % 2
                    dve.wait_ge(lt_done, f + 1)
                    if f >= 2:
                        dve.wait_ge(lt_stored[p], 32 * (f // 2))
                    dve.tensor_tensor((XS, US)[p][:, :, :], ACC[p][:, 0:T].rearrange("p (c t) -> p c t", c=NCH),
                                      TRI_S.unsqueeze(1).broadcast_to([P, NCH, CHUNK]), ALU.mult).then_inc(lt_ready, 1)

            dve.wait_ge(inv_in, 32)
            dve.wait_ge(inv_init, 1)
            for s_ in range(H - 1):
                n, r = s_ + 1, H - 1 - s_
                o = OUTER[:, 0:2 * n * r].rearrange("p (b j t) -> p b j t", b=2, j=n)
                link(dve.tensor_tensor(o, LT[:, :, s_:s_ + 1, s_ + 1:].broadcast_to([P, 2, n, r]),
                                       TDIAG[:, :, 0:n, s_:s_ + 1].broadcast_to([P, 2, n, r]), ALU.mult))
                part = TDIAG[:, :, 0:n, s_ + 1:H]
                ins = dve.tensor_tensor(part, part, o, ALU.add)
                if s_ < H - 2:
                    link(ins)
            ins.then_inc(inverted, 1)

            wide = lambda x: x.rearrange("p i (h t) -> p i h t", h=2)

            def read_pairs(g, c, first=False):
                m = c % 2
                dve.wait_ge(prep_done, seen(prep_done))
                if not first:
                    dve.wait_ge(y_done, seen(y_done))
                k2 = ACC[0][:, :].rearrange("p (i x t) -> p i x t", i=4, x=2)
                b2 = ACC[1][:, :].rearrange("p (i x t) -> p i x t", i=4, x=2)
                tri_2 = TRI2.rearrange("p (o h t) -> p o h t", o=1, h=2).broadcast_to([P, 4, 2, CHUNK])
                quarter = QUARTER.rearrange("p (o h t) -> p o h t", o=1, h=2).broadcast_to([P, 4, 2, H])
                dve.tensor_tensor(wide(blocks(m, AKK)), diag(k2[:, :, 1, :]), tri_2, ALU.mult)
                dve.tensor_tensor(wide(cross(m))[:, :, :, H:], b2[:, :, 1:2, H:].broadcast_to([P, 4, 2, H]), quarter, ALU.mult)\
                    .then_inc(pairs_read, 1)

            def read_rest(g, c):
                m = c % 2
                tri_i = TRI_I.unsqueeze(1).broadcast_to([P, 4, CHUNK])
                for n, bank in ((ARK, ACC[0]), (ARB, ACC[1])):
                    a_ = dve.tensor_tensor(small(m, n), bank[:, :].rearrange("p (i x t) -> p i x t", i=4, x=2)[:, :, 0, :], tri_i, ALU.mult)
                a_.then_inc(rest_out, 1)

            def read_v(g, c, first=False):
                m = c % 2
                dve.wait_ge(vb_ready, seen(vb_ready))
                v2 = wide(blocks(m, VBD))
                dve.tensor_tensor(small(m, VC), v2[:, :, 0, :], v2[:, :, 1, :], ALU.add).then_inc(vc_ready, 1)

            def step(g, c, nxt):
                if nxt:
                    read_pairs(*nxt)
                dve.wait_ge(w_done, seen(w_done))
                dve.tensor_tensor(XS[:, :, :], AUX[0][:, 0:T].rearrange("p (i c) -> p i c", i=4), XS[:, :, :], ALU.add).then_inc(ws_ready, 1)
                if c > 0:
                    if not nxt:
                        dve.wait_ge(y_done, 4 * NCH)
                    dve.wait_ge(s_ready, seen(s_ready))
                    dve.tensor_tensor(wide(SBD[:, :, :]), diag(S[:, :, :]), MASK4, ALU.mult).then_inc(sbd_ready, 1)
                if nxt:
                    read_rest(*nxt)
                dve.wait_ge(us_ready, seen(us_ready, 2))
                dve.tensor_tensor(wide(UBD[:, :, :]), diag(US[:, :, :]), MASK4, ALU.mult).then_inc(ubd_ready, 1)
                if c > 0:
                    dve.wait_ge(sbd_ready, seen(sbd_ready))
                if c < 3:
                    dve.wait_ge(s_done, seen(s_done))
                    ps = AUX[3][:, 0:T].rearrange("p (i c) -> p i c", i=4)
                    if c > 0:
                        link(dve.tensor_tensor(S[:, :, :], ps, S[:, :, :], ALU.add))
                        ps = S[:, :, :]
                    dve.tensor_tensor(S[:, :, :], ps, GCE[:, ds(4 * g, 4), c:c + 1].broadcast_to([P, 4, CHUNK]), ALU.mult)\
                       .then_inc(s_ready, 1)
                if nxt:
                    read_v(*nxt)

            dve.wait_ge(t_stored, 16)
            read_pairs(0, 0, True)
            read_rest(0, 0)
            read_v(0, 0)
            with seen.loop(3, {prep_done: 4, y_done: 4, us_ready: 8, s_done: 3, dstep: 2, s_ready: 3, w_done: 4, vb_ready: 4, sbd_ready: 3}) as g:
                for c in range(NCH):
                    step(g, c, (g + (c + 1) // NCH, (c + 1) % NCH))
            for c in range(NCH):
                step(3, c, (3, c + 1) if c < 3 else None)

            dve.wait_ge(y_out, 1 + 4 * NCH)
            for f in range(KD):
                dve.wait_ge(gn_sum, f + 1)
                dve.scalar_tensor_tensor(BET[:, f, :], AUX[f % 2][:, 0:T], -1.0 / CHUNK, BET[:, f, :], ALU.mult, ALU.add)\
                    .then_inc(gn_centred, 1)
            dve.wait_ge(gn_sq_sum, KD)
            link(dve.tensor_scalar(RS4[:, 0, :], AUX[2][0:32, 0:T], 1.0 / CHUNK, GN_EPS, ALU.mult, ALU.add))
            dve.reciprocal(RS4[:, 0, :], RS4[:, 0, :]).then_inc(gn_var, 1)
            for s_ in range(KD + 2):
                if s_ >= 2:
                    f = s_ - 2
                    dve.wait_ge(gn_hi, f + 1)
                    dve.tensor_tensor(C4L[:, f, :], gnt(1, f), C4H[:, f, :].bitcast(F32), ALU.subtract).then_inc(gn_ready, 1)
                if s_ < KD:
                    f = s_
                    gg, gb = COL["a_gn_g_2"] + f, COL["a_gn_b_2"] + f
                    dve.wait_ge(gn_wide, f + 1)
                    if f >= 4:
                        dve.wait_ge(gn_ready, f - 3)
                    link(dve.scalar_tensor_tensor(gnt(1, f), BET[:, f, :], PV[:, gg:gg + 1], AUX[f % 2][:, 0:T], ALU.mult, ALU.mult))
                    dve.scalar_tensor_tensor(gnt(1, f), gnt(1, f), PV[:, gb:gb + 1], BON[:, f, :], ALU.add, ALU.add).then_inc(gn_out, 1)
            gemm(4, idle())

            def layer_norm(y, which, bufs, tiles, seen_operand):
                sq, mu, ms, rstd = bufs
                dve.wait_ge(acc_free, 4 + tiles)
                for q in range(4):
                    x4 = X[:, 4 * q:4 * q + 4, :]
                    dve.scalar_tensor_tensor(x4, x4, ALPHA, y[:, 4 * q:4 * q + 4, :], ALU.mult, ALU.add).then_inc(xr_ready, 1)
                dve.wait_ge(ln_sum, seen(ln_sum))
                wide = lambda v: v[:, :].unsqueeze(1).broadcast_to([P, 4, T])
                link(dve.tensor_scalar(mu[:, :], AUX[1][:, 0:T], 1.0 / D, None, ALU.mult))
                for q in range(4):
                    x4 = X[:, 4 * q:4 * q + 4, :]
                    dve.tensor_tensor(x4, x4, wide(mu), ALU.subtract).then_inc(xc_ready, 1)
                variance(ms, LN_EPS)
                dve.wait_ge(rstd_ready, seen(rstd_ready))
                for q in range(4):
                    x4 = X[:, 4 * q:4 * q + 4, :]
                    link(dve.tensor_tensor(x4, x4, wide(rstd), ALU.mult))
                    for k in range(4):
                        kt = 4 * q + k
                        g, b = COL["ln_g_2"] + which * KD + kt, COL["ln_b_2"] + which * KD + kt
                        ins = dve.tensor_scalar(X[:, kt, :], X[:, kt, :], PV[:, g:g + 1], PV[:, b:b + 1], ALU.mult, ALU.add)
                    ins.then_inc(xn_ready, 1)

            layer_norm(Y4, 0, L4, ALL_TILES + KD, True)

            for q in range(4):
                dve.wait_ge(nh_made, seen(nh_made))
                dve.tensor_tensor(A5L[:, 4 * q:4 * q + 4, :], X[:, 4 * q:4 * q + 4, :], A5H[:, 4 * q:4 * q + 4, :].bitcast(F32),
                                  ALU.subtract).then_inc(operand, 1)
            bl = COL["b_lambda_2"]
            dve.wait_ge(gn_ready, KD)
            for n in range(2):
                ins = dve.tensor_tensor(LAM[:, n:n + 1], PV[:, bl + 2 * n:bl + 2 * n + 1], PV[:, bl + 2 * n + 1:bl + 2 * n + 2], ALU.mult)
            ins.then_inc(lam_prod, 1)
            pend = None
            for n in range(4):
                pend = gemm(4, idle(), pending=pend, keep=True)
            pend()
            dve.wait_ge(lam_exp, 1)
            link(dve.tensor_tensor(LAM[:, 2:3], LAM[:, 3:4], LAM[:, 2:3], ALU.subtract))
            link(dve.tensor_scalar(LAM[:, 2:3], LAM[:, 2:3], -LAM_INIT, None, ALU.add))
            dve.wait_ge(dist_in, 16)
            for s_ in range(8 + 1):
                if s_ < 8:
                    n, p = s_, s_ % 2
                    dve.wait_ge(d_scored, n + 1)
                    if n >= 2:
                        dve.wait_ge(d_turned, n - 1)
                    for m in range(2):
                        ins = dve.scalar_tensor_tensor(SS5[:, p, 2 * m:2 * m + 2, :], DIST[:, :, :], -2.0 ** -(n + 1),
                                                       AUX[2 * p + m][:, :].rearrange("p (q t) -> p q t", q=2), ALU.mult, ALU.add)
                    link(ins)
                    link(dve.tensor_reduce(ST5[:, p, 0:4], SS5[:, p, :, :], AX.X, ALU.max))
                    dve.tensor_scalar(ST5[:, p, 0:4], ST5[:, p, 0:4], -1.0, None, ALU.mult).then_inc(d_max, 1)
                if s_ >= 1:
                    n, p = s_ - 1, (s_ - 1) % 2
                    dve.wait_ge(d_exp, n + 1)
                    link(dve.reciprocal(ST5[:, p, 4:8], ST5[:, p, 4:8]))
                    link(dve.tensor_scalar(ST5[:, p, 6:8], ST5[:, p, 6:8], LAM[:, 2:3], None, ALU.mult))
                    for q in range(2):
                        ins = dve.tensor_scalar(SS5[:, p, 2 + q, :], SS5[:, p, 2 + q, :], ST5[:, p, 6 + q:7 + q], None, ALU.mult)
                    link(ins)
                    for q in range(2):
                        ins = dve.scalar_tensor_tensor(SS5[:, p, q, :], SS5[:, p, q, :], ST5[:, p, 4 + q:5 + q], SS5[:, p, 2 + q, :],
                                                       ALU.mult, ALU.add)
                    ins.then_inc(d_probs, 1)
            sc = (1.0 - LAM_INIT) ** -2
            for s_ in range(8 + 3):
                if s_ < 8:
                    n, p = s_, s_ % 2
                    dve.wait_ge(o_sum, n + 1)
                    link(dve.tensor_scalar(SS5[:, p, 2, :], AUX[p][:, 0:T], sc / 256, SUBLN_EPS * sc, ALU.mult, ALU.add))
                    dve.reciprocal(SS5[:, p, 2, :], SS5[:, p, 2, :]).then_inc(o_var, 1)
                if 1 <= s_ < 9:
                    n, p = s_ - 1, (s_ - 1) % 2
                    dve.wait_ge(o_rstd, n + 1)
                    for d in range(2):
                        g = COL["b_subln_g_2"] + d
                        dve.scalar_tensor_tensor(Q5[:, 2 * n + d, :], Q5[:, 2 * n + d, :], PV[:, g:g + 1], SS5[:, p, 3, :],
                                                 ALU.mult, ALU.mult).then_inc(o_scaled, 1)
                if s_ >= 3:
                    n = s_ - 3
                    dve.wait_ge(o_hi, n + 1)
                    dve.tensor_tensor(C5L[:, 2 * n:2 * n + 2, :], Q5[:, 2 * n:2 * n + 2, :], C5H[:, 2 * n:2 * n + 2, :].bitcast(F32),
                                      ALU.subtract).then_inc(o_ready, 2)
            gemm(4, idle())
            layer_norm(Y5, 1, L5, ALL_TILES + 6 * KD, False)


def kernel(**inputs):
    import concourse.bacc as _bacc
    from concourse.bass_utils import run_bass_kernel_spmd as _run

    x = {k: np.ascontiguousarray(v) for k, v in inputs.items()}
    arrays = {n: x[n] for n in ("w_in", "pool_w", "w_o", "w_up", "w_down", "a_w_in_2", "a_w1_2", "a_w2_2", "a_a1_2",
                                "a_a2_2", "a_w_out_2", "w_k_shared_2", "w_v_shared_2", "b_w_qg_2", "b_w_out_2")}
    arrays["x_t"] = np.ascontiguousarray(x["x"][0].T)
    arrays["params"] = np.ascontiguousarray(np.concatenate([x[n].reshape(-1, P).T for n, _ in PARAMS], 1))
    arrays["consts"] = constants()
    distance = 255 - (np.arange(P)[:, None] + np.arange(384)[None])
    rows = x["rel_bias"][0][:, np.clip(distance, -P, P) + P]
    arrays["bias_rows"] = np.ascontiguousarray(rows.transpose(1, 0, 2))

    nc = _bacc.Bacc("TRN2", target_bir_lowering=False, num_devices=1)
    h = {n: nc.dram_tensor("in_" + n, a.shape, F32, kind="ExternalInput").ap() for n, a in arrays.items()}
    h["out"] = nc.dram_tensor("out_t", (D, T), F32, kind="ExternalOutput").ap()
    program(nc, h)
    r = _run(nc, [{"in_" + n: a for n, a in arrays.items()}], core_ids=[0])
    return np.ascontiguousarray(r.results[0]["out_t"].T)[None]
```

```python
import math
from contextlib import ExitStack

import numpy as np
import concourse.bass as bass
from concourse import mybir

F32 = mybir.dt.float32
F32R = mybir.dt.float32r
ALU = mybir.AluOpType
ACT = mybir.ActivationFunctionType
AX = mybir.AxisListType
ds = bass.ds

P = 128
T = 256
D = 2048
KD = D // P
FF = 5632
KF = FF // P
HALF = D // 2
HT = HALF // P
CHUNK = 64
NCH = T // CHUNK
POOL_WINDOWS = (2, 4, 8, 16)
NEG = -1e30
NORM_EPS = 1e-6
LN_EPS = 1e-5
GN_EPS = 64e-5
SUBLN_EPS = 1e-5
ALPHA = 4.0 ** 0.25
DECAY = -math.exp(-0.5)
LAM_INIT = 0.8 - 0.6 * math.exp(-0.3)
LORA = 96
HEAD_SCALE = 128.0 ** -0.5

PARAMS = [("pre_mix_g", KD), ("post_mix_g", KD), ("pre_ffn_g", KD), ("post_ffn_g", KD),
          ("pool_scale", HT), ("conv_w", 3 * 2 * KF), ("conv_b", 2 * KF),
          ("a_mu_proj_2", 4 * KD), ("a_mu_lora_2", 2 * KD), ("a_w0_2", KD), ("a_a0_2", KD),
          ("a_k_k_2", KD), ("a_k_a_2", KD), ("a_r_k_2", KD), ("a_gn_g_2", KD), ("a_gn_b_2", KD),
          ("ln_g_2", 2 * KD), ("ln_b_2", 2 * KD), ("b_subln_g_2", 2), ("b_lambda_2", 4)]
COL = {}
_n = 0
for _name, _cols in PARAMS:
    COL[_name] = _n
    _n += _cols
N_PARAM = _n

CONSTS = [("ident", P), ("ones", P), ("headones", P), ("stack", CHUNK), ("quarter", CHUNK), ("headsel", CHUNK), ("pairsel", CHUNK), ("flip", P),
          ("band", 2 * T), ("dist", 2 * T), ("invcount", 4 * T), ("scan", T), ("tri", 2 * 2 * CHUNK), ("expand", D)]
CCOL = {}
_n = 0
for _name, _cols in CONSTS:
    CCOL[_name] = _n
    _n += _cols
N_CONST = _n


def constants():
    c = np.zeros((P, N_CONST), np.float32)

    def put(name, a):
        c[:, CCOL[name]:CCOL[name] + a.shape[1]] = a

    p = np.arange(P)[:, None]
    t = np.arange(T)[None]
    put("ident", np.eye(P))
    put("ones", np.ones((P, P)))
    put("headones", (p // 64 == np.arange(P)[None] // 64))
    put("stack", (p % 64 == np.arange(64)[None]))
    put("quarter", (p // 64 == np.arange(64)[None] // 32) & (p % 64 < 32))
    put("headsel", (np.arange(64)[None] == 30 + p // 64))
    put("pairsel", np.repeat(np.arange(64)[None] // 2 == 15, P, 0))
    put("expand", (np.arange(D)[None] // 64 == p))
    put("flip", np.eye(P)[::-1])
    q = [p, p + P]
    seen = [(t // CHUNK) <= (x // CHUNK) for x in q]
    put("band", np.concatenate([np.where(s, 0.0, NEG) for s in seen], 1))
    put("dist", np.concatenate([np.where(s, np.abs(x - t), -100 * NEG) for s, x in zip(seen, q)], 1))
    put("invcount", np.concatenate([np.repeat(1.0 / np.minimum(t + 1, w), P, 0) for w in POOL_WINDOWS], 1))
    put("scan", np.repeat((t % CHUNK != 0), P, 0))
    h, s = p // 64, p % 64
    col = np.arange(2 * CHUNK)[None]
    same = (col // 64) == h
    tc = col[:, :64]
    put("tri", np.concatenate([same & (col % 64 > s), tc > s, tc >= s], 1))
    return c


KU = 4
UNIT_COLS = 256
RAW = 8
SPL = 4


class Counts:

    def __init__(self, eng):
        self.eng, self.n, self.reg = eng, {}, None

    def __call__(self, sem, k=1, what=""):
        key = (sem.name, what)
        self.n[key] = self.n.get(key, 0) + k
        if self.reg is None:
            return self.n[key]
        self.used.add(key)
        return self.n[key] + self.reg * self.per[key]

    def total(self, sem, what=""):
        return self.n[(sem.name, what)]

    def loop(self, iters, per):
        return _Loop(self, iters, {(s.name, "") if not isinstance(s, tuple) else (s[0].name, s[1]): k for s, k in per.items()})


class _Loop:
    def __init__(self, counts, iters, per):
        self.c, self.iters, self.per = counts, iters, per

    def __enter__(self):
        self.cm = self.c.eng.Fori(0, self.iters)
        i = self.cm.__enter__()
        self.c.reg, self.c.per, self.c.used = i, self.per, set()
        self.start = dict(self.c.n)
        return i

    def __exit__(self, *exc):
        if exc[0] is not None:
            return False
        c = self.c
        for key in c.used:
            did = c.n[key] - self.start.get(key, 0)
            assert did == self.per[key], (key, did, self.per[key])
            c.n[key] = self.start.get(key, 0) + self.per[key] * self.iters
        c.reg = None
        return self.cm.__exit__(*exc)


def program(nc, h):
    root = ExitStack()
    sems = {}

    def sem(name):
        sems[name] = root.enter_context(nc.semaphore(name))
        return sems[name]

    def sb(scope, name, shape, dt=F32):
        return scope.enter_context(nc.sbuf_tensor(name, shape, dt))

    def dram(name, shape):
        return nc.dram_tensor(name, shape, F32, kind="Internal").ap()

    with root:
        PV = sb(root, "params", [P, N_PARAM])
        NFIX = CCOL["flip"]
        CF = sb(root, "consts", [P, NFIX + 4 * CHUNK])
        IDENT, ONES, HEADONES = (CF[:, CCOL[n]:CCOL[n] + P] for n in ("ident", "ones", "headones"))
        TRI2 = CF[:, NFIX:NFIX + P]
        TRI_S = CF[:, NFIX + P:NFIX + P + CHUNK]
        TRI_I = CF[:, NFIX + P + CHUNK:]
        QUARTER = CF[:, CCOL["quarter"]:CCOL["quarter"] + CHUNK]
        HEADSEL = CF[:, CCOL["headsel"]:CCOL["headsel"] + CHUNK]
        PAIRSEL = CF[:, CCOL["pairsel"]:CCOL["pairsel"] + CHUNK]
        STACK = CF[:, CCOL["stack"]:CCOL["stack"] + CHUNK]
        RAWW = sb(root, "raw_w", [P, RAW, KU, UNIT_COLS])
        WHI = sb(root, "w_hi", [P, SPL, KU, UNIT_COLS], F32R)
        WLO = sb(root, "w_lo", [P, SPL, KU, UNIT_COLS], F32R)
        X = sb(root, "x", [P, KD, T])

        def norm_buffers(scope, tag, deep=2):
            return (sb(scope, "sq" + tag, [P, deep, 4, T]), sb(scope, "ht" + tag, [P, 2, 4, T]),
                    sb(scope, "ms" + tag, [P, T]), sb(scope, "rstd" + tag, [P, T]))

        with ExitStack() as s1:
            B1H, B1L = (sb(s1, n, [P, KD, T], F32R) for n in ("mix_hi", "mix_lo"))
            Z = sb(s1, "z", [P, 2 * KD, T])
            with ExitStack() as s2:
                A1H, A1L = (sb(s2, n, [P, KD, T], F32R) for n in ("h1_hi", "h1_lo"))
                HT1 = sb(s2, "ht_1", [P, 2, 4, T])
                sb(s2, "place_of_bias", [P, 11 * T])
                MS1, RSTD1 = sb(s2, "ms_1", [P, T]), sb(s2, "rstd_1", [P, T])
                SQ1 = Z[:, KD:2 * KD, :]
            with ExitStack() as s2:
                VTOK = sb(s2, "v_tok", [P, 8, 2, P])
                POOLW = sb(s2, "pool_w", [P, 4, 2, 2 * P])
                PA = sb(s2, "pool_a", [P, HT, T])
                PB = sb(s2, "pool_b", [P, HT, T])
                HANK = sb(s2, "bias_hankel", [P, 8, 384])
                FLIP = sb(s2, "flip", [P, P])
                BAND = sb(s2, "band", [P, 2, T])
                INVC = sb(s2, "invcount", [P, 4, T])
                SS = sb(s2, "scores", [P, 2, 2, T])
                PT = sb(s2, "probs_t", [P, 2, 384])
                ST = sb(s2, "softmax_stats", [P, 2, 4])
        with ExitStack() as s1:
            B2H, B2L = (sb(s1, n, [P, KD, T], F32R) for n in ("ff_hi", "ff_lo"))
            Y = sb(s1, "y", [P, KD, T])
            A2H, A2L = (sb(s1, n, [P, KD, T], F32R) for n in ("h2_hi", "h2_lo"))
            N2 = norm_buffers(s1, "_2", deep=4)
            SQY = N2[0][:, :, :, :].rearrange("p a b t -> p (a b) t")
            CV = sb(s1, "conv", [P, 4, T])
            GE = sb(s1, "gate", [P, 2, T])
            HG = sb(s1, "gated", [P, 2, T])

        with ExitStack() as s1:
            K, V = (sb(s1, n, [P, KD, T]) for n in ("k", "v"))
            with ExitStack() as s2:
                RK = sb(s2, "r_kappa", [P, 2, KD, T])
                R, KAP = RK[:, 0, :, :], RK[:, 1, :, :]
            with ExitStack() as s2:
                sb(s2, "place_of_r", [P, KD, T])
                A3H, A3L, B3H, B3L = (sb(s2, n, [P, KD, T], F32R) for n in ("xs_a_hi", "xs_a_lo", "xs_b_hi", "xs_b_lo"))
                XX3 = sb(s2, "shift_diff", [P, 4, T])
                HT3 = sb(s2, "xs_quarter", [P, 4, T])
            with ExitStack() as s2:
                sb(s2, "place_of_r_a", [P, 3, KD, T])
                HT3B = sb(s2, "xs_quarter_b", [P, 4, T])
            with ExitStack() as s2:
                sb(s2, "place_of_r_kappa", [P, 2, KD, T])
                BET, BON = (sb(s2, n, [P, KD, T]) for n in ("beta", "bonus"))
                with ExitStack() as s3:
                    W2S = sb(s3, "lora_2", [LORA, 2, D])
                    LOW = sb(s3, "lora_low", [LORA, 2, T])
                with ExitStack() as s3:
                    FMB = sb(s3, "beta_k_v_blocks", [P, 2, 3, 4, P])
                    XS, US, S = (sb(s3, n, [P, 4, CHUNK]) for n in ("wkv_x", "wkv_u", "wkv_s"))
                    SBD, UBD = (sb(s3, n, [P, 4, P]) for n in ("wkv_s_blocks", "wkv_u_blocks"))
                    OUTER = sb(s3, "outer", [P, 1024])
                    GCE = sb(s3, "chunk_decay", [P, KD, NCH])
                with ExitStack() as s3:
                    GNT = sb(s3, "group_norm_temps", [P, 2, 4, T])
                    EXP4 = sb(s3, "head_expand", [32, D])
                    RS4 = sb(s3, "head_rstd", [32, 2, T])
        with ExitStack() as s1:
            C4H, C4L = (sb(s1, n, [P, KD, T], F32R) for n in ("wkv_hi", "wkv_lo"))
            G4 = sb(s1, "silu_g", [P, KD, T])
            sb(s1, "place_of_kappa", [P, KD, T])
            L4 = (sb(s1, "ln_sq_4", [P, 2, 4, T]), sb(s1, "ln_mean_4", [P, T]), sb(s1, "ln_var_4", [P, T]), sb(s1, "ln_rstd_4", [P, T]))
        with ExitStack() as s1:
            A5H, A5L = (sb(s1, n, [P, KD, T], F32R) for n in ("x_hi", "x_lo"))
            KS5, VS5, Q5, G5 = (sb(s1, n, [P, KD, T]) for n in ("k_shared", "v_shared", "q_diff", "silu_g_diff"))
            DIST = sb(s1, "distance", [P, 2, T])
            SS5 = sb(s1, "diff_scores", [P, 2, 4, T])
            PT5 = sb(s1, "diff_probs_t", [P, 2, 384])
            ST5 = sb(s1, "diff_stats", [P, 2, 8])
            LAM = sb(s1, "lambda", [P, 4])
            OSQ = sb(s1, "o_squares", [P, 2, 2, T])
            EXP5 = sb(s1, "row_expand", [32, D // 2])
            RS5 = sb(s1, "o_rstd_rows", [32, 2, T])
        with ExitStack() as s1:
            VT5 = sb(s1, "v_shared_tok", [P, 2, KD, P])
            sb(s1, "place_of_operand_lo", [P, KD, T])
            C5H, C5L = (sb(s1, n, [P, KD, T], F32R) for n in ("o_hi", "o_lo"))
            sb(s1, "place_of_o", [P, KD, T])
            L5 = (sb(s1, "ln_sq_5", [P, 2, 4, T]), sb(s1, "ln_mean_5", [P, T]), sb(s1, "ln_var_5", [P, T]), sb(s1, "ln_rstd_5", [P, T]))

        def tmp(n):
            return RAWW[:, n // 4, n % 4, :]

        ACC = [root.enter_context(nc.psum_tensor(f"acc{i}", [P, 512], F32)) for i in range(4)]
        AUX = [root.enter_context(nc.psum_tensor(f"aux{i}", [P, 512], F32)) for i in range(4)]

        loaded, const_in = sem("params_loaded"), sem("consts_loaded")
        x_in = [sem(f"x_loaded{q}") for q in range(4)]
        side = sem("side_loaded")
        pool_w_in, pool_mix_ready = sem("pool_w_loaded"), sem("pool_mix_ready")
        landed = [sem(f"raw_landed{i}") for i in range(RAW)]
        hi_made = sem("hi_made")
        lo_made = sem("lo_made")
        unit_done = sem("unit_done")
        acc_free = sem("acc_free")
        sq_ready, sq_free = sem("sq_ready"), sem("sq_free")
        y_sum = sem("y_squares_summed")
        var_ready, rstd_ready = sem("var_ready"), sem("rstd_ready")
        normed = sem("normed")
        nh_made = sem("operand_hi_made")
        operand = sem("operand_ready")
        dstep, gstep = sem("dve_step"), sem("pool_step")
        v_turned, v_tok = sem("v_turned"), sem("v_tok")
        scored, sc_free = sem("scored"), sem("score_bank_free")
        maxed, expd, probs = sem("maxed"), sem("exp_done"), sem("probs_ready")
        turned, pt_ready = sem("probs_turned"), sem("probs_t_ready")
        pv_done, pv_hi = sem("pv_done"), sem("pv_hi")
        mixed, mixed_hi = sem("pool_mixed"), sem("pool_mixed_hi")
        mix_ready = sem("mix_ready")
        pooled = sem("pooled")
        conv_base, gelu_done = sem("conv_base"), sem("gelu_done")
        gated, gated_hi, gated_ready = sem("gated"), sem("gated_hi"), sem("gated_ready")
        x_ready = sem("x_ready")
        stored = sem("stored")
        g_stored, lora_in, xw_ready = sem("silu_g_stored"), sem("lora_loaded"), sem("xw_quarters")
        low_done, low_ready = sem("lora_low_done"), sem("lora_low_ready")
        lora_done, sig_ready = sem("lora_done"), sem("sigmoids_ready")
        kk_summed, kk_sq, kk_inverse = sem("kk_summed"), sem("kk_squares"), sem("kk_inverse")
        kk_norm, kk_ready, kk_wide = sem("kk_norm"), sem("kk_ready"), sem("kk_wide")
        exp_in, exp4_in = sem("expand_loaded"), sem("expand_loaded_again")
        l_ready, ones_ready, decays = sem("log_decay"), sem("decay_ones"), sem("decays_ready")
        rk_ready, bonus_sum, b1_ready = sem("rk_product"), sem("bonus_sum"), sem("kk_a_ready")
        tile_done, pool_done = sem("tile_prepared"), sem("rho_ready")
        blk_ready, lt_done, lt_ready = sem("beta_blocks"), sem("lt_done"), sem("lt_ready")
        lt_stored = [sem("lt_stored_even"), sem("lt_stored_odd")]
        inv_in, inv_init = sem("lt_loaded"), sem("inverse_started")
        inverted, t_stored = sem("inverted"), sem("inverse_stored")
        fm_ready, kap_ready, prep_done, tok_done = sem("blocks_ready"), sem("kappa_blocks"), sem("pairs_done"), sem("tok_turned")
        pairs_read, rest_out, tok_out = sem("pairs_read"), sem("output_pairs_read"), sem("tok_ready")
        t_loaded = [sem("t_loaded_even"), sem("t_loaded_odd")]
        t_zero, cross_zero = sem("t_zeroed"), sem("cross_zeroed")
        vb_ready = sem("v_tok_blocks")
        v_done, vc_ready, w_done, ws_ready = sem("v_tok_turned"), sem("v_tok_ready"), sem("wkv_w_done"), sem("wkv_xw_ready")
        x_done, xs_ready, u_done, us_ready = sem("wkv_x_done"), sem("wkv_x_ready"), sem("wkv_u_done"), sem("wkv_u_ready")
        s_done, s_ready, sbd_ready, ubd_ready = sem("wkv_s_done"), sem("wkv_s_ready"), sem("s_blocks"), sem("u_blocks")
        y_done, y_out = sem("wkv_y_done"), sem("wkv_y_out")
        g_loaded = sem("silu_g_loaded")
        gn_sum, gn_centred, gn_sq = sem("gn_sum"), sem("gn_centred"), sem("gn_squares")
        gn_sq_sum, gn_var, gn_rstd = sem("gn_sq_sum"), sem("gn_var"), sem("gn_rstd")
        gn_wide = sem("gn_rstd_wide")
        gn_out, gn_gated, gn_hi, gn_ready = sem("gn_out"), sem("gn_gated"), sem("gn_hi"), sem("gn_ready")
        xm_ready = sem("ln_over_spread")
        ln_sum, xc_ready, xn_ready = sem("ln_sum"), sem("ln_centred"), sem("ln_scaled")
        dist_in, lam_prod, lam_sum, lam_exp = sem("dist_loaded"), sem("lam_products"), sem("lam_sum"), sem("lam_exp")
        v5_turned, v5_tok = sem("v_shared_turned"), sem("v_shared_tok")
        d_scored, d_max, d_exp, d_probs = sem("diff_scored"), sem("diff_maxed"), sem("diff_exp"), sem("diff_probs")
        d_turned, d_pt, d_pv, o_out = sem("diff_turned"), sem("diff_probs_t"), sem("diff_pv"), sem("diff_o")
        o_sum, o_var, o_rstd, o_wide = sem("o_sum"), sem("o_var"), sem("o_rstd"), sem("o_rstd_wide")
        o_scaled, o_gated, o_hi, o_ready = sem("o_scaled"), sem("o_gated"), sem("o_hi"), sem("o_ready")

        FIRST_TILES = 2 * KD + KD + 2 * KF + 3 * KD
        ALL_TILES = FIRST_TILES + 4 * KD

        def gnt(kind, f):
            return GNT[:, kind, f % 4, :]

        block = root.enter_context(nc.Block())
        w_in = h["w_in"][0]
        w_up, w_down = h["w_up"][0], h["w_down"][0]
        GROUPS = [(0, 16), (16, 16), (32, 12)]

        STREAMS = [(3, A3H, A3L, V), (0, B3H, B3L, R), (1, A3H, A3L, K), (2, B3H, B3L, V)]
        W1S = RAWW[:, 0:3, :, :].rearrange("p a b c -> p (a b c)").rearrange("p (w k n) -> p w k n", w=2, k=KD)
        SCAN = tmp(30)
        FLAT = RAWW[:, :, :, :].rearrange("p a b c -> p (a b c)")
        EXP3 = FLAT[0:32, 22 * T:30 * T]
        H = CHUNK // 2
        def decay(f):
            return FLAT[:, (16 + 2 * (f % 2)) * T:][:, 0:NCH * (CHUNK + 1)].rearrange("p (c t) -> p c t", c=NCH)

        def by_chunk(x):
            return x.rearrange("p (c t) -> p c t", c=NCH)
        lt_dram, t_dram, g_dram = dram("lt_scratch", (P, CHUNK, CHUNK)), dram("t_scratch", (P, 2, H, H)), dram("g_scratch", (P, KD, T))
        LT = RAWW[:, 1:3, :, :].rearrange("p a b c -> p (a b c)").rearrange("p (b s t) -> p b s t", b=2, t=H)
        TT = RAWW[:, 5:7, :, :].rearrange("p a b c -> p (a b c)").rearrange("p (b s t) -> p b s t", b=2, t=H)

        def blocks(m, kind):
            return RAWW[:, 4 * m + kind // 2, 2 * (kind % 2):2 * (kind % 2) + 2, :].rearrange("p a c -> p (a c)")\
                .rearrange("p (i c) -> p i c", i=4)
        KBD, TBD, AKK, BT, KT, VBD = 0, 1, 2, 3, 4, 5

        def small(m, n):
            return RAWW[:, 4 * m + 3, n, :].rearrange("p (i c) -> p i c", i=4)
        ARK, ARB, VC = 0, 1, 2

        def cross(m):
            return OUTER[:, m * 512:(m + 1) * 512].rearrange("p (i c) -> p i c", i=4)

        def diag(x):
            return x.unsqueeze(2).broadcast_to([P, 4, 2, CHUNK])
        MASK4 = HEADONES.rearrange("p (o h t) -> p o h t", o=1, h=2).broadcast_to([P, 4, 2, CHUNK])

        @block.sync
        def _(sp):
            seen = Counts(sp)

            def weights(iters, at, ku=KU, kt0=0, k0=0):
                with seen.loop(iters, {lo_made: RAW}) as i:
                    for b in range(2):
                        w, col = at(i, b)
                        wk = w.rearrange("(k p) n -> p k n", p=P)
                        for q in range(4):
                            u = 4 * b + q
                            sp.wait_ge(lo_made, seen(lo_made))
                            sp.dma_start(RAWW[:, u, 0:ku, :],
                                         wk[:, kt0 + q * ku:kt0 + (q + 1) * ku, ds(col, UNIT_COLS)])\
                              .then_inc(landed[u], 16)

            sp.dma_start(PV[:, :], h["params"]).then_inc(loaded, 16)
            for q in range(4):
                sp.dma_start(X[:, 4 * q:4 * q + 4, :], h["x_t"][4 * q * P:4 * (q + 1) * P].rearrange("(k p) t -> p k t", p=P))\
                  .then_inc(x_in[q], 16)
            weights(8, lambda i, b: (w_in, i * 512 + b * 256))
            weights(4, lambda i, b: (h["w_o"][0], i * 512 + b * 256))
            for t0, tiles in GROUPS:
                weights(tiles // 2, lambda i, b: (w_up, i * 256 + (t0 * P + b * FF)))
                weights(4, lambda i, b: (w_down, i * 512 + b * 256), ku=tiles // 4, kt0=t0)
            for s_, *_ in STREAMS:
                weights(4, lambda i, b: (h["a_w_in_2"][0, s_], i * 512 + b * 256))
            sp.wait_ge(lo_made, seen.total(lo_made) + RAW)
            for w, n in enumerate(("a_w1_2", "a_a1_2")):
                sp.dma_start(W1S[:, w, :, :], h[n][0].rearrange("(k p) n -> p k n", p=P)).then_inc(lora_in, 16)
            sp.dma_start(EXP3, h["consts"][0:32, CCOL["expand"]:CCOL["expand"] + D]).then_inc(exp_in, 16)
            sp.dma_start(SCAN, h["consts"][:, CCOL["scan"]:CCOL["scan"] + T]).then_inc(lora_in, 16)
            sp.wait_ge(acc_free, 4 + ALL_TILES)
            for w, n in enumerate(("a_w2_2", "a_a2_2")):
                sp.dma_start(W2S[:, w, :], h[n][0]).then_inc(lora_in, 16)
            def load_lt(f):
                sp.wait_ge(lt_stored[f % 2], 32 * (f // 2 + 1))
                for b in range(2):
                    sp.dma_start(LT[8 * f:8 * f + 8, b, :, :], lt_dram[8 * f:8 * f + 8, b * H:(b + 1) * H, b * H:(b + 1) * H])\
                      .then_inc(inv_in, 16)

            def load_t(g, c):
                m = c % 2
                src = t_dram.rearrange("(f c h) b s t -> c h b s f t", c=NCH, h=2)
                for hh in range(2):
                    for b in range(2):
                        at = 64 * hh + H * b
                        sp.dma_start(blocks(m, TBD)[at:at + H, :, at:at + H], src[c, hh, b, :, ds(4 * g, 4), :])\
                          .then_inc(t_loaded[m], 16)

            for f in range(KD):
                sp.wait_ge(lt_ready, f + 1)
                for hh in range(2):
                    dst = lt_dram[8 * f:8 * f + 8].rearrange("(c h) s t -> h s c t", h=2)[hh]
                    sp.dma_start(dst, (XS, US)[f % 2][64 * hh:64 * hh + 64, :, :]).then_inc(lt_stored[f % 2], 16)
                if f >= 1:
                    load_lt(f - 1)
            load_lt(KD - 1)
            sp.wait_ge(inverted, 1)
            sp.dma_start(t_dram, TT).then_inc(t_stored, 16)
            sp.wait_ge(t_zero, 1)
            sp.wait_ge(t_stored, 16)
            load_t(0, 0)
            load_t(0, 1)

            seen(y_done, 1)
            with seen.loop(3, {y_done: 4}) as g:
                for c in range(NCH):
                    sp.wait_ge(y_done, seen(y_done))
                    load_t(g + (c + 2) // NCH, (c + 2) % NCH)
            for c in range(2):
                sp.wait_ge(y_done, seen(y_done))
                load_t(3, c + 2)

            sp.wait_ge(y_done, 1 + 4 * NCH)
            sp.wait_ge(y_out, 1 + 4 * NCH)
            sp.dma_start(EXP4[:, :], h["consts"][0:32, CCOL["expand"]:CCOL["expand"] + D]).then_inc(exp4_in, 16)
            sp.dma_start(G4[:, :, :], g_dram).then_inc(g_loaded, 16)
            weights(4, lambda i, b: (h["a_w_out_2"][0], i * 512 + b * 256))
            for w in (h["w_k_shared_2"], h["w_v_shared_2"]):
                weights(4, lambda i, b: (w, i * 512 + b * 256))
            weights(8, lambda i, b: (h["b_w_qg_2"][0], i * 512 + b * 256))
            weights(4, lambda i, b: (h["b_w_out_2"][0], i * 512 + b * 256))
            out = h["out"].rearrange("(k p) t -> p k t", p=P)
            for q in range(4):
                sp.wait_ge(xn_ready, 4 + q + 1)
                sp.dma_start(out[:, 4 * q:4 * q + 4, :], X[:, 4 * q:4 * q + 4, :]).then_inc(stored, 16)
            sp.wait_ge(stored, 64)

        @block.gpsimd
        def _(pool):
            seen = Counts(pool)
            pool.dma_start(CF[:, 0:NFIX], h["consts"][:, 0:NFIX]).then_inc(const_in, 16)
            pool.dma_start(CF[:, NFIX:], h["consts"][:, CCOL["tri"]:CCOL["expand"]]).then_inc(const_in, 16)
            pool.sem_inc(lo_made, RAW)
            pool.sem_inc(unit_done, SPL)
            pool.sem_inc(acc_free, 4)
            pool.sem_inc(sq_free, 2)
            pool.sem_inc(sc_free, 2)
            pool.sem_inc(y_done, 1)
            pool.sem_inc(y_out, 1)

            pool.wait_ge(operand, 4)
            band0 = CCOL["band"]
            for dst, src in ((HANK[:, :, :], h["bias_rows"]),
                             (FLIP[:, :], h["consts"][:, CCOL["flip"]:CCOL["flip"] + P]),
                             (BAND[:, :, :], h["consts"][:, band0:band0 + 2 * T].rearrange("p (q t) -> p q t", q=2)),
                             (INVC[:, :, :], h["consts"][:, CCOL["invcount"]:CCOL["invcount"] + 4 * T].rearrange("p (g t) -> p g t", g=4))):
                pool.dma_start(dst, src).then_inc(side, 16)
            pool.wait_ge(acc_free, 4 + 32)
            pool.dma_start(POOLW[:, :, :, :], h["pool_w"][0].rearrange("g (c p) d -> p g c d", p=P)).then_inc(pool_w_in, 16)

            def link(ins):
                ins.then_inc(gstep, 1)
                pool.wait_ge(gstep, seen(gstep))

            U = Z[:, 3 * HT:4 * HT, :]
            src, dst, first = U, PA, 0
            for n, w in enumerate(POOL_WINDOWS):
                r = w // 2
                link(pool.tensor_tensor(dst[:, first:, r:], src[:, first:, r:], src[:, first:, 0:T - r], ALU.add))
                link(pool.tensor_copy(dst[:, first:, 0:r], src[:, first:, 0:r]))
                src, dst, first = dst, (PB if dst is PA else PA), first + 2
            pool.wait_ge(side, 4 * 16)
            for g in range(4):
                W = (PA, PB)[g % 2][:, 2 * g:2 * g + 2, :]
                link(pool.tensor_tensor(W, W, INVC[:, g:g + 1, :].broadcast_to([P, 2, T]), ALU.mult))
                pool.tensor_tensor(W, W, U[:, 2 * g:2 * g + 2, :], ALU.subtract).then_inc(pooled, 1)

            pool.wait_ge(acc_free, 4 + FIRST_TILES + 16)
            pool.dma_start(g_dram, V[:, :, :]).then_inc(g_stored, 16)

            def widen(dst, src):
                return pool.tensor_tensor(dst.rearrange("p i (h t) -> p i h t", h=2), diag(src), MASK4, ALU.mult)

            pool.wait_ge(kk_summed, KD)
            for f in range(2):
                z = pool.memset(decay(f)[:, :, 0:1], 1.0)
            z.then_inc(ones_ready, 1)
            for s_ in range(KD + 2):
                if s_ < KD:
                    f, p = s_, s_ % 2
                    pool.wait_ge(l_ready, f + 1)
                    if f >= 2:
                        pool.wait_ge(tile_done, f - 1)
                    pool.tensor_tensor(tmp(24 + p), BON[:, f, :], BET[:, f, :], ALU.mult).then_inc(b1_ready, 1)
                if 1 <= s_ < KD + 1:
                    f, p = s_ - 1, (s_ - 1) % 2
                    pool.wait_ge(decays, f + 1)
                    pool.wait_ge(rk_ready, f + 1)
                    pool.tensor_copy(GCE[:, f, :], decay(f)[:, :, CHUNK])
                    pool.tensor_tensor(by_chunk(R[:, f, :]), by_chunk(R[:, f, :]), decay(f)[:, :, 1:], ALU.mult).then_inc(pool_done, 1)
                if s_ >= 2:
                    f, p = s_ - 2, s_ % 2
                    pool.wait_ge(tile_done, f + 1)
                    if f >= 2:
                        pool.wait_ge(lt_done, f - 1)
                    widen(FMB[:, p, 0, :, :], BET[:, f, :].rearrange("p (c t) -> p c t", c=NCH)).then_inc(blk_ready, 1)
            pool.wait_ge(tile_done, KD)
            pool.wait_ge(lt_done, KD)
            pool.wait_ge(pool_done, KD)
            link(pool.memset(TT[:, :, :, :], 0.0))
            pool.memset(TT.rearrange("p b s t -> p b (s t)")[:, :, 0:H * H:H + 1], 1.0).then_inc(inv_init, 1)

            for m in range(2):
                z = pool.memset(blocks(m, TBD), 0.0)
            z.then_inc(t_zero, 1)

            def widen_step(g, c, first=False):
                m = c % 2
                sl = lambda x: x[:, ds(4 * g, 4), c * CHUNK:(c + 1) * CHUNK]
                if not first:
                    pool.wait_ge(tok_done, seen(tok_done))
                for n, x in enumerate((BET, K, V)):
                    w = widen(FMB[:, m, n, :, :], sl(x))
                w.then_inc(fm_ready, 1)
                if not first:
                    pool.wait_ge(x_done, seen(x_done))
                widen(blocks(m, KBD), sl(KAP)).then_inc(kap_ready, 1)
            widen_step(0, 0, True)
            widen_step(0, 1, True)
            pool.wait_ge(inverted, 1)
            for m in range(2):
                z = pool.memset(cross(m), 0.0)
            z.then_inc(cross_zero, 1)
            with seen.loop(3, {tok_done: 4, x_done: 4}) as g:
                for c in range(NCH):
                    widen_step(g + (c + 2) // NCH, (c + 2) % NCH)
            for c in range(2):
                widen_step(3, c + 2)

            pool.wait_ge(g_loaded, 16)
            for f in range(KD):
                pool.wait_ge(gn_out, f + 1)
                pool.tensor_tensor(gnt(1, f), gnt(1, f), G4[:, f, :], ALU.mult).then_inc(gn_gated, 1)

            pool.wait_ge(gn_ready, KD)
            pool.dma_start(DIST[:, :, :], h["consts"][:, CCOL["dist"]:CCOL["dist"] + 2 * T].rearrange("p (q t) -> p q t", q=2))\
                .then_inc(dist_in, 16)
            pool.dma_start(EXP5[:, :], h["consts"][0:32, CCOL["expand"]:CCOL["expand"] + D // 2]).then_inc(dist_in, 16)
            for n in range(8):
                pool.wait_ge(o_out, n + 1)
                pool.tensor_tensor(Q5[:, 2 * n:2 * n + 2, :], Q5[:, 2 * n:2 * n + 2, :], G5[:, 2 * n:2 * n + 2, :], ALU.mult).then_inc(o_gated, 1)

        @block.tensor
        def _(pe):
            seen = Counts(pe)
            seen(lo_made, RAW)

            def gemm(iters, hi, lo, gates, ku=KU, side=None, side_per={}, between=None):
                def body(between=None):
                    for b in range(2):
                        if b == 1 and between is not None:
                            between()
                        for q in range(4):
                            if b == 0 and q < len(gates):
                                pe.wait_ge(*gates[q])
                            pe.wait_ge(lo_made, seen(lo_made))
                            for f in range(2):
                                if q == 0:
                                    pe.wait_ge(acc_free, seen(acc_free))
                                out = ACC[2 * b + f][:, 0:T]
                                for k in range(ku):
                                    kt = q * ku + k
                                    wh = WHI[:, q, k, f * P:(f + 1) * P]
                                    wl = WLO[:, q, k, f * P:(f + 1) * P]
                                    first, last = kt == 0, kt == 4 * ku - 1
                                    pe.matmul(out, wh, hi[:, kt, :], start=first, stop=False)
                                    pe.matmul(out, wh, lo[:, kt, :], start=False, stop=False)
                                    mm = pe.matmul(out, wl, hi[:, kt, :], start=False, stop=last)
                            mm.then_inc(unit_done, 1)
                if between is not None:
                    body(between)
                    iters -= 1
                if side is None:
                    with seen.loop(iters, {lo_made: 8, acc_free: 4}):
                        body()
                    return
                body()
                body()
                side(0)
                with seen.loop(iters - 2, {lo_made: 8, acc_free: 4, **side_per}) as j:
                    body()
                    side(j + 1)
                pe.wait_ge(acc_free, seen.total(acc_free) + 4)
                side(iters - 1)

            def sum_of(x, bank, ready=None, done=None):
                def side(i):
                    if ready is not None:
                        pe.wait_ge(ready, seen(ready, 2))
                    for k in range(4):
                        last = isinstance(i, int) and i == 3 and k == 3
                        mm = pe.matmul(bank[:, 0:T], ONES, x[:, ds(4 * i + k, 1), :], start=(isinstance(i, int) and i == 0 and k == 0), stop=last)
                    if last:
                        mm.then_inc(done, 1)
                return side

            def square_sum():
                for j in range(4):
                    pe.wait_ge(sq_ready, seen(sq_ready))
                    for k in range(4):
                        mm = pe.matmul(AUX[0][:, 0:T], ONES, SQB[0][:, j % 2, k, :],
                                       start=(j + k == 0), stop=(j + k == 6))
                    mm.then_inc(sq_free, 1)

            def quarters(sem_, per):
                base = seen(sem_, 4 * per) - 4 * per
                return [(sem_, base + per * (q + 1)) for q in range(4)]

            SQB = [None]

            def x_squares():
                pe.wait_ge(const_in, 32)
                pe.wait_ge(sq_ready, seen(sq_ready, 4))
                for k in range(KD):
                    mm = pe.matmul(AUX[0][:, 0:T], ONES, SQ1[:, k, :], start=(k == 0), stop=(k == KD - 1))
                mm.then_inc(y_sum, 1)
            gemm(8, A1H, A1L, quarters(operand, 1), between=x_squares)

            pe.wait_ge(acc_free, 4 + 32)
            for b in range(4):
                for j in range(4):
                    hd, kt = 2 * b + j // 2, j % 2
                    mm = pe.transpose(AUX[b][:, j * P:(j + 1) * P], Z[:, 2 * HT + hd, kt * P:(kt + 1) * P], IDENT)
                mm.then_inc(v_turned, 1)

            def scores(n):
                pe.wait_ge(sc_free, seen(sc_free))
                for q in range(2):
                    out = AUX[n % 2][:, q * T:(q + 1) * T]
                    pe.matmul(out, Z[:, n, q * P:(q + 1) * P], Z[:, HT + n, :], start=True, stop=False)
                    mm = pe.matmul(out, FLIP[:, :], HANK[:, n, (1 - q) * P:(1 - q) * P + T], start=False, stop=True)
                mm.then_inc(scored, 1)

            def turn(n):
                pe.wait_ge(probs, seen(probs))
                if n >= 1:
                    pe.wait_ge(pt_ready, seen(pt_ready))
                for j, (q, kt) in enumerate(((0, 0), (1, 0), (1, 1))):
                    mm = pe.transpose(AUX[2 + n % 2][:, j * P:(j + 1) * P], SS[:, n % 2, q, kt * P:(kt + 1) * P], IDENT)
                mm.then_inc(turned, 1)

            def pv(n):
                if n == 7:
                    pe.wait_ge(pt_ready, seen(pt_ready))
                if n >= 2:
                    pe.wait_ge(mix_ready, seen(mix_ready))
                out = ACC[n % 2]
                pe.matmul(out[:, 0:T], VTOK[:, n, 0, :], PT[:, n % 2, 0:T], start=True, stop=False)
                pe.matmul(out[:, P:T], VTOK[:, n, 1, :], PT[:, n % 2, T:384], start=False, stop=True).then_inc(pv_done, 1)

            def pool_mix(n):
                g, d = n // 2, n % 2
                if n == 0:
                    pe.wait_ge(pool_w_in, 16)
                pe.wait_ge(pooled, g + 1)
                if n >= 2:
                    pe.wait_ge(pool_mix_ready, n - 1)
                for c in range(2):
                    mm = pe.matmul(ACC[2 + n % 2][:, 0:T], POOLW[:, g, c, d * P:(d + 1) * P],
                                   (PA, PB)[g % 2][:, 2 * g + c, :], start=(c == 0), stop=(c == 1))
                mm.then_inc(mixed, 1)

            pe.wait_ge(side, 4 * 16)
            pe.wait_ge(v_tok, 4)
            scores(0)
            for s in range(8 + 2):
                if s < 7:
                    scores(s + 1)
                if 1 <= s < 9:
                    turn(s - 1)
                if s >= 2:
                    pv(s - 2)
                if 5 <= s < 9:
                    pool_mix(2 * (s - 5))
                    pool_mix(2 * (s - 5) + 1)
            gemm(4, B1H, B1L, [(mix_ready, 8), (mix_ready, 8), (pool_mix_ready, 4), (pool_mix_ready, 8)], side=sum_of(SQY, AUX[0], done=y_sum))
            seen(mix_ready, 2)

            SQB[0] = N2[0]
            square_sum()
            gates = quarters(operand, 1)
            for n, (t0, tiles) in enumerate(GROUPS):
                gemm(tiles // 2, A2H, A2L, gates)
                last = {"side": sum_of(SQY, AUX[0], ready=sq_ready, done=y_sum), "side_per": {sq_ready: 2}} if n == len(GROUPS) - 1 else {}
                gemm(4, B2H, B2L, quarters(gated_ready, tiles // 4), ku=tiles // 4, **last)

            for s_, ah, al, _ in STREAMS:
                gemm(4, ah, al, quarters(operand, 1))
            pe.wait_ge(acc_free, seen.total(acc_free) + 4)

            for f in range(KD):
                pe.wait_ge(kk_sq, f + 1)
                pe.matmul(AUX[2][0:32, 0:T], HEADSEL[:, 30 - 2 * f:62 - 2 * f], tmp(16 + f % 4), start=(f == 0), stop=(f == KD - 1))\
                    .then_inc(kk_summed, 1)

            pe.wait_ge(lora_in, 80)
            pe.wait_ge(xw_ready, 4)
            for w, x in enumerate((KAP, BET)):
                for k in range(KD):
                    mm = pe.matmul(AUX[w][0:LORA, 0:T], W1S[:, w, k, :], x[:, k, :], start=(k == 0), stop=(k == KD - 1))
                mm.then_inc(low_done, 1)
            pe.wait_ge(exp_in, 16)
            pe.wait_ge(kk_inverse, 1)
            pe.wait_ge(low_ready, 2)
            for f in range(KD):
                if f >= 2:
                    pe.wait_ge(kk_ready, f - 1)
                pe.matmul(AUX[f % 2][:, 0:T], EXP3[:, f * P:(f + 1) * P], tmp(20)[0:32, :], start=True, stop=True).then_inc(kk_wide, 1)
            for n in range(2 * KD):
                f, w = n // 2, n % 2
                if n < 2:
                    pe.wait_ge(low_ready, n + 1)
                if n >= 4:
                    pe.wait_ge(sig_ready, n - 3)
                pe.matmul(ACC[n % 4][:, 0:T], W2S[:, w, f * P:(f + 1) * P], LOW[:, w, :], start=True, stop=True).then_inc(lora_done, 1)
            for s_ in range(KD + 3):
                if s_ >= 3:
                    f = s_ - 3
                    pe.wait_ge(blk_ready, f + 1)
                    if f >= 2:
                        pe.wait_ge(lt_ready, f - 1)
                    for c in range(NCH):
                        mm = pe.matmul(ACC[f % 2][:, c * CHUNK:(c + 1) * CHUNK], FMB[:, f % 2, 0, c, :],
                                       KAP[:, f, c * CHUNK:(c + 1) * CHUNK], start=(c == 0), stop=(c == NCH - 1))
                    mm.then_inc(lt_done, 1)
                if s_ < KD:
                    f = s_
                    pe.wait_ge(rk_ready, f + 1)
                    if f >= 2:
                        pe.wait_ge(tile_done, f - 1)
                    pe.matmul(AUX[2 + f % 2][:, 0:T], HEADONES, tmp(26 + f % 2), start=True, stop=True).then_inc(bonus_sum, 1)

            def pairs(g, c, first=False):
                m = c % 2
                fm = FMB[:, m, :, :, :]
                pe.wait_ge(fm_ready, seen(fm_ready))
                if not first:
                    pe.wait_ge(rest_out, seen(rest_out))
                for i in range(4):
                    rho_kappa = RK[:, :, ds(4 * g + i, 1), c * CHUNK:(c + 1) * CHUNK]
                    pe.matmul(ACC[0][:, i * P:(i + 1) * P], fm[:, 1, i, :], rho_kappa, start=(i == 0), stop=(i == 3))
                    mm = pe.matmul(ACC[1][:, i * P:(i + 1) * P], fm[:, 0, i, :], rho_kappa, start=(i == 0), stop=(i == 3))
                mm.then_inc(prep_done, 1)

            def turns(g, c, first=False):
                m = c % 2
                if not first:
                    pe.wait_ge(tok_out, seen(tok_out))
                for n, bank in ((2, AUX[2]), (0, ACC[2]), (1, ACC[3])):
                    for i in range(4):
                        mm = pe.transpose(bank[:, i * P:(i + 1) * P], FMB[:, m, n, i, :], IDENT)
                    if n == 2:
                        mm.then_inc(v_done, 1)
                mm.then_inc(tok_done, 1)

            def four(bank, lhs, rhs, start, stop):
                for i in range(4):
                    mm = pe.matmul(bank[:, i * CHUNK:(i + 1) * CHUNK], lhs[:, i, :], rhs(i), start=(start and i == 0),
                                   stop=(stop and i == 3))
                return mm

            def step(g, c, nxt):
                m = c % 2
                of = lambda x: (lambda i: x[:, i, :])
                pe.wait_ge(pairs_read, seen(pairs_read))
                pe.wait_ge(vc_ready, seen(vc_ready))
                pe.wait_ge(kap_ready, seen(kap_ready))
                mm = four(AUX[0], blocks(m, AKK), of(small(m, VC)), True, c == 0)
                if c > 0:
                    pe.wait_ge(s_ready, seen(s_ready))
                    mm = four(AUX[0], blocks(m, KBD), of(S), False, True)
                mm.then_inc(x_done, 1)
                if nxt:
                    pairs(*nxt)
                pe.wait_ge(t_loaded[m], seen(t_loaded[m], 64))
                pe.wait_ge(xs_ready, seen(xs_ready))
                four(AUX[1], blocks(m, TBD), of(XS), True, True).then_inc(u_done, 1)
                pe.wait_ge(tok_out, seen(tok_out, 1, "step"))
                if c < 3:
                    four(AUX[3], blocks(m, KT), of(small(m, VC)), True, False)
                pe.wait_ge(us_ready, seen(us_ready))
                four(AUX[0], cross(m), of(US), True, True).then_inc(w_done, 1)
                if nxt:
                    turns(*nxt)
                pe.wait_ge(ws_ready, seen(ws_ready))
                four(AUX[1], blocks(m, TBD), of(XS), True, True).then_inc(u_done, 1)
                pe.wait_ge(us_ready, seen(us_ready))
                if c < 3:
                    four(AUX[3], blocks(m, BT), of(US), False, True).then_inc(s_done, 1)
                pe.wait_ge(rest_out, seen(rest_out, 1, "step"))
                y = AUX[1][:, T:]
                four(y, blocks(m, VBD), of(small(m, ARK)), True, False)
                if c > 0:
                    pe.wait_ge(sbd_ready, seen(sbd_ready))
                    four(y, SBD, lambda i: R[:, ds(4 * g + i, 1), c * CHUNK:(c + 1) * CHUNK], False, False)
                pe.wait_ge(ubd_ready, seen(ubd_ready))
                four(y, UBD, of(small(m, ARB)), False, True).then_inc(y_done, 1)

            pe.wait_ge(lt_ready, KD)
            pairs(0, 0, True)
            turns(0, 0, True)
            with seen.loop(3, {fm_ready: 4, rest_out: 4, (rest_out, "step"): 4, pairs_read: 4, tok_out: 4, (tok_out, "step"): 4,
                               kap_ready: 4, vc_ready: 4, s_ready: 3, xs_ready: 4, ws_ready: 4, t_loaded[0]: 128, t_loaded[1]: 128,
                               sbd_ready: 3, us_ready: 8, ubd_ready: 4}) as g:
                for c in range(NCH):
                    step(g, c, (g + (c + 1) // NCH, (c + 1) % NCH))
            for c in range(NCH):
                step(3, c, (3, c + 1) if c < 3 else None)

            pe.wait_ge(y_out, 1 + 4 * NCH)
            for s_ in range(KD + 2):
                if s_ < KD:
                    if s_ >= 2:
                        pe.wait_ge(gn_centred, s_ - 1)
                    pe.matmul(AUX[s_ % 2][:, 0:T], HEADONES, BET[:, s_, :], start=True, stop=True).then_inc(gn_sum, 1)
                if s_ >= 2:
                    f = s_ - 2
                    pe.wait_ge(gn_sq, f + 1)
                    pe.matmul(AUX[2][0:32, 0:T], HEADSEL[:, 30 - 2 * f:62 - 2 * f], gnt(0, f), start=(f == 0), stop=(f == KD - 1))\
                        .then_inc(gn_sq_sum, 1)
            pe.wait_ge(exp4_in, 16)
            pe.wait_ge(gn_rstd, 1)
            for f in range(KD):
                if f >= 2:
                    pe.wait_ge(gn_out, f - 1)
                pe.matmul(AUX[f % 2][:, 0:T], EXP4[:, f * P:(f + 1) * P], RS4[:, 1, :], start=True, stop=True).then_inc(gn_wide, 1)
            gemm(4, C4H, C4L, quarters(gn_ready, 4), side=sum_of(X, AUX[1], done=ln_sum))

            SQB[0] = L4[0]
            square_sum()

            gates = quarters(operand, 1)
            for n in range(4):
                gemm(4, A5H, A5L, gates)
            pe.wait_ge(acc_free, seen.total(acc_free) + 4)
            pe.wait_ge(lam_prod, 1)
            pe.matmul(AUX[0][:, 0:2], ONES, LAM[:, 0:2], start=True, stop=True).then_inc(lam_sum, 1)
            for n in range(8):
                if n >= 4:
                    pe.wait_ge(v5_tok, n - 3)
                for j in range(4):
                    mm = pe.transpose(ACC[n % 4][:, j * P:(j + 1) * P], VS5[:, 4 * (n % 4) + j, (n // 4) * P:(n // 4 + 1) * P], IDENT)
                mm.then_inc(v5_turned, 1)

            def scores(n):
                if n >= 2:
                    pe.wait_ge(d_max, n - 1)
                for m in range(2):
                    for q in range(2):
                        mm = pe.matmul(AUX[2 * (n % 2) + m][:, q * T:(q + 1) * T], Q5[:, 2 * n + m, q * P:(q + 1) * P],
                                       KS5[:, 2 * n + m, :], start=(q == 0), stop=(q == 1))
                mm.then_inc(d_scored, 1)

            def turn(n):
                pe.wait_ge(d_probs, n + 1)
                if n >= 1:
                    pe.wait_ge(d_pt, n)
                for j, (q, kt) in enumerate(((0, 0), (1, 0), (1, 1))):
                    mm = pe.transpose(ACC[2][:, j * P:(j + 1) * P], SS5[:, n % 2, q, kt * P:(kt + 1) * P], IDENT)
                mm.then_inc(d_turned, 1)

            def pv(n):
                pe.wait_ge(d_pt, n + 1)
                if n >= 2:
                    pe.wait_ge(o_out, n - 1)
                out = ACC[n % 2]
                for d in range(2):
                    pe.matmul(out[:, d * T:(d + 1) * T], VT5[:, 0, 2 * n + d, :], PT5[:, n % 2, 0:T], start=(d == 0), stop=False)
                    mm = pe.matmul(out[:, d * T + P:(d + 1) * T], VT5[:, 1, 2 * n + d, :], PT5[:, n % 2, T:384], start=False, stop=(d == 1))
                mm.then_inc(d_pv, 1)

            pe.wait_ge(v5_tok, 8)
            pe.wait_ge(lam_exp, 1)
            scores(0)
            for s_ in range(8 + 3):
                if s_ < 7:
                    scores(s_ + 1)
                if 1 <= s_ < 9:
                    turn(s_ - 1)
                if 2 <= s_ < 10:
                    pv(s_ - 2)
                if s_ >= 3:
                    n = s_ - 3
                    pe.wait_ge(o_out, n + 1)
                    for d in range(2):
                        mm = pe.matmul(ACC[3][0:32, 0:T], PAIRSEL[:, 30 - 2 * n:62 - 2 * n], OSQ[:, n % 2, d, :],
                                       start=(n + d == 0), stop=(n + d == 8))
                    mm.then_inc(o_sum, 1)
            pe.wait_ge(o_rstd, 1)
            for n in range(8):
                if n >= 2:
                    pe.wait_ge(o_scaled, n - 1)
                pe.matmul(AUX[n % 2][:, 0:T], EXP5[:, n * P:(n + 1) * P], RS5[:, 1, :], start=True, stop=True).then_inc(o_wide, 1)
            gemm(4, C5H, C5L, quarters(o_ready, 4), side=sum_of(X, AUX[1], done=ln_sum))
            SQB[0] = L5[0]
            square_sum()

        @block.scalar
        def _(act):
            seen = Counts(act)
            seen(unit_done, SPL, "tile")
            seen(acc_free, 4, "tile")

            def split(b, ku=KU):
                for q in range(4):
                    u = 4 * b + q
                    act.wait_ge(landed[u], seen(landed[u], 16))
                    act.wait_ge(unit_done, seen(unit_done))
                    act.activation(WHI[:, q, 0:ku, :], RAWW[:, u, 0:ku, :], ACT.Copy).then_inc(hi_made, 1)

            def gemm(iters, evac, pending=None, ku=KU, keep=False, ahead=False):

                def out(i, j0):
                    act.wait_ge(unit_done, seen(unit_done, 4, "tile"))
                    seen(acc_free, 2, "tile")
                    evac(i, j0)

                if not ahead:
                    split(0, ku)
                if pending is not None:
                    pending()
                split(1, ku)
                out(0, 0)
                with seen.loop(iters - 1, {**{s: 16 for s in landed}, unit_done: 8, (unit_done, "tile"): 8,
                                           (acc_free, "tile"): 4, **evac.per}) as j:
                    split(0, ku)
                    out(j, 2)
                    split(1, ku)
                    out(j + 1, 0)

                def rest():
                    out(iters - 1, 2)
                    if evac.last:
                        evac.last(iters)
                if keep:
                    return rest
                rest()

            def copier(dst, scale=1.0, tile0=0):
                def evac(i, j0):
                    for j in (j0, j0 + 1):
                        act.activation(dst[:, ds(4 * i + (tile0 + j), 1), :], ACC[j][:, 0:T].rearrange("p (o t) -> p o t", o=1), ACT.Copy, scale=scale)\
                           .then_inc(acc_free, 1)
                evac.per, evac.last = {}, None
                return evac

            def adder():
                def evac(i, j0):
                    pass
                evac.per, evac.last = {}, None
                return evac

            def squares(src, sq, ready=None):
                for j in range(4):
                    if ready is not None:
                        act.wait_ge(ready, seen(ready))
                    act.wait_ge(sq_free, seen(sq_free))
                    act.activation(sq[:, j % 2, :, :], src[:, 4 * j:4 * j + 4, :], ACT.Square).then_inc(sq_ready, 1)

            def rsqrt(ms, rstd):
                act.wait_ge(var_ready, seen(var_ready))
                act.activation(rstd[:, :], ms[:, :], ACT.Sqrt).then_inc(rstd_ready, 1)

            def operand_hi(ht, hi):
                for j in range(4):
                    act.wait_ge(normed, seen(normed))
                    act.activation(hi[:, 4 * j:4 * j + 4, :], ht[:, j % 2, :, :], ACT.Copy).then_inc(nh_made, 1)

            for j in range(4):
                act.wait_ge(normed, seen(normed))
                act.activation(A1H[:, 4 * j:4 * j + 4, :], HT1[:, j % 2, :, :], ACT.Copy).then_inc(nh_made, 1)
                if j == 1:
                    split(0)
            for j in range(4):
                act.activation(SQ1[:, 4 * j:4 * j + 4, :], X[:, 4 * j:4 * j + 4, :], ACT.Square).then_inc(sq_ready, 1)

            def spread():
                def evac(i, j0):
                    if isinstance(i, int) and i + j0 == 0:
                        rsqrt(MS1, RSTD1)
                evac.per, evac.last = {}, None
                return evac
            act.wait_ge(loaded, 16)
            pend = gemm(2, spread(), keep=True, ahead=True)
            pend = gemm(6, adder(), pending=pend, keep=True)
            split(0)
            pend()

            for b in range(4):
                act.wait_ge(v_turned, seen(v_turned))
                act.activation(VTOK[:, 2 * b:2 * b + 2, :, :], AUX[b][:, :].rearrange("p (a b c) -> p a b c", a=2, b=2), ACT.Copy).then_inc(v_tok, 1)

            def exps(n):
                act.wait_ge(maxed, seen(maxed))
                for q in range(2):
                    e = act.activation(SS[:, n % 2, q, :], SS[:, n % 2, q, :], ACT.Exp, bias=ST[:, n % 2, q:q + 1],
                                       accum_out=ST[:, n % 2, 2 + q:3 + q])
                e.then_inc(expd, 1)

            def turned_out(n):
                act.wait_ge(turned, seen(turned))
                if n >= 2:
                    act.wait_ge(pv_done, n - 1)
                act.activation(PT[:, n % 2, :], AUX[2 + n % 2][:, 0:384], ACT.Copy).then_inc(pt_ready, 1)

            def head_hi(n):
                act.wait_ge(pv_done, n + 1)
                act.activation(B1H[:, n, :], ACC[n % 2][:, 0:T], ACT.Copy).then_inc(pv_hi, 1)

            ps = COL["pool_scale"]
            for s in range(8 + 2):
                if 6 <= s < 10:
                    for n in (2 * (s - 6), 2 * (s - 6) + 1):
                        act.wait_ge(mixed, seen(mixed))
                        act.activation(B1H[:, HT + n, :], ACC[2 + n % 2][:, 0:T], ACT.Copy, scale=PV[:, ps + n:ps + n + 1])\
                           .then_inc(mixed_hi, 1)
                if s < 8:
                    exps(s)
                if 1 <= s < 9:
                    turned_out(s - 1)
                if s >= 2:
                    head_hi(s - 2)
            def copy_and_square(dst):
                def evac(i, j0):
                    for j in (j0, j0 + 1):
                        t = ACC[j][:, 0:T].rearrange("p (o t) -> p o t", o=1)
                        act.activation(dst[:, ds(4 * i + j, 1), :], t, ACT.Copy)
                        act.activation(SQY[:, ds(4 * i + j, 1), :], t, ACT.Square).then_inc(acc_free, 1)
                evac.per, evac.last = {}, None
                return evac

            pend = gemm(4, copy_and_square(Y), keep=True, ahead=True)
            split(0)
            pend()

            rsqrt(N2[2], N2[3])
            squares(X, N2[0], x_ready)
            rsqrt(N2[2], N2[3])
            operand_hi(N2[1], A2H)

            def up_evac(t0):
                cw, cb = COL["conv_w"], COL["conv_b"]

                def base(i, j):
                    col = 2 * i + (t0 + (j % 2) + KF * (j // 2))
                    act.activation(CV[:, j, :], ACC[j][:, 0:T], ACT.Identity,
                                   bias=PV[:, ds(col + cb, 1)], scale=PV[:, ds(col + (cw + 4 * KF), 1)]).then_inc(conv_base, 1)

                def split(i):
                    act.wait_ge(gated, seen(gated, 2))
                    act.activation(B2H[:, ds(2 * i, 2), :], HG[:, :, :], ACT.Copy).then_inc(gated_hi, 1)

                def evac(i, j0):
                    if j0 == 0:
                        if not isinstance(i, int):
                            split(i - 1)
                        base(i, 0)
                        base(i, 1)
                    else:
                        base(i, 2)
                        base(i, 3)
                        act.wait_ge(acc_free, seen(acc_free, 0, "tile") - 2)
                        for j in range(2):
                            act.activation(GE[:, j, :], CV[:, j, :], ACT.Gelu_apprx_tanh).then_inc(gelu_done, 1)
                evac.per = {gated: 2}
                evac.last = lambda iters: split(iters - 1)
                return evac

            def squarer():
                def evac(i, j0):
                    act.wait_ge(acc_free, seen(acc_free, 0, "tile"))
                    act.activation(SQY[:, ds(4 * i + j0, 2), :], Y[:, ds(4 * i + j0, 2), :], ACT.Square).then_inc(sq_ready, 1)
                evac.per, evac.last = {}, None
                return evac

            pend = None
            for n, (t0, tiles) in enumerate(GROUPS):
                pend = gemm(tiles // 2, up_evac(t0), pending=pend, keep=True, ahead=(n == 0))
                pend = gemm(4, (copier(Y), adder(), squarer())[n], pending=pend, ku=tiles // 4, keep=True)
            split(0)
            pend()

            rsqrt(N2[2], N2[3])

            def with_side(evac, side, per):
                def both(i, j0):
                    evac(i, j0)
                    if j0 == 0:
                        side(i)
                both.per, both.last = {**evac.per, **per}, evac.last
                return both

            def mixed_hi_part(hi):
                def side(i, ht=HT3):
                    act.wait_ge(normed, seen(normed))
                    act.activation(hi[:, ds(4 * i, 4), :], ht[:, :, :], ACT.Copy).then_inc(nh_made, 1)
                return side

            def silu_out(dst):
                def evac(i, j0):
                    for j in (j0, j0 + 1):
                        act.activation(dst[:, ds(4 * i + j, 1), :], ACC[j][:, 0:T].rearrange("p (o t) -> p o t", o=1), ACT.Silu)\
                           .then_inc(acc_free, 1)
                evac.per, evac.last = {}, None
                return evac

            first_part = mixed_hi_part(A3H)
            for i in range(4):
                first_part(i, (HT3, HT3B)[i % 2])
            pend = None
            for n, (s_, _, _, dst) in enumerate(STREAMS):
                ev = silu_out(dst) if n == 0 else copier(dst)
                if n < 3:
                    ev = with_side(ev, mixed_hi_part(STREAMS[n + 1][1]), {normed: 1})
                if n == 3:
                    pend()
                    pend = None
                    act.wait_ge(g_stored, 16)
                pend = gemm(4, ev, pending=pend, keep=True, ahead=(n == 0))
            pend()

            act.wait_ge(acc_free, 4 + ALL_TILES)
            for f in range(KD):
                if f >= 4:
                    act.wait_ge(kk_summed, f - 3)
                c = COL["a_k_k_2"] + f
                act.activation(tmp(16 + f % 4), K[:, f, :], ACT.Square, scale=PV[:, c:c + 1]).then_inc(kk_sq, 1)

            act.wait_ge(kk_summed, KD)
            act.activation(tmp(20)[0:32, :], AUX[2][0:32, 0:T], ACT.Sqrt).then_inc(kk_norm, 1)
            act.wait_ge(low_done, 1)
            act.activation(LOW[:, 0, :], AUX[0][0:LORA, 0:T], ACT.Tanh).then_inc(low_ready, 1)
            act.wait_ge(low_done, 2)
            act.activation(LOW[:, 1, :], AUX[1][0:LORA, 0:T], ACT.Copy).then_inc(low_ready, 1)
            for n in range(2 * KD):
                f, w = n // 2, n % 2
                act.wait_ge(lora_done, n + 1)
                b = COL[("a_w0_2", "a_a0_2")[w]] + f
                act.activation((KAP, BET)[w][:, f, :], ACC[n % 4][:, 0:T], ACT.Sigmoid, bias=PV[:, b:b + 1]).then_inc(sig_ready, 1)
            for f in range(KD):
                p = f % 2
                act.wait_ge(l_ready, f + 1)
                if f >= 2:
                    act.wait_ge(tile_done, f - 1)
                    act.wait_ge(pool_done, f - 1)
                act.activation(decay(f)[:, :, 1:], by_chunk(tmp(12 + p)), ACT.Exp, scale=DECAY)
                act.activation(tmp(20 + p), tmp(12 + p), ACT.Exp, scale=-DECAY).then_inc(decays, 1)

            def step(g, c, nxt):
                m = c % 2
                w4 = lambda bank: bank[:, 0:T].rearrange("p (i c) -> p i c", i=4)

                act.wait_ge(x_done, seen(x_done))
                act.activation(XS[:, :, :], w4(AUX[0]), ACT.Copy).then_inc(xs_ready, 1)
                act.wait_ge(tok_done, seen(tok_done))
                act.activation(blocks(m, BT), ACC[2][:, :].rearrange("p (i c) -> p i c", i=4), ACT.Copy)
                act.activation(blocks(m, KT), ACC[3][:, :].rearrange("p (i c) -> p i c", i=4), ACT.Copy).then_inc(tok_out, 1)
                act.wait_ge(u_done, seen(u_done))
                act.activation(US[:, :, :], w4(AUX[1]), ACT.Copy).then_inc(us_ready, 1)
                act.wait_ge(u_done, seen(u_done))
                act.activation(US[:, :, :], w4(AUX[1]), ACT.Copy).then_inc(us_ready, 1)
                if nxt:
                    v_copy(*nxt)
                act.wait_ge(y_done, seen(y_done))
                act.activation(BET[:, ds(4 * g, 4), c * CHUNK:(c + 1) * CHUNK], w4(AUX[1][:, T:]), ACT.Copy).then_inc(y_out, 1)

            def v_copy(g, c):
                act.wait_ge(v_done, seen(v_done))
                act.activation(blocks(c % 2, VBD), AUX[2][:, :].rearrange("p (i c) -> p i c", i=4), ACT.Copy).then_inc(vb_ready, 1)

            act.wait_ge(inverted, 1)
            seen(y_done, 1)
            v_copy(0, 0)
            with seen.loop(3, {tok_done: 4, x_done: 4, u_done: 8, y_done: 4, v_done: 4}) as g:
                for c in range(NCH):
                    step(g, c, (g + (c + 1) // NCH, (c + 1) % NCH))
            for c in range(NCH):
                step(3, c, (3, c + 1) if c < 3 else None)

            for f in range(KD):
                act.wait_ge(gn_centred, f + 1)
                if f >= 4:
                    act.wait_ge(gn_sq_sum, f - 3)
                act.activation(gnt(0, f), BET[:, f, :], ACT.Square).then_inc(gn_sq, 1)
            split(0)
            act.wait_ge(gn_var, 1)
            act.activation(RS4[:, 1, :], RS4[:, 0, :], ACT.Sqrt).then_inc(gn_rstd, 1)
            for f in range(KD):
                act.wait_ge(gn_gated, f + 1)
                act.activation(C4H[:, f, :], gnt(1, f), ACT.Copy).then_inc(gn_hi, 1)
            pend = gemm(4, adder(), keep=True, ahead=True)
            split(0)
            pend()

            def layer_norm_part(bufs):
                squares(X, bufs[0], xc_ready)
                rsqrt(bufs[2], bufs[3])

            def gain_and_bias(which, hi=None):
                for q in range(4):
                    act.wait_ge(xm_ready, 4 * which + q + 1)
                    for k in range(4):
                        kt = 4 * q + k
                        g, b = COL["ln_g_2"] + which * KD + kt, COL["ln_b_2"] + which * KD + kt
                        ins = act.activation(X[:, kt, :], X[:, kt, :], ACT.Identity, scale=PV[:, g:g + 1], bias=PV[:, b:b + 1])
                    ins.then_inc(xn_ready, 1)
                    if hi is not None:
                        act.wait_ge(xn_ready, q + 1)
                        act.activation(hi[:, 4 * q:4 * q + 4, :], X[:, 4 * q:4 * q + 4, :], ACT.Copy).then_inc(nh_made, 1)

            layer_norm_part(L4)

            gain_and_bias(0, A5H)
            pend = gemm(4, copier(KS5), keep=True, ahead=True)
            pend = gemm(4, copier(VS5), pending=pend, keep=True)
            pend = gemm(4, copier(Q5, HEAD_SCALE), pending=pend, keep=True)
            pend = gemm(4, silu_out(G5), pending=pend, keep=True)
            split(0)
            pend()
            act.wait_ge(lam_sum, 1)
            act.activation(LAM[:, 2:4], AUX[0][:, 0:2], ACT.Exp).then_inc(lam_exp, 1)
            for n in range(8):
                act.wait_ge(v5_turned, n + 1)
                act.activation(VT5[:, n // 4, 4 * (n % 4):4 * (n % 4) + 4, :], ACC[n % 4][:, :].rearrange("p (a b) -> p a b", a=4), ACT.Copy)\
                   .then_inc(v5_tok, 1)

            for s_ in range(8 + 2):
                if s_ < 8:
                    act.wait_ge(d_max, s_ + 1)
                    for m in range(4):
                        e = act.activation(SS5[:, s_ % 2, m, :], SS5[:, s_ % 2, m, :], ACT.Exp, bias=ST5[:, s_ % 2, m:m + 1],
                                           accum_out=ST5[:, s_ % 2, 4 + m:5 + m])
                    e.then_inc(d_exp, 1)
                if 1 <= s_ < 9:
                    n = s_ - 1
                    act.wait_ge(d_turned, n + 1)
                    if n >= 2:
                        act.wait_ge(d_pv, n - 1)
                    act.activation(PT5[:, n % 2, :], ACC[2][:, 0:384], ACT.Copy).then_inc(d_pt, 1)
                if s_ >= 2:
                    n = s_ - 2
                    act.wait_ge(d_pv, n + 1)
                    if n >= 2:
                        act.wait_ge(o_sum, n - 1)
                    g = COL["b_subln_g_2"]
                    for d in range(2):
                        act.activation(Q5[:, 2 * n + d, :], ACC[n % 2][:, d * T:(d + 1) * T], ACT.Copy, scale=PV[:, g + d:g + d + 1])
                    act.activation(OSQ[:, n % 2, :, :], ACC[n % 2][:, :].rearrange("p (d t) -> p d t", d=2), ACT.Square).then_inc(o_out, 1)
            act.wait_ge(o_var, 1)
            act.activation(RS5[:, 1, :], RS5[:, 0, :], ACT.Sqrt).then_inc(o_rstd, 1)
            for n in range(8):
                act.wait_ge(o_scaled, n + 1)
                act.activation(C5H[:, 2 * n:2 * n + 2, :], Q5[:, 2 * n:2 * n + 2, :], ACT.Copy).then_inc(o_hi, 1)
            gemm(4, adder(), ahead=True)
            layer_norm_part(L5)
            gain_and_bias(1)

        @block.vector
        def _(dve):
            seen = Counts(dve)
            seen(unit_done, SPL, "tile")
            seen(acc_free, 4, "tile")
            seen(sq_free, 2)

            def link(ins):
                ins.then_inc(dstep, 1)
                dve.wait_ge(dstep, seen(dstep))

            def split(b, ku=KU):
                for q in range(4):
                    u = 4 * b + q
                    dve.wait_ge(hi_made, seen(hi_made))
                    dve.tensor_tensor(WLO[:, q, 0:ku, :], RAWW[:, u, 0:ku, :],
                                      WHI[:, q, 0:ku, :].bitcast(F32), ALU.subtract)\
                       .then_inc(lo_made, 1)

            def gemm(iters, evac, pending=None, ku=KU, keep=False, ahead=False):

                def out(i, j0):
                    seen(unit_done, 4, "tile")
                    seen(acc_free, 2, "tile")
                    evac(i, j0)

                if not ahead:
                    split(0, ku)
                if pending is not None:
                    pending()
                split(1, ku)
                out(0, 0)
                with seen.loop(iters - 1, {hi_made: 8, (unit_done, "tile"): 8, (acc_free, "tile"): 4,
                                           **evac.per}) as j:
                    split(0, ku)
                    out(j, 2)
                    split(1, ku)
                    out(j + 1, 0)

                def rest():
                    out(iters - 1, 2)
                    if evac.last:
                        evac.last(iters)
                if keep:
                    return rest
                rest()

            def idle():
                def evac(i, j0):
                    pass
                evac.per, evac.last = {}, None
                return evac

            def variance(ms, eps=NORM_EPS, beside_gemm=False):
                if beside_gemm:
                    dve.wait_ge(y_sum, seen(y_sum))
                else:
                    dve.wait_ge(sq_free, seen(sq_free, 4))
                link(dve.tensor_scalar(ms[:, :], AUX[0][:, 0:T], 1.0 / D, eps, ALU.mult, ALU.add))
                dve.reciprocal(ms[:, :], ms[:, :]).then_inc(var_ready, 1)

            def apply_norm(src, gain, ht, rstd, hi, lo):
                def low(j):
                    dve.wait_ge(nh_made, seen(nh_made))
                    dve.tensor_tensor(lo[:, 4 * j:4 * j + 4, :], ht[:, j % 2, :, :],
                                      hi[:, 4 * j:4 * j + 4, :].bitcast(F32), ALU.subtract).then_inc(operand, 1)
                g = COL[gain]
                dve.wait_ge(rstd_ready, seen(rstd_ready))
                for j in range(4):
                    if j >= 2:
                        dve.wait_ge(operand, seen(operand))
                    for k in range(4):
                        kt = 4 * j + k
                        ins = dve.scalar_tensor_tensor(ht[:, j % 2, k, :], src[:, kt, :], PV[:, g + kt:g + kt + 1],
                                                       rstd[:, :], ALU.mult, ALU.mult)
                    ins.then_inc(normed, 1)
                    if j >= 1:
                        low(j - 1)
                low(3)
                seen(operand, 2)

            def add_quarter(src, gain, rstd, j):
                g = COL[gain]
                for k in range(4):
                    kt = 4 * j + k
                    ins = dve.scalar_tensor_tensor(src[:, kt, :], src[:, kt, :], PV[:, g + kt:g + kt + 1],
                                                   rstd[:, :], ALU.mult, ALU.mult)
                link(ins)
                dve.tensor_tensor(X[:, 4 * j:4 * j + 4, :], X[:, 4 * j:4 * j + 4, :],
                                  src[:, 4 * j:4 * j + 4, :], ALU.add).then_inc(x_ready, 1)

            def add_norm(src, gain, rstd):
                dve.wait_ge(rstd_ready, seen(rstd_ready))
                for j in range(4):
                    add_quarter(src, gain, rstd, j)

            def low1(j):
                dve.wait_ge(nh_made, seen(nh_made))
                dve.tensor_tensor(A1L[:, 4 * j:4 * j + 4, :], HT1[:, j % 2, :, :], A1H[:, 4 * j:4 * j + 4, :].bitcast(F32),
                                  ALU.subtract).then_inc(operand, 1)

            dve.wait_ge(loaded, 16)
            g = COL["pre_mix_g"]
            for j in range(4):
                dve.wait_ge(x_in[j], 16)
                if j >= 2:
                    dve.wait_ge(operand, seen(operand))
                for k in range(4):
                    kt = 4 * j + k
                    ins = dve.tensor_scalar(HT1[:, j % 2, k, :], X[:, kt, :], PV[:, g + kt:g + kt + 1], None, ALU.mult)
                ins.then_inc(normed, 1)
                if j >= 1:
                    low1(j - 1)
                if j == 2:
                    split(0)
            low1(3)
            seen(operand, 2)

            def spread(scale, tile0):
                def evac(i, j0):
                    if scale != 1.0 and isinstance(i, int) and i + j0 == 0:
                        variance(MS1, beside_gemm=True)
                        dve.wait_ge(rstd_ready, seen(rstd_ready))
                    dve.wait_ge(unit_done, seen(unit_done, 0, "tile"))
                    for j in (j0, j0 + 1):
                        dve.scalar_tensor_tensor(Z[:, ds(4 * i + (tile0 + j), 1), :], ACC[j][:, 0:T].rearrange("p (o t) -> p o t", o=1), scale,
                                                 RSTD1[:, :].unsqueeze(1), ALU.mult, ALU.mult).then_inc(acc_free, 1)
                evac.per, evac.last = {}, None
                return evac
            pend = gemm(2, spread(HEAD_SCALE, 0), keep=True, ahead=True)
            pend = gemm(6, spread(1.0, 8), pending=pend, keep=True)
            split(0)
            pend()

            dve.wait_ge(side, 4 * 16)

            def softmax_max(n):
                dve.wait_ge(scored, seen(scored))
                if n >= 2:
                    dve.wait_ge(turned, n - 1)
                s = dve.tensor_tensor(SS[:, n % 2, :, :], AUX[n % 2][:, :].rearrange("p (q t) -> p q t", q=2), BAND[:, :, :], ALU.add)
                s.then_inc(sc_free, 1)
                dve.wait_ge(sc_free, 2 + n + 1)
                link(dve.tensor_reduce(ST[:, n % 2, 0:2], SS[:, n % 2, :, :], AX.X, ALU.max))
                dve.tensor_scalar(ST[:, n % 2, 0:2], ST[:, n % 2, 0:2], -1.0, None, ALU.mult).then_inc(maxed, 1)

            def softmax_norm(n):
                dve.wait_ge(expd, seen(expd))
                link(dve.reciprocal(ST[:, n % 2, 2:4], ST[:, n % 2, 2:4]))
                for q in range(2):
                    ins = dve.tensor_scalar(SS[:, n % 2, q, :], SS[:, n % 2, q, :], ST[:, n % 2, 2 + q:3 + q], None, ALU.mult)
                ins.then_inc(probs, 1)

            def head_lo(n):
                dve.wait_ge(pv_hi, seen(pv_hi))
                dve.tensor_tensor(B1L[:, n, :], ACC[n % 2][:, 0:T], B1H[:, n, :].bitcast(F32), ALU.subtract).then_inc(mix_ready, 1)

            ps = COL["pool_scale"]
            for s in range(8 + 2):
                if 6 <= s < 10:
                    for n in (2 * (s - 6), 2 * (s - 6) + 1):
                        dve.wait_ge(mixed_hi, seen(mixed_hi))
                        dve.scalar_tensor_tensor(B1L[:, HT + n, :], ACC[2 + n % 2][:, 0:T], PV[:, ps + n:ps + n + 1],
                                                 B1H[:, HT + n, :].bitcast(F32), ALU.mult, ALU.subtract).then_inc(pool_mix_ready, 1)
                if s < 8:
                    softmax_max(s)
                if 1 <= s < 9:
                    softmax_norm(s - 1)
                if s >= 2:
                    head_lo(s - 2)
            gemm(4, idle(), ahead=True)
            split(0)

            variance(N2[2], beside_gemm=True)
            add_norm(Y, "post_mix_g", N2[3])
            variance(N2[2])
            apply_norm(X, "pre_ffn_g", N2[1], N2[3], A2H, A2L)

            def up_evac(t0):
                cw = COL["conv_w"]

                def conv(i, j):
                    col = 2 * i + (t0 + (j % 2) + KF * (j // 2))
                    dve.wait_ge(conv_base, seen(conv_base))
                    link(dve.scalar_tensor_tensor(CV[:, j, 1:T], ACC[j][:, 0:T - 1], PV[:, ds(col + (cw + 2 * KF), 1)],
                                                  CV[:, j, 1:T], ALU.mult, ALU.add))
                    dve.scalar_tensor_tensor(CV[:, j, 2:T], ACC[j][:, 0:T - 2], PV[:, ds(col + cw, 1)],
                                             CV[:, j, 2:T], ALU.mult, ALU.add).then_inc(acc_free, 1)

                def low(i):
                    dve.wait_ge(gated_hi, seen(gated_hi))
                    dve.tensor_tensor(B2L[:, ds(2 * i, 2), :], HG[:, :, :], B2H[:, ds(2 * i, 2), :].bitcast(F32),
                                      ALU.subtract).then_inc(gated_ready, 2)

                def evac(i, j0):
                    if j0 == 0:
                        if not isinstance(i, int):
                            low(i - 1)
                        conv(i, 0)
                        conv(i, 1)
                    else:
                        conv(i, 2)
                        conv(i, 3)
                        dve.wait_ge(acc_free, seen(acc_free, 0, "tile"))
                        for j in range(2):
                            dve.wait_ge(gelu_done, seen(gelu_done))
                            dve.tensor_tensor(HG[:, j, :], GE[:, j, :], CV[:, 2 + j, :], ALU.mult).then_inc(gated, 1)
                evac.per = {conv_base: 4, dstep: 4, gelu_done: 2, gated_hi: 1}
                evac.last = lambda iters: low(iters - 1)
                return evac

            def adder():
                def evac(i, j0):
                    dve.wait_ge(unit_done, seen(unit_done, 0, "tile"))
                    for j in (j0, j0 + 1):
                        y = Y[:, ds(4 * i + j, 1), :]
                        dve.tensor_tensor(y, ACC[j][:, 0:T].rearrange("p (o t) -> p o t", o=1), y, ALU.add).then_inc(acc_free, 1)
                evac.per, evac.last = {}, None
                return evac

            pend = None
            for n, (t0, tiles) in enumerate(GROUPS):
                pend = gemm(tiles // 2, up_evac(t0), pending=pend, keep=True, ahead=(n == 0))
                pend = gemm(4, idle() if n == 0 else adder(), pending=pend, ku=tiles // 4, keep=True)
            split(0)
            pend()

            variance(N2[2], beside_gemm=True)

            def shift_diff(i):
                x4 = X[:, ds(4 * i, 4), :]
                dve.tensor_tensor(XX3[:, :, 1:T], x4[:, :, 0:T - 1], x4[:, :, 1:T], ALU.subtract)
                link(dve.tensor_scalar(XX3[:, :, 0:1], x4[:, :, 0:1], -1.0, None, ALU.mult))

            def mix(s_, i, ht):
                g = COL["a_mu_proj_2"] + s_ * KD
                shift_diff(i)
                for k in range(4):
                    ins = dve.scalar_tensor_tensor(ht[:, k:k + 1, :], XX3[:, k:k + 1, :], PV[:, ds(4 * i + (g + k), 1)],
                                                   X[:, ds(4 * i + k, 1), :], ALU.mult, ALU.add)
                ins.then_inc(normed, 1)

            def mix_lo(i, ht, hi, lo):
                dve.wait_ge(nh_made, seen(nh_made))
                dve.tensor_tensor(lo[:, ds(4 * i, 4), :], ht[:, :, :], hi[:, ds(4 * i, 4), :].bitcast(F32), ALU.subtract)\
                   .then_inc(operand, 1)

            def mixed_part(s_, hi, lo):
                def side(i):
                    mix(s_, i, HT3)
                    mix_lo(i, HT3, hi, lo)
                    dve.wait_ge(operand, seen(operand))
                return side

            def lora_part():
                g = COL["a_mu_lora_2"]

                def side(i):
                    shift_diff(i)
                    for w, dst in enumerate((KAP, BET)):
                        for k in range(4):
                            ins = dve.scalar_tensor_tensor(dst[:, ds(4 * i + k, 1), :], XX3[:, k:k + 1, :],
                                                           PV[:, ds(4 * i + (g + w * KD + k), 1)],
                                                           X[:, ds(4 * i + k, 1), :], ALU.mult, ALU.add)
                    ins.then_inc(xw_ready, 1)
                    dve.wait_ge(xw_ready, seen(xw_ready))
                return side

            def beside(side, per):
                def evac(i, j0):
                    if j0 == 0:
                        if isinstance(i, int):
                            dve.wait_ge(unit_done, seen(unit_done, 0, "tile") - 4)
                        side(i)
                evac.per, evac.last = per, None
                return evac

            dve.wait_ge(rstd_ready, seen(rstd_ready))
            for i in range(4):
                add_quarter(Y, "post_ffn_g", N2[3], i)
                dve.wait_ge(x_ready, 4 + i + 1)
                if i >= 2:
                    dve.wait_ge(operand, seen(operand))
                mix(3, i, (HT3, HT3B)[i % 2])
                if i >= 1:
                    mix_lo(i - 1, (HT3, HT3B)[(i - 1) % 2], A3H, A3L)
            mix_lo(3, HT3B, A3H, A3L)
            seen(operand, 2)
            dve.wait_ge(operand, seen.total(operand))
            pend = None
            for n in range(4):
                if n < 3:
                    ev = beside(mixed_part(STREAMS[n + 1][0], STREAMS[n + 1][1], STREAMS[n + 1][2]), {dstep: 1, nh_made: 1, operand: 1})
                else:
                    ev = beside(lora_part(), {dstep: 1, xw_ready: 1})
                pend = gemm(4, ev, pending=pend, keep=True, ahead=(n == 0))
            pend()

            dve.wait_ge(acc_free, 4 + ALL_TILES)
            dve.wait_ge(kk_norm, 1)
            link(dve.tensor_scalar(tmp(20)[0:32, :], tmp(20)[0:32, :], 1e-12, None, ALU.max))
            dve.reciprocal(tmp(20)[0:32, :], tmp(20)[0:32, :]).then_inc(kk_inverse, 1)
            for f in range(KD):
                c = COL["a_k_k_2"] + f
                dve.wait_ge(kk_wide, f + 1)
                dve.scalar_tensor_tensor(BON[:, f, :], K[:, f, :], PV[:, c:c + 1], AUX[f % 2][:, 0:T], ALU.mult, ALU.mult).then_inc(kk_ready, 1)

            dve.wait_ge(kk_ready, KD)
            dve.wait_ge(ones_ready, 1)
            for s_ in range(KD + 3):
                if s_ < KD:
                    f, p = s_, s_ % 2
                    ka, rk = COL["a_k_a_2"] + f, COL["a_r_k_2"] + f
                    if f >= 2:
                        dve.wait_ge(tile_done, f - 1)
                    dve.wait_ge(sig_ready, 2 * f + 2)
                    dve.wait_ge(lora_in, 80)
                    dve.tensor_tensor_scan(tmp(12 + p), SCAN, KAP[:, f, :], 0.0, ALU.mult, ALU.add).then_inc(l_ready, 1)
                    link(dve.tensor_scalar(tmp(22 + p), BET[:, f, :], -1.0, PV[:, ka:ka + 1], ALU.add, ALU.mult))
                    link(dve.scalar_tensor_tensor(tmp(22 + p), tmp(22 + p), 1.0, K[:, f, :], ALU.add, ALU.mult))
                    dve.scalar_tensor_tensor(tmp(26 + p), R[:, f, :], PV[:, rk:rk + 1], tmp(22 + p), ALU.mult, ALU.mult).then_inc(rk_ready, 1)
                if 1 <= s_ < KD + 1:
                    f, p = s_ - 1, (s_ - 1) % 2
                    dve.wait_ge(decays, f + 1)
                    dve.wait_ge(b1_ready, f + 1)
                    link(dve.scalar_tensor_tensor(by_chunk(KAP[:, f, :]), by_chunk(BON[:, f, :]), -1.0, decay(f)[:, :, 0:CHUNK],
                                                  ALU.mult, ALU.mult))
                    dve.tensor_tensor(BET[:, f, :], tmp(24 + p), tmp(20 + p), ALU.mult)
                    dve.tensor_tensor(K[:, f, :], tmp(22 + p), tmp(20 + p), ALU.mult)
                    dve.wait_ge(bonus_sum, f + 1)
                    dve.tensor_tensor(BON[:, f, :], AUX[2 + p][:, 0:T], V[:, f, :], ALU.mult).then_inc(tile_done, 1)
                if s_ >= 3:
                    f, p = s_ - 3, (s_ - 3) % 2
                    dve.wait_ge(lt_done, f + 1)
                    if f >= 2:
                        dve.wait_ge(lt_stored[p], 32 * (f // 2))
                    dve.tensor_tensor((XS, US)[p][:, :, :], ACC[p][:, 0:T].rearrange("p (c t) -> p c t", c=NCH),
                                      TRI_S.unsqueeze(1).broadcast_to([P, NCH, CHUNK]), ALU.mult).then_inc(lt_ready, 1)

            dve.wait_ge(inv_in, 32 * KD)
            dve.wait_ge(inv_init, 1)
            for s_ in range(H - 1):
                n, r = s_ + 1, H - 1 - s_
                o = OUTER[:, 0:2 * n * r].rearrange("p (b j t) -> p b j t", b=2, j=n)
                link(dve.tensor_tensor(o, LT[:, :, s_:s_ + 1, s_ + 1:].broadcast_to([P, 2, n, r]),
                                       TT[:, :, 0:n, s_:s_ + 1].broadcast_to([P, 2, n, r]), ALU.mult))
                part = TT[:, :, 0:n, s_ + 1:H]
                ins = dve.tensor_tensor(part, part, o, ALU.add)
                if s_ < H - 2:
                    link(ins)
            ins.then_inc(inverted, 1)

            wide = lambda x: x.rearrange("p i (h t) -> p i h t", h=2)

            def read_pairs(g, c, first=False):
                m = c % 2
                dve.wait_ge(prep_done, seen(prep_done))
                if not first:
                    dve.wait_ge(y_done, seen(y_done))
                k2 = ACC[0][:, :].rearrange("p (i x t) -> p i x t", i=4, x=2)
                b2 = ACC[1][:, :].rearrange("p (i x t) -> p i x t", i=4, x=2)
                tri_2 = TRI2.rearrange("p (o h t) -> p o h t", o=1, h=2).broadcast_to([P, 4, 2, CHUNK])
                quarter = QUARTER.rearrange("p (o h t) -> p o h t", o=1, h=2).broadcast_to([P, 4, 2, H])
                dve.tensor_tensor(wide(blocks(m, AKK)), diag(k2[:, :, 1, :]), tri_2, ALU.mult)
                dve.tensor_tensor(wide(cross(m))[:, :, :, H:], b2[:, :, 1:2, H:].broadcast_to([P, 4, 2, H]), quarter, ALU.mult)\
                    .then_inc(pairs_read, 1)

            def read_rest(g, c):
                m = c % 2
                tri_i = TRI_I.unsqueeze(1).broadcast_to([P, 4, CHUNK])
                for n, bank in ((ARK, ACC[0]), (ARB, ACC[1])):
                    ins = dve.tensor_tensor(small(m, n), bank[:, :].rearrange("p (i x t) -> p i x t", i=4, x=2)[:, :, 0, :], tri_i, ALU.mult)
                ins.then_inc(rest_out, 1)

            def read_v(g, c, first=False):
                m = c % 2
                dve.wait_ge(vb_ready, seen(vb_ready))
                v2 = wide(blocks(m, VBD))
                dve.tensor_tensor(small(m, VC), v2[:, :, 0, :], v2[:, :, 1, :], ALU.add).then_inc(vc_ready, 1)

            def step(g, c, nxt):
                if nxt:
                    read_pairs(*nxt)
                dve.wait_ge(w_done, seen(w_done))
                dve.tensor_tensor(XS[:, :, :], AUX[0][:, 0:T].rearrange("p (i c) -> p i c", i=4), XS[:, :, :], ALU.add).then_inc(ws_ready, 1)
                if c > 0:
                    if not nxt:
                        dve.wait_ge(y_done, 4 * NCH)
                    dve.wait_ge(s_ready, seen(s_ready))
                    dve.tensor_tensor(wide(SBD[:, :, :]), diag(S[:, :, :]), MASK4, ALU.mult).then_inc(sbd_ready, 1)
                if nxt:
                    read_rest(*nxt)
                dve.wait_ge(us_ready, seen(us_ready, 2))
                dve.tensor_tensor(wide(UBD[:, :, :]), diag(US[:, :, :]), MASK4, ALU.mult).then_inc(ubd_ready, 1)
                if c > 0:
                    dve.wait_ge(sbd_ready, seen(sbd_ready))
                if c < 3:
                    dve.wait_ge(s_done, seen(s_done))
                    ps = AUX[3][:, 0:T].rearrange("p (i c) -> p i c", i=4)
                    if c > 0:
                        link(dve.tensor_tensor(S[:, :, :], ps, S[:, :, :], ALU.add))
                        ps = S[:, :, :]
                    dve.tensor_tensor(S[:, :, :], ps, GCE[:, ds(4 * g, 4), c:c + 1].broadcast_to([P, 4, CHUNK]), ALU.mult)\
                       .then_inc(s_ready, 1)
                if nxt:
                    read_v(*nxt)

            dve.wait_ge(t_stored, 16)
            dve.wait_ge(cross_zero, 1)
            read_pairs(0, 0, True)
            read_rest(0, 0)
            read_v(0, 0)
            with seen.loop(3, {prep_done: 4, y_done: 4, us_ready: 8, s_done: 3, dstep: 2, s_ready: 3, w_done: 4, vb_ready: 4, sbd_ready: 3}) as g:
                for c in range(NCH):
                    step(g, c, (g + (c + 1) // NCH, (c + 1) % NCH))
            for c in range(NCH):
                step(3, c, (3, c + 1) if c < 3 else None)

            dve.wait_ge(y_out, 1 + 4 * NCH)
            for f in range(KD):
                dve.wait_ge(gn_sum, f + 1)
                dve.scalar_tensor_tensor(BET[:, f, :], AUX[f % 2][:, 0:T], -1.0 / CHUNK, BET[:, f, :], ALU.mult, ALU.add)\
                    .then_inc(gn_centred, 1)
            dve.wait_ge(gn_sq_sum, KD)
            link(dve.tensor_scalar(RS4[:, 0, :], AUX[2][0:32, 0:T], 1.0 / CHUNK, GN_EPS, ALU.mult, ALU.add))
            dve.reciprocal(RS4[:, 0, :], RS4[:, 0, :]).then_inc(gn_var, 1)
            split(0)
            for s_ in range(KD + 2):
                if s_ >= 2:
                    f = s_ - 2
                    dve.wait_ge(gn_hi, f + 1)
                    dve.tensor_tensor(C4L[:, f, :], gnt(1, f), C4H[:, f, :].bitcast(F32), ALU.subtract).then_inc(gn_ready, 1)
                if s_ < KD:
                    f = s_
                    gg, gb = COL["a_gn_g_2"] + f, COL["a_gn_b_2"] + f
                    dve.wait_ge(gn_wide, f + 1)
                    if f >= 4:
                        dve.wait_ge(gn_ready, f - 3)
                    link(dve.scalar_tensor_tensor(gnt(1, f), BET[:, f, :], PV[:, gg:gg + 1], AUX[f % 2][:, 0:T], ALU.mult, ALU.mult))
                    dve.scalar_tensor_tensor(gnt(1, f), gnt(1, f), PV[:, gb:gb + 1], BON[:, f, :], ALU.add, ALU.add).then_inc(gn_out, 1)
            def residual():
                def evac(i, j0):
                    dve.wait_ge(unit_done, seen(unit_done, 0, "tile"))
                    for j in (j0, j0 + 1):
                        x = X[:, ds(4 * i + j, 1), :]
                        dve.scalar_tensor_tensor(x, x, ALPHA, ACC[j][:, 0:T].rearrange("p (o t) -> p o t", o=1), ALU.mult, ALU.add)\
                            .then_inc(acc_free, 1)
                evac.per, evac.last = {}, None
                return evac

            pend = gemm(4, residual(), keep=True, ahead=True)
            split(0)
            pend()

            def layer_norm(which, bufs, tiles, lo=None):
                sq, mu, ms, rstd = bufs
                dve.wait_ge(acc_free, 4 + tiles)
                dve.wait_ge(ln_sum, seen(ln_sum))

                def low(q):
                    dve.wait_ge(nh_made, seen(nh_made))
                    dve.tensor_tensor(lo[0][:, 4 * q:4 * q + 4, :], X[:, 4 * q:4 * q + 4, :], lo[1][:, 4 * q:4 * q + 4, :].bitcast(F32),
                                      ALU.subtract).then_inc(operand, 1)
                wide = lambda v: v[:, :].unsqueeze(1).broadcast_to([P, 4, T])
                link(dve.tensor_scalar(mu[:, :], AUX[1][:, 0:T], 1.0 / D, None, ALU.mult))
                for q in range(4):
                    x4 = X[:, 4 * q:4 * q + 4, :]
                    dve.tensor_tensor(x4, x4, wide(mu), ALU.subtract).then_inc(xc_ready, 1)
                variance(ms, LN_EPS)
                dve.wait_ge(rstd_ready, seen(rstd_ready))
                for q in range(4):
                    x4 = X[:, 4 * q:4 * q + 4, :]
                    dve.tensor_tensor(x4, x4, wide(rstd), ALU.mult).then_inc(xm_ready, 1)
                    if lo is not None and q >= 1:
                        low(q - 1)
                if lo is not None:
                    low(3)

            layer_norm(0, L4, ALL_TILES + KD, lo=(A5L, A5H))

            bl = COL["b_lambda_2"]
            dve.wait_ge(gn_ready, KD)
            for n in range(2):
                ins = dve.tensor_tensor(LAM[:, n:n + 1], PV[:, bl + 2 * n:bl + 2 * n + 1], PV[:, bl + 2 * n + 1:bl + 2 * n + 2], ALU.mult)
            ins.then_inc(lam_prod, 1)
            pend = None
            for n in range(4):
                pend = gemm(4, idle(), pending=pend, keep=True, ahead=(n == 0))
            split(0)
            pend()
            dve.wait_ge(lam_exp, 1)
            link(dve.tensor_tensor(LAM[:, 2:3], LAM[:, 3:4], LAM[:, 2:3], ALU.subtract))
            link(dve.tensor_scalar(LAM[:, 2:3], LAM[:, 2:3], -LAM_INIT, None, ALU.add))
            dve.wait_ge(dist_in, 32)
            for s_ in range(8 + 1):
                if s_ < 8:
                    n, p = s_, s_ % 2
                    dve.wait_ge(d_scored, n + 1)
                    if n >= 2:
                        dve.wait_ge(d_turned, n - 1)
                    for m in range(2):
                        ins = dve.scalar_tensor_tensor(SS5[:, p, 2 * m:2 * m + 2, :], DIST[:, :, :], -2.0 ** -(n + 1),
                                                       AUX[2 * p + m][:, :].rearrange("p (q t) -> p q t", q=2), ALU.mult, ALU.add)
                    link(ins)
                    link(dve.tensor_reduce(ST5[:, p, 0:4], SS5[:, p, :, :], AX.X, ALU.max))
                    dve.tensor_scalar(ST5[:, p, 0:4], ST5[:, p, 0:4], -1.0, None, ALU.mult).then_inc(d_max, 1)
                if s_ >= 1:
                    n, p = s_ - 1, (s_ - 1) % 2
                    dve.wait_ge(d_exp, n + 1)
                    link(dve.reciprocal(ST5[:, p, 4:8], ST5[:, p, 4:8]))
                    link(dve.tensor_scalar(ST5[:, p, 6:8], ST5[:, p, 6:8], LAM[:, 2:3], None, ALU.mult))
                    for q in range(2):
                        ins = dve.tensor_scalar(SS5[:, p, 2 + q, :], SS5[:, p, 2 + q, :], ST5[:, p, 6 + q:7 + q], None, ALU.mult)
                    link(ins)
                    for q in range(2):
                        ins = dve.scalar_tensor_tensor(SS5[:, p, q, :], SS5[:, p, q, :], ST5[:, p, 4 + q:5 + q], SS5[:, p, 2 + q, :],
                                                       ALU.mult, ALU.add)
                    ins.then_inc(d_probs, 1)
            sc = (1.0 - LAM_INIT) ** -2
            dve.wait_ge(o_sum, 8)
            link(dve.tensor_scalar(RS5[:, 0, :], ACC[3][0:32, 0:T], sc / 256, SUBLN_EPS * sc, ALU.mult, ALU.add))
            dve.reciprocal(RS5[:, 0, :], RS5[:, 0, :]).then_inc(o_var, 1)
            for s_ in range(8 + 1):
                if s_ < 8:
                    n = s_
                    dve.wait_ge(o_wide, n + 1)
                    dve.wait_ge(o_gated, n + 1)
                    dve.tensor_tensor(Q5[:, 2 * n:2 * n + 2, :], Q5[:, 2 * n:2 * n + 2, :],
                                      AUX[n % 2][:, 0:T].unsqueeze(1).broadcast_to([P, 2, T]), ALU.mult).then_inc(o_scaled, 1)
                if s_ >= 1:
                    n = s_ - 1
                    dve.wait_ge(o_hi, n + 1)
                    dve.tensor_tensor(C5L[:, 2 * n:2 * n + 2, :], Q5[:, 2 * n:2 * n + 2, :], C5H[:, 2 * n:2 * n + 2, :].bitcast(F32),
                                      ALU.subtract).then_inc(o_ready, 2)
            gemm(4, residual(), ahead=True)
            layer_norm(1, L5, ALL_TILES + 6 * KD)


def kernel(**inputs):
    import concourse.bacc as _bacc
    from concourse.bass_utils import run_bass_kernel_spmd as _run

    x = {k: np.ascontiguousarray(v) for k, v in inputs.items()}
    arrays = {n: x[n] for n in ("w_in", "pool_w", "w_o", "w_up", "w_down", "a_w_in_2", "a_w1_2", "a_w2_2", "a_a1_2",
                                "a_a2_2", "a_w_out_2", "w_k_shared_2", "w_v_shared_2", "b_w_qg_2", "b_w_out_2")}
    arrays["x_t"] = np.ascontiguousarray(x["x"][0].T)
    arrays["params"] = np.ascontiguousarray(np.concatenate([x[n].reshape(-1, P).T for n, _ in PARAMS], 1))
    arrays["consts"] = constants()
    distance = 255 - (np.arange(P)[:, None] + np.arange(384)[None])
    rows = x["rel_bias"][0][:, np.clip(distance, -P, P) + P]
    arrays["bias_rows"] = np.ascontiguousarray(rows.transpose(1, 0, 2))

    nc = _bacc.Bacc("TRN2", target_bir_lowering=False, num_devices=1)
    h = {n: nc.dram_tensor("in_" + n, a.shape, F32, kind="ExternalInput").ap() for n, a in arrays.items()}
    h["out"] = nc.dram_tensor("out_t", (D, T), F32, kind="ExternalOutput").ap()
    program(nc, h)
    r = _run(nc, [{"in_" + n: a for n, a in arrays.items()}], core_ids=[0])
    return np.ascontiguousarray(r.results[0]["out_t"].T)[None]
```
